# Optimizing a Trainium2 kernel written in Bass

```python
import math
import jax, jax.numpy as jnp
from jax import lax
import numpy as np

D_MODEL = 1024
BATCH = 1
SEQ = 512
DEPTH = 2

CTX_LEN = 256
GRID_W = 64
DIFF_HEADS = 4
DIFF_HEAD_DIM = 64
DIFF_WIDTH = DIFF_HEADS * 2 * DIFF_HEAD_DIM
POOL_WINDOWS = (2, 4, 8, 16)
POOL_GROUPS = 4
POOL_WIDTH = 512
POOL_GROUP_DIM = POOL_WIDTH // POOL_GROUPS
NAT_HEADS = 8
NAT_HEAD_DIM = 64
NAT_WIDTH = NAT_HEADS * NAT_HEAD_DIM
WIN_ROWS = 8
WIN_COLS = 16
N_BRANCHES = 3
IN_COLS = 3 * DIFF_WIDTH + POOL_WIDTH + 3 * NAT_WIDTH + N_BRANCHES * D_MODEL
D_FF = 4 * D_MODEL
Q_BLOCK = 128
ROPE_BASE = 10000.0
NORM_EPS = 1e-6

kernel_name = "hybrid_gated_diffattn_pool_natten_block"

def rms_norm(x, g):
    xf = x.astype(jnp.float32)
    y = xf * lax.rsqrt(jnp.mean(xf * xf, axis=-1, keepdims=True) + NORM_EPS)
    return (y * g.astype(jnp.float32)).astype(x.dtype)

def modulate(h, shift, scale):
    return h * (1 + scale) + shift

def adaln(cond, w, b):
    m = jax.nn.silu(cond) @ w + b
    m = m.reshape(m.shape[:-1] + (1, 6, D_MODEL))
    return tuple(m[..., i, :] for i in range(6))

def split_in(z):
    sizes = (DIFF_WIDTH,) * 3 + (POOL_WIDTH,) + (NAT_WIDTH,) * 3
    idx = [int(v) for v in np.cumsum(sizes)]
    return jnp.split(z, idx, axis=-1)

def axial_rope(x):
    L, dh = x.shape[1], x.shape[-1]
    half = dh // 2
    nf = half // 2
    pos = jnp.arange(L)
    row = (pos // GRID_W).astype(jnp.float32)
    col = (pos % GRID_W).astype(jnp.float32)
    inv = ROPE_BASE ** (-jnp.arange(nf, dtype=jnp.float32) / nf)

    def rot(u, p):
        ang = p[:, None] * inv
        cos = jnp.cos(ang)[None, :, None, None, :].astype(x.dtype)
        sin = jnp.sin(ang)[None, :, None, None, :].astype(x.dtype)
        u1, u2 = u[..., :nf], u[..., nf:]
        return jnp.concatenate([u1 * cos - u2 * sin, u1 * sin + u2 * cos], axis=-1)

    return jnp.concatenate([rot(x[..., :half], row), rot(x[..., half:], col)], axis=-1)

def diff_attention(q, k, v, lam):
    B, Lq, H, _, dh = q.shape
    nb = Lq // Q_BLOCK
    qb = q.reshape(B, nb, Q_BLOCK, H, 2, dh).swapaxes(0, 1)
    sc = dh ** -0.5

    def block(qq):
        s = jnp.einsum('bqhmd,bkhmd->bhmqk', qq, k).astype(jnp.float32) * sc
        p = jax.nn.softmax(s, axis=-1)
        a = (p[:, :, 0] - lam * p[:, :, 1]).astype(v.dtype)
        return jnp.einsum('bhqk,bkhe->bqhe', a, v)

    o = lax.map(block, qb)
    return o.swapaxes(0, 1).reshape(B, Lq, H, v.shape[-1])

def diff_head_out(o, g_subln, lam_init):
    B, L = o.shape[0], o.shape[1]
    return (rms_norm(o, g_subln) * (1.0 - lam_init)).reshape(B, L, DIFF_WIDTH)

def dense_attention(q, k, v):
    s = jnp.einsum('bqhd,bkhd->bhqk', q, k).astype(jnp.float32) * (q.shape[-1] ** -0.5)
    p = jax.nn.softmax(s, axis=-1).astype(v.dtype)
    return jnp.einsum('bhqk,bkhd->bqhd', p, v)

def neighbourhood_attention(q, k, v, kc, vc, rpb):
    B, L, H, d = q.shape
    rows = L // GRID_W
    kr = min(WIN_ROWS, rows)
    sc = d ** -0.5
    qg = q.reshape(B, rows, GRID_W, H, d)
    kg = k.reshape(B, rows, GRID_W, H, d)
    vg = v.reshape(B, rows, GRID_W, H, d)
    r = jnp.arange(rows)
    row_idx = jnp.clip(r - kr // 2, 0, rows - kr)[:, None] + jnp.arange(kr)
    cq = jnp.arange(GRID_W)
    col_idx = jnp.clip(cq - WIN_COLS // 2, 0, GRID_W - WIN_COLS)[:, None] + jnp.arange(WIN_COLS)
    d_row = row_idx - r[:, None] + (WIN_ROWS - 1)
    d_col = col_idx - cq[:, None] + (WIN_COLS - 1)
    rpb_c = rpb[:, :, d_col]
    n_loc = kr * WIN_COLS

    def one_row(args):
        q_r, ridx, dr = args
        k_win = kg[:, ridx][:, :, col_idx]
        v_win = vg[:, ridx][:, :, col_idx]
        bias = rpb_c[:, dr].transpose(0, 2, 1, 3).astype(jnp.float32)
        s_loc = jnp.einsum('bwhd,brwkhd->bhwrk', q_r, k_win).astype(jnp.float32) * sc + bias
        s_ctx = jnp.einsum('bwhd,bchd->bhwc', q_r, kc).astype(jnp.float32) * sc
        s = jnp.concatenate([s_loc.reshape(B, H, GRID_W, n_loc), s_ctx], axis=-1)
        p = jax.nn.softmax(s, axis=-1).astype(v.dtype)
        p_loc = p[..., :n_loc].reshape(B, H, GRID_W, kr, WIN_COLS)
        p_ctx = p[..., n_loc:]
        return (jnp.einsum('bhwrk,brwkhd->bwhd', p_loc, v_win)
                + jnp.einsum('bhwc,bchd->bwhd', p_ctx, vc))

    o = lax.map(one_row, (qg.swapaxes(0, 1), row_idx, d_row))
    return o.swapaxes(0, 1).reshape(B, L, H, d)

def multiscale_pool(u, group_w, chan_scale):
    B, L, _ = u.shape
    uf = u.astype(jnp.float32)
    csum = jnp.concatenate([jnp.zeros((B, 1, POOL_WIDTH), jnp.float32), jnp.cumsum(uf, axis=1)], axis=1)
    t = jnp.arange(L)
    parts = []
    for gi, w in enumerate(POOL_WINDOWS):
        sl = slice(gi * POOL_GROUP_DIM, (gi + 1) * POOL_GROUP_DIM)
        lo = jnp.clip(t - w // 2, 0, L)
        hi = jnp.clip(t + w // 2, 0, L)
        cnt = (hi - lo).astype(jnp.float32)[None, :, None]
        cg = csum[:, :, sl]
        parts.append((cg[:, hi] - cg[:, lo]) / cnt - uf[:, :, sl])
    p = jnp.concatenate(parts, axis=-1).astype(u.dtype).reshape(B, L, POOL_GROUPS, POOL_GROUP_DIM)
    y = jnp.einsum('blgc,gce->blge', p, group_w).reshape(B, L, POOL_WIDTH)
    return y * chan_scale

def merge_branches(o_a, o_b, o_c, gate_logits, w_branch, w_out):
    g = jax.nn.sigmoid(gate_logits.astype(jnp.float32)).astype(o_a.dtype)
    g = g.reshape(gate_logits.shape[:-1] + (N_BRANCHES, D_MODEL))
    merged = (g[..., 0, :] * (o_a @ w_branch[0])
              + g[..., 1, :] * (o_b @ w_branch[1])
              + g[..., 2, :] * (o_c @ w_branch[2]))
    return merged @ w_out

def sq_relu_mlp(h, w1, w2):
    return jnp.square(jax.nn.relu(h @ w1)) @ w2

def setup_inputs(seed: int = 0) -> dict:
    key = jax.random.key(seed)
    ks = jax.random.split(key, 24)

    def nrm(k, shape, std):
        return jax.random.normal(k, shape, jnp.float32) * std

    dh = DIFF_HEAD_DIM
    return {
        "x": nrm(ks[0], (BATCH, SEQ, D_MODEL), 1.0),
        "c": nrm(ks[1], (BATCH, D_MODEL), 1.0),
        "ctx": nrm(ks[2], (BATCH, CTX_LEN, D_MODEL), 1.0),
        "c_ctx": nrm(ks[3], (D_MODEL,), 1.0),
        "w_ada": nrm(ks[4], (DEPTH, D_MODEL, 6 * D_MODEL), 0.5 * D_MODEL ** -0.5),
        "b_ada": nrm(ks[5], (DEPTH, 6 * D_MODEL), 0.01),
        "g_mix": 1.0 + nrm(ks[6], (DEPTH, D_MODEL), 0.05),
        "g_mlp": 1.0 + nrm(ks[7], (DEPTH, D_MODEL), 0.05),
        "w_in": nrm(ks[8], (DEPTH, D_MODEL, IN_COLS), D_MODEL ** -0.5),
        "lambda_q1": nrm(ks[9], (DEPTH, dh), 0.1),
        "lambda_k1": nrm(ks[10], (DEPTH, dh), 0.1),
        "lambda_q2": nrm(ks[11], (DEPTH, dh), 0.1),
        "lambda_k2": nrm(ks[12], (DEPTH, dh), 0.1),
        "g_subln": 1.0 + nrm(ks[13], (DEPTH, 2 * dh), 0.05),
        "pool_w": nrm(ks[14], (DEPTH, POOL_GROUPS, POOL_GROUP_DIM, POOL_GROUP_DIM), POOL_GROUP_DIM ** -0.5),
        "pool_scale": 1.0 + nrm(ks[15], (DEPTH, POOL_WIDTH), 0.1),
        "nat_rpb": nrm(ks[16], (DEPTH, NAT_HEADS, 2 * WIN_ROWS - 1, 2 * WIN_COLS - 1), 0.1),
        "w_branch": nrm(ks[17], (DEPTH, N_BRANCHES, DIFF_WIDTH, D_MODEL), DIFF_WIDTH ** -0.5),
        "w_out": nrm(ks[18], (DEPTH, D_MODEL, D_MODEL), D_MODEL ** -0.5),
        "w_mlp1": nrm(ks[19], (DEPTH, D_MODEL, D_FF), D_MODEL ** -0.5),
        "w_mlp2": nrm(ks[20], (DEPTH, D_FF, D_MODEL), D_FF ** -0.5),
        "g_final": 1.0 + nrm(ks[21], (D_MODEL,), 0.05),
    }

def reference(x, c, ctx, c_ctx, w_ada, b_ada, g_mix, g_mlp, w_in, lambda_q1, lambda_k1, lambda_q2, lambda_k2,
              g_subln, pool_w, pool_scale, nat_rpb, w_branch, w_out, w_mlp1, w_mlp2, g_final):
    B, L, _ = x.shape
    C = ctx.shape[1]
    H, dh = DIFF_HEADS, DIFF_HEAD_DIM
    xc = ctx
    for l in range(DEPTH):
        last = l == DEPTH - 1
        lam_init = 0.8 - 0.6 * math.exp(-0.3 * l)
        f32 = jnp.float32
        lam = (jnp.exp(jnp.sum(lambda_q1[l].astype(f32) * lambda_k1[l].astype(f32)))
               - jnp.exp(jnp.sum(lambda_q2[l].astype(f32) * lambda_k2[l].astype(f32))) + lam_init)
        sh1, sc1, ga1, sh2, sc2, ga2 = adaln(c, w_ada[l], b_ada[l])
        csh1, csc1, cga1, csh2, csc2, cga2 = adaln(c_ctx, w_ada[l], b_ada[l])

        h = modulate(rms_norm(x, g_mix[l]), sh1, sc1)
        hc = modulate(rms_norm(xc, g_mix[l]), csh1, csc1)
        qa, ka, va, pu, qn, kn, vn, gl = split_in(h @ w_in[l])
        qac, kac, vac, puc, qnc, knc, vnc, glc = split_in(hc @ w_in[l])

        qa = axial_rope(qa.reshape(B, L, H, 2, dh))
        ka = axial_rope(ka.reshape(B, L, H, 2, dh))
        va = va.reshape(B, L, H, 2 * dh)
        kac = kac.reshape(B, C, H, 2, dh)
        vac = vac.reshape(B, C, H, 2 * dh)
        o_a = diff_attention(qa, jnp.concatenate([kac, ka], axis=1), jnp.concatenate([vac, va], axis=1), lam)
        o_a = diff_head_out(o_a, g_subln[l], lam_init)

        o_b = multiscale_pool(pu, pool_w[l], pool_scale[l])

        knc = knc.reshape(B, C, NAT_HEADS, NAT_HEAD_DIM)
        vnc = vnc.reshape(B, C, NAT_HEADS, NAT_HEAD_DIM)
        o_c = neighbourhood_attention(qn.reshape(B, L, NAT_HEADS, NAT_HEAD_DIM),
                                      kn.reshape(B, L, NAT_HEADS, NAT_HEAD_DIM),
                                      vn.reshape(B, L, NAT_HEADS, NAT_HEAD_DIM),
                                      knc, vnc, nat_rpb[l]).reshape(B, L, NAT_WIDTH)

        x = x + ga1 * merge_branches(o_a, o_b, o_c, gl, w_branch[l], w_out[l])

        if not last:
            o_ac = diff_head_out(diff_attention(qac.reshape(B, C, H, 2, dh), kac, vac, lam), g_subln[l], lam_init)
            o_bc = multiscale_pool(puc, pool_w[l], pool_scale[l])
            o_cc = dense_attention(qnc.reshape(B, C, NAT_HEADS, NAT_HEAD_DIM), knc, vnc).reshape(B, C, NAT_WIDTH)
            xc = xc + cga1 * merge_branches(o_ac, o_bc, o_cc, glc, w_branch[l], w_out[l])

        h = modulate(rms_norm(x, g_mlp[l]), sh2, sc2)
        x = x + ga2 * sq_relu_mlp(h, w_mlp1[l], w_mlp2[l])
        if not last:
            hc = modulate(rms_norm(xc, g_mlp[l]), csh2, csc2)
            xc = xc + cga2 * sq_relu_mlp(hc, w_mlp1[l], w_mlp2[l])

    return rms_norm(x, g_final)


_drawn_inputs = setup_inputs


def setup_inputs(seed=0):
    import zlib

    import numpy as np

    out = dict(_drawn_inputs(seed))
    spreads = {}
    factors = {'g_mix': 3.927,
     'lambda_q1': 8.0,
     'lambda_k1': 8.0,
     'lambda_q2': 8.0,
     'lambda_k2': 7.026,
     'g_subln': 6.471,
     'pool_scale': 2.786,
     'nat_rpb': 8.0}
    for name, (base, spread) in spreads.items():
        noise = np.random.default_rng([zlib.crc32(name.encode()), seed]).standard_normal(out[name].shape)
        drawn = base * np.exp(spread * noise) if base else spread * noise
        out[name] = __import__('jax').numpy.asarray(drawn.astype(out[name].dtype))
    for name, factor in factors.items():
        out[name] = (out[name] * factor).astype(out[name].dtype)
    return out
```

```python
import math
from contextlib import ExitStack

import concourse.bass as bass
from concourse import mybir

ALU = mybir.AluOpType
ACT = mybir.ActivationFunctionType
F32 = mybir.dt.float32
F32R = mybir.dt.float32r
AX_X = mybir.AxisListType.X

P = 128
DEPTH = 2
D = 1024
KC = D // P
SEQ, CTX = 512, 256
TOK = SEQ + CTX
ROWS, COLS = 8, 64
DH, DW = 64, 512
WC = DW // P
HEADS = 4
IN_A, IN_P, IN_N, IN_G = 0, 3 * DW, 4 * DW, 7 * DW
DFF = 4 * D
EPS = 1e-6
SCALE = DH ** -0.5
RING = 4
UNIT = 1024
MASKW = (192, 256, 192)
MASKO = (0, 192, 448)
UPAD = 8
UW = SEQ + 2 * UPAD + CTX + 2 * UPAD


class Signal:

    def __init__(self, handle, known):
        self.handle, self.known, self.count, self.seen = handle, known, 0, {}

    def made(self, key=None, by=1):
        self.count += by
        self.seen[key] = self.count
        return by

    def after(self, key):
        return self.known.get(key, 1)


class Counter:

    def __init__(self, nc, ctx, known):
        self.nc, self.ctx, self.known, self.signals = nc, ctx, known, {}

    def __call__(self, name):
        s = Signal(self.ctx.enter_context(self.nc.semaphore(name)), self.known.get(name, {}))
        self.signals[name] = s
        return s

    def counted(self):
        return {n: dict(s.seen) for n, s in self.signals.items()}


def unit_plan():
    plan = []
    for l in range(DEPTH):
        plan += [("in_a", l, 12), ("branch0", l, 12), ("in_n", l, 12), ("branch2", l, 12), ("in_p", l, 4),
                 ("branch1", l, 12), ("out", l, 8)]
        for g in range(4):
            plan += [(f"up{g}", l, 8), (f"down{g}", l, 8)]
    first, tile, unit0, tile0 = {}, {}, 0, 0
    for name, l, n in plan:
        first[name, l], tile[name, l] = unit0, tile0
        unit0 += n
        tile0 += 16 if name.startswith("branch") else n
    return plan, first, tile, unit0


def hybrid_block(nc, a, out, known):
    plan, FIRST, TILE, UNITS = unit_plan()
    with ExitStack() as ctx:
        base = (nc.sbuf_base + 31) // 32 * 32
        X0 = base
        H0 = X0 + KC * TOK * 4
        RAW0 = H0 + 2 * KC * TOK * 4
        WH0 = RAW0 + RING * UNIT * 4
        WL0 = WH0 + RING * UNIT * 4
        QK0 = WL0 + RING * UNIT * 4
        M0 = QK0 + 2 * WC * TOK * 4
        V0 = M0 + KC * TOK * 4
        OL0 = V0 + 7 * DW * 4
        WK0 = OL0 + WC * TOK * 4
        C0 = WK0 + 24576

        def at(name, shape, dt, off):
            return nc.alloc_sbuf_tensor_at(name, [P] + shape, dt, offset=off)

        x = at("x", [KC, TOK], F32, X0)
        h_hi = at("h_hi", [KC, TOK], F32R, H0)
        h_lo = at("h_lo", [KC, TOK], F32R, H0 + KC * TOK * 4)
        h_f = at("h_f", [KC, TOK], F32, H0 + KC * TOK * 4)
        ada_ring = at("ada_ring", [6, KC, 256], F32, H0)
        raw = at("raw", [RING, UNIT], F32, RAW0)
        w_hi = at("w_hi", [RING, UNIT], F32R, WH0)
        w_lo = at("w_lo", [RING, UNIT], F32R, WL0)
        q = at("q", [WC, TOK], F32, QK0)
        k = at("k", [WC, TOK], F32, QK0 + WC * TOK * 4)
        x_rows = at("x_rows", [6, D], F32, QK0)
        u_pad = at("u_pad", [WC, UW], F32, QK0)
        win = at("win", [2, UW], F32, QK0 + WC * UW * 4)
        o_hi = at("o_hi", [WC, TOK], F32R, QK0)
        m_hi = at("m_hi", [KC, TOK], F32R, QK0)
        m_f = at("m_f", [KC, TOK], F32, M0)
        m_lo = at("m_lo", [KC, TOK], F32R, M0)
        cos = at("cos", [SEQ], F32, M0)
        sin = at("sin", [SEQ], F32, M0 + 4 * SEQ)
        rope_t = at("rope_t", [2, SEQ], F32, M0 + 8 * SEQ)
        o_rows = at("o_rows", [24, P], F32, M0 + 16 * SEQ)
        v = at("v", [7, DW], F32, V0)
        v_f = at("v_f", [WC, TOK], F32, OL0)
        o_f = at("o_f", [WC, TOK], F32, OL0)
        o_lo = at("o_lo", [WC, TOK], F32R, OL0)
        pooled = at("pooled", [WC, TOK], F32, OL0)
        probs_a = at("probs_a", [2, 2, TOK], F32, WK0)
        probsT_a = at("probsT_a", [2, 6, P], F32, WK0 + 16 * TOK)
        square_o = at("square_o", [P], F32, WK0 + 16 * TOK + 12 * P * 4)
        probs_n = at("probs_n", [2, 512], F32, WK0)
        probsT_n = at("probsT_n", [2, 4, P], F32, WK0 + 4096)
        bias_raw = at("bias_raw", [8, 8, 32], F32, WK0 + 8192)
        bias = at("bias", [2, 640], F32, WK0 + 16384)
        o_rows_n = at("o_rows_n", [2, P], F32, WK0 + 16384 + 5120)
        gate = at("gate", [4, TOK], F32, WK0)
        ob_hi = at("ob_hi", [WC, TOK], F32R, WK0 + 4 * TOK * 4)
        pool_w = at("pool_w", [WC, P], F32, WK0)
        square = at("square", [2, TOK], F32, WK0)
        rstd = at("rstd", [TOK], F32, WK0 + 8 * TOK)
        vec_rows = at("vec_rows", [2, P], F32, WK0 + 12 * TOK)
        y_n = at("y_n", [TOK], F32, WK0 + 12 * TOK)
        hid = [(at(f"hid_hi{i}", [KC, TOK], F32R, o), at(f"hid_lo{i}", [KC, TOK], F32R, o + KC * TOK * 4),
                at(f"hid_f{i}", [KC, TOK], F32, o + KC * TOK * 4)) for i, o in enumerate((QK0, V0))]
        off = [C0]

        def const(name, shape, dt=F32):
            n = 1
            for s in shape:
                n *= s
            t = at(name, shape, dt, off[0])
            off[0] += (n * 4 + 31) // 32 * 32
            return t

        ident = const("ident", [P])
        ones = const("ones", [P])
        mask = const("mask", [640])
        mods = const("mods", [DEPTH, 6, KC, 2])
        coef = const("coef", [DEPTH, 2, KC, 2])
        vecs = const("vecs", [66])
        edge = const("edge", [4, 2, 8])
        cond = const("cond", [KC, 2])
        cond_t = const("cond_t", [KC, 2])
        eps = const("eps", [1])
        lam_in = const("lam_in", [DEPTH, 4])
        lam_pr = const("lam_pr", [DEPTH, 2])
        lam_e = const("lam_e", [DEPTH, 2])
        neg_lam = const("neg_lam", [DEPTH])
        g_sub = const("g_sub", [DEPTH])
        neg_max = const("neg_max", [4])
        total = const("total", [4])
        rtotal = const("rtotal", [4])
        sumsq = const("sumsq", [24])
        rms_o = const("rms_o", [24])
        assert off[0] <= nc.sbuf_usable_end, (off[0], nc.sbuf_usable_end)
        G_MIX, G_MLP, G_FIN, P_SC, G_SUB, COND = 0, 16, 32, 40, 48, 50

        ps = ctx.enter_context(nc.psum_tensor("ps", [P, 8, 512], F32))
        psf = ps[:, :, :].rearrange("p b n -> p (b n)")

        count = Counter(nc, ctx, known)
        consts_in = count("consts_in")
        x_in = count("x_in")
        vecs_in = count("vecs_in")
        lam_loaded = count("lam_loaded")
        setup = count("setup")
        ada_in = [count(f"ada_in{i}") for i in range(6)]
        ada_used = count("ada_used")
        ada_made = count("ada_made")
        silu_t = count("silu_t")
        lam_exp = count("lam_exp")
        rope_in = count("rope_in")
        bias_in = count("bias_in")
        pw_in = count("pw_in")
        unit_in = [count(f"unit_in{i}") for i in range(RING)]
        hi_made = count("hi_made")
        lo_made = count("lo_made")
        tile_made = count("tile_made")
        turned = count("turned")
        stat_made = count("stat_made")
        scores_made = count("scores_made")
        pv_made = count("pv_made")
        pool_made = count("pool_made")
        tile_v = count("tile_v")
        tile_a = count("tile_a")
        turn_v = count("turn_v")
        turn_a = count("turn_a")
        rope_s = count("rope_s")
        squared = count("squared")
        root = count("root")
        rstd_v = count("rstd_v")
        normed = count("normed")
        affine = count("affine")
        act_hi = count("act_hi")
        act_lo = count("act_lo")
        biased = count("biased")
        max_made = count("max_made")
        exp_made = count("exp_made")
        rsum = count("rsum")
        probs_made = count("probs_made")
        o_out = count("o_out")
        o_sq = count("o_sq")
        o_scaled = count("o_scaled")
        mixed = count("mixed")
        pooled_s = count("pooled_s")
        hid_s = count("hid_s")
        stored = count("stored")
        block = ctx.enter_context(nc.Block())

        def toks(l):
            return TOK if l + 1 < DEPTH else SEQ

        def segs(n):
            return [(0, SEQ)] + ([(SEQ, TOK)] if n > SEQ else [])

        def tile_ps(tau, n=TOK, lo=0):
            b = 1024 * (tau % 2)
            return psf[:, b + lo:b + n]

        def in_tokens(l, name, j):
            return TOK if (name != "in_p" and j >= WC) else toks(l)

        taker = {}
        for name, l, n in plan:
            for j in range(16 if name.startswith("branch") else n):
                tau = TILE[name, l] + j
                by_act = name.startswith("up") or (name.startswith("branch") and j % 8 < 4)
                taker[tau] = tile_a if by_act else tile_v

        def wait_taken(eng, tau):
            if tau >= 2:
                eng.wait_ge(taker[tau - 2].handle, taker[tau - 2].after(("tile", tau - 2)))

        def diff_items(l):
            items = [(h, P * b, (0, TOK)) for h in range(HEADS) for b in range(SEQ // P)]
            if toks(l) > SEQ:
                items += [(h, SEQ + P * b, (SEQ, TOK)) for h in range(HEADS) for b in range(CTX // P)]
            return items

        def nat_items(l):
            items = []
            for c in range(WC):
                for g in range(4):
                    kind = 0 if g == 0 else 2 if g == 3 else 1
                    k0, k1 = max(0, P * g - 64), min(SEQ, P * g + 192)
                    tiles = {0: [(0, 0, 64), (1, 64, 128)], 2: [(4, 128, 64), (3, 0, 128)],
                             1: [(g, 0, 128), (g + 1, 128, 128)]}[kind]
                    loc = k1 - k0
                    items.append((c, P * g, kind, k0, k1, tiles + [(5, loc, 128), (6, loc + 128, 128)]))
                if toks(l) > SEQ:
                    for b in range(2):
                        items.append((c, SEQ + P * b, None, 0, 0, [(5, 0, 128), (6, 128, 128)]))
            return items

        def o_bank(i):
            return 6 if i % 2 == 0 else 3

        V_TILES_N = [(0, 64), (64, 128), (192, 128), (320, 128), (448, 64), (512, 128), (640, 128)]
        V_TILES_A = [(P * j, P) for j in range(6)]

        @block.sync
        def _(sp):
            sp.dma_start(ident[:, :], a["c_ident"]).then_inc(consts_in.handle, 16)
            sp.dma_start(mask[:, :], a["c_mask"]).then_inc(consts_in.handle, 16)
            sp.dma_start(edge[:, :, :], a["c_edge"]).then_inc(consts_in.handle, 16)
            rows = [("g_mix", 16), ("g_mlp", 16), ("g_final", 8), ("pool_scale", 8), ("g_subln", 2), ("c", 8), ("c_ctx", 8)]
            r0 = 0
            for name, n in rows:
                sp.dma_start(vec_rows[r0:r0 + n, 0, :], a[name].rearrange("(n p) -> n p", p=P)).then_inc(vecs_in.handle, 16)
                r0 += n
            sp.dma_start(vec_rows[0:96, 1, :], a["b_ada"].rearrange("(n p) -> n p", p=P)).then_inc(vecs_in.handle, 16)
            for i, name in enumerate(("lambda_q1", "lambda_k1", "lambda_q2", "lambda_k2")):
                sp.dma_start(lam_in[0:DH, :, i], a[name].rearrange("l d -> d l"), allow_slow_non_contiguous=True).then_inc(lam_loaded.handle, 16)

            for j in range(6):
                load_ada_l(sp, a, ada_ring, 0, j, j).then_inc(ada_in[j].handle, 16)
            for i in range(4):
                for r in range(ROWS):
                    sp.dma_start(x_rows[r:P:ROWS, i, :], a["x"][COLS * r + 16 * i:COLS * r + 16 * i + 16, :]).then_inc(x_in.handle, 16)
            for i in range(2):
                sp.dma_start(x_rows[:, 4 + i, :], a["ctx"][P * i:P * i + P, :]).then_inc(x_in.handle, 16)
            sp.dma_start(cos[:, :], a["c_cos"]).then_inc(rope_in.handle, 16)
            sp.dma_start(sin[:, :], a["c_sin"]).then_inc(rope_in.handle, 16)

            for l in range(DEPTH):
                first = 6 if l == 0 else 0
                with sp.Fori(0, (24 - first) // 6) as i:
                    for j in range(6):
                        sp.wait_ge(ada_used.handle, i * 6 + (24 * l + first + j - 5))
                        load_ada_l(sp, a, ada_ring, l, i * 6 + (first + j), j).then_inc(ada_in[j].handle, 16)

            def load(u, s, src, rows, i=None):
                if u >= RING:
                    sp.wait_ge(lo_made.handle, u - RING + 1 if i is None else i * RING + (u - RING + 1))
                dst = raw[:, s, :].rearrange("p (k n) -> p k n", k=rows)
                sp.dma_start(dst, src).then_inc(unit_in[s].handle, 16)

            def cols(w, j, n=P):
                return w.rearrange("(k p) n -> p k n", p=P)[:, :, bass.ts(j, n)]

            for name, l, n in plan:
                u0 = FIRST[name, l]
                if name in ("in_a", "in_n", "in_p"):
                    c0 = {"in_a": IN_A, "in_n": IN_N, "in_p": IN_P}[name]
                    w = a["w_in"][l][:, c0:c0 + n * P]
                elif name == "out":
                    w = a["w_out"][l]
                elif name.startswith("up"):
                    g = int(name[-1])
                    w = a["w_mlp1"][l][:, g * D:(g + 1) * D]
                elif name.startswith("down"):
                    g = int(name[-1])
                    w = a["w_mlp2"][l][g * D:(g + 1) * D, :]
                else:
                    b = int(name[-1])
                    wg = a["w_in"][l][:, IN_G + b * D:IN_G + (b + 1) * D]
                    for half in range(2):
                        for j in range(4):
                            load(u0 + 6 * half + j, (6 * half + j) % RING, cols(wg, 4 * half + j), KC)
                        for j in range(2):
                            load(u0 + 6 * half + 4 + j, (6 * half + j) % RING, cols(a["w_branch"][l, b], 2 * half + j, 256), WC)
                    continue
                if name == "in_a" and l:
                    sp.wait_ge(tile_made.handle, tile_made.after(("tile", TILE["down2", l - 1] + 7)))
                    sp.dma_start(cos[:, :], a["c_cos"]).then_inc(rope_in.handle, 16)
                    sp.dma_start(sin[:, :], a["c_sin"]).then_inc(rope_in.handle, 16)
                f = RING if u0 == 0 else 0
                for s in range(f):
                    load(s, s, cols(w, s), KC)
                with sp.Fori(0, (n - f) // RING) as i:
                    for s in range(RING):
                        load(u0 + f + s, s, cols(w, i * RING + (f + s)), KC, i)
                if name == "in_n":
                    sp.wait_ge(biased.handle, biased.after(("clear", l)))
                    for cl in range(16):
                        k0, k1 = max(0, cl - 7), min(32, cl + 24)
                        src = bass.AP(a["nat_rpb"].tensor, a["nat_rpb"].offset + l * 8 * 15 * 31 + k0 + 7 - cl,
                                      [[8 * 31, 8], [31, 64], [1, k1 - k0]])
                        sp.dma_start(bias_raw[8 * cl:8 * cl + 8, :, :, k0:k1].rearrange("p r h c -> p (r h) c"), src).then_inc(bias_in.handle, 16)
                if name == "in_p":
                    sp.wait_ge(tile_v.handle, tile_v.after(("tile", TILE["branch2", l] + 15)))
                    sp.dma_start(pool_w[:, :, :], a["pool_w"][l].rearrange("g c e -> c g e")).then_inc(pw_in.handle, 16)

            for i in range(4):
                sp.wait_ge(turn_v.handle, turn_v.after(("y", i, 1)))
                for r in range(ROWS):
                    sp.dma_start(out[COLS * r + 16 * i:COLS * r + 16 * i + 16, :], x_rows[r:P:ROWS, i, :]).then_inc(stored.handle, 16)
            sp.wait_ge(stored.handle, 16 * 4 * ROWS)

        @block.gpsimd
        def _(pool):
            with pool.Fori(0, UNITS // RING) as i:
                for s in range(RING):
                    pool.wait_ge(hi_made.handle, i * RING + (s + 1))
                    nc.gpsimd.tensor_tensor(w_lo[:, s, :], raw[:, s, :], w_hi[:, s, :], ALU.subtract).then_inc(lo_made.handle, 1)

        def tiles_through(u):
            for name, l, n in plan:
                if u < FIRST[name, l] + n:
                    j = u - FIRST[name, l]
                    t = TILE[name, l] + (j + 1 if not name.startswith("branch") else
                                         8 * (j // 6) + (j % 6 + 1 if j % 6 < 4 else 4 + 2 * (j % 6 - 3)))
                    return t
            raise AssertionError(u)

        @block.scalar
        def _(act):
            def split_hi(u, tiles=None):
                if isinstance(u, int):
                    if u >= UNITS:
                        return
                    act.wait_ge(unit_in[u % RING].handle, 16 * (u // RING + 1))
                    if u >= RING:
                        act.wait_ge(tile_made.handle, tiles_through(u - RING))
                    s = u % RING
                nc.scalar.activation(w_hi[:, s, :], raw[:, s, :], ACT.Copy).then_inc(hi_made.handle, 1)

            def split_hi_loop(i, u, t):
                s = u % RING
                act.wait_ge(unit_in[s].handle, i * 16 + 16 * (u // RING + 1))
                act.wait_ge(tile_made.handle, i * RING + t)
                nc.scalar.activation(w_hi[:, s, :], raw[:, s, :], ACT.Copy).then_inc(hi_made.handle, 1)

            def stream(name, l, body):
                n = dict(((a_, b_), c_) for a_, b_, c_ in plan)[name, l]
                u0, t0 = FIRST[name, l], TILE[name, l]
                linear = all(tiles_through(u0 + j + 3 - RING) == t0 + j for j in range(1, n)) and u0 + n + 3 <= UNITS
                if linear and body is None:
                    with act.Fori(0, n // RING) as i:
                        for s in range(RING):
                            split_hi_loop(i, u0 + s + 3, t0 + s)
                    return
                for j in range(n):
                    split_hi(u0 + j + 3)
                    if body:
                        body(j)

            def norm_act(l, which, n):
                if which != 2 or True:
                    for c in range(KC):
                        if c == 0 or which == 0 and l == 0:
                            key = ("x", c) if (which == 0 and l == 0) else \
                                ("tile", (TILE["out", l] if which == 1 else TILE["down3", l - 1]) + 7)
                            sem = turn_v if (which == 0 and l == 0) else tile_v
                            act.wait_ge(sem.handle, sem.after(key))
                        if c >= 2:
                            act.wait_ge(stat_made.handle, stat_made.after(("sq", l, which, c - 2)))
                        nc.scalar.activation(square[:, c % 2, 0:n], x[:, c, 0:n], ACT.Square).then_inc(squared.handle, squared.made(("sq", l, which, c)))
                act.wait_ge(stat_made.handle, stat_made.after(("sq", l, which, KC - 1)))
                if (l, which) == (0, 0):
                    act.wait_ge(setup.handle, setup.after("ones"))
                nc.scalar.activation(rstd[:, 0:n], psf[:, 3072:3072 + n], ACT.Sqrt, bias=eps[:, 0:1]).then_inc(root.handle, root.made((l, which)))
                if which == 2:
                    return
                for c in range(KC):
                    act.wait_ge(normed.handle, normed.after((l, which, c)))
                    if c == 0 and (l, which) == (0, 0):
                        act.wait_ge(setup.handle, setup.after("coef"))
                    for s, (t0, t1) in enumerate(segs(n)):
                        nc.scalar.activation(h_f[:, c, t0:t1], h_f[:, c, t0:t1], ACT.Identity,
                                             bias=mods[:, l, 3 * which, c, s:s + 1], scale=coef[:, l, which, c, s:s + 1]
                                             ).then_inc(affine.handle, affine.made((l, which, c)))
                    act.wait_ge(affine.handle, affine.after((l, which, c)))
                    if c == 0 and (l, which) != (0, 0):
                        pass
                    nc.scalar.activation(h_hi[:, c, 0:n], h_f[:, c, 0:n], ACT.Copy).then_inc(act_hi.handle, act_hi.made(("h", l, which, c)))

            act.wait_ge(setup.handle, setup.after("vecs"))
            nc.scalar.activation(cond_t[:, :, :], vecs[:, COND:COND + 16].rearrange("p (s k) -> p k s", s=2), ACT.Tanh,
                                 scale=0.5).then_inc(silu_t.handle, silu_t.made("tanh"))
            act.wait_ge(turned.handle, turned.after("lam"))
            nc.scalar.activation(lam_e[:, :, :], psf[:, 3072:3072 + 2 * DEPTH], ACT.Exp).then_inc(lam_exp.handle, lam_exp.made("exp"))
            for u in range(3):
                split_hi(u)

            for l in range(DEPTH):
                n = toks(l)
                norm_act(l, 0, TOK)
                stream("in_a", l, None)

                items = diff_items(l)

                def exp_a(i):
                    h, q0, (k0, k1) = items[i]
                    for m in range(2):
                        act.wait_ge(max_made.handle, max_made.after(("a", l, i, m)))
                        if i >= 2:
                            act.wait_ge(turned.handle, turned.after(("a", l, i - 2)))
                        s = (2 * i + m) % 4
                        nc.scalar.activation(probs_a[:, i % 2, m, 0:k1 - k0], psf[:, 1024 * m:1024 * m + k1 - k0], ACT.Exp,
                                             bias=neg_max[:, s:s + 1], accum_out=total[:, s:s + 1]
                                             ).then_inc(exp_made.handle, exp_made.made(("a", l, i, m)))

                def turn_out_a(i):
                    h, q0, (k0, k1) = items[i]
                    act.wait_ge(turned.handle, turned.after(("a4", l, i)))
                    if i >= 2:
                        act.wait_ge(pv_made.handle, pv_made.after(("pv", l, i - 2)))
                    nb = min(3, (k1 - k0) // P)
                    nc.scalar.copy(probsT_a[:, i % 2, 0:nb, :], ps[:, 4, 0:nb * P]).then_inc(turn_a.handle, turn_a.made(("a", l, i)))

                def square_oa(i):
                    act.wait_ge(o_out.handle, o_out.after(("a", l, i)))
                    if i:
                        act.wait_ge(o_sq.handle, o_sq.after(("a", l, i - 1)))
                    nc.scalar.activation(square_o[:, :], o_rows[:, i, :], ACT.Square, accum_out=sumsq[:, i:i + 1]
                                         ).then_inc(o_sq.handle, o_sq.made(("a", l, i)))

                for i in range(len(items) + 2):
                    if i < len(items):
                        exp_a(i)
                    if 1 <= i <= len(items):
                        turn_out_a(i - 1)
                    if i >= 2:
                        square_oa(i - 2)
                act.wait_ge(o_sq.handle, o_sq.after(("a", l, len(items) - 1)))
                nc.scalar.activation(rms_o[:, 0:len(items)], sumsq[:, 0:len(items)], ACT.Sqrt, bias=eps[:, 0:1], scale=1.0 / P
                                     ).then_inc(root.handle, root.made(("o", l)))
                for h in range(HEADS):
                    act.wait_ge(turned.handle, turned.after(("oT", l, h)))
                    b = 2048 + 1024 * (h % 2)
                    nc.scalar.activation(o_f[:, h, 0:n], psf[:, b:b + n], ACT.Identity, scale=g_sub[:, l:l + 1]
                                         ).then_inc(turn_a.handle, turn_a.made(("oT", l, h)))
                    act.wait_ge(turn_a.handle, turn_a.after(("oT", l, h)))
                    nc.scalar.activation(o_hi[:, h, 0:n], o_f[:, h, 0:n], ACT.Copy).then_inc(act_hi.handle, act_hi.made(("oa", l, h)))

                def gates(name):
                    u0, t0 = FIRST[name, l], TILE[name, l]
                    for half in range(2):
                        for j in range(4):
                            split_hi(u0 + 6 * half + j + 3)
                            tau = t0 + 8 * half + j
                            act.wait_ge(tile_made.handle, tau + 1)
                            if half:
                                act.wait_ge(tile_v.handle, tile_v.after(("tile", t0 + 4 + j)))
                                if name != "branch0":
                                    act.wait_ge(mixed.handle, mixed.after(("m", l, int(name[-1]), j)))
                            nc.scalar.activation(gate[:, j, 0:n], tile_ps(tau, n), ACT.Tanh, scale=0.5
                                                 ).then_inc(tile_a.handle, tile_a.made(("tile", tau)))
                        for j in range(2):
                            split_hi(u0 + 6 * half + 4 + j + 3)
                            if name == "branch1":
                                for e in range(2):
                                    c = 4 * half + 2 * j + e
                                    act.wait_ge(mixed.handle, mixed.after(("m", l, 1, c)))
                                    nc.scalar.activation(m_hi[:, c, 0:n], m_f[:, c, 0:n], ACT.Copy
                                                         ).then_inc(act_hi.handle, act_hi.made(("m", l, c)))

                gates("branch0")
                stream("in_n", l, None)

                nitems = nat_items(l)
                subs = [(i, hh) for i in range(len(nitems)) for hh in range(2)]

                def exp_n(s):
                    i, hh = subs[s]
                    c, q0, kind, k0, k1, tiles = nitems[i]
                    act.wait_ge(max_made.handle, max_made.after(("n", l, s)))
                    if s >= 2:
                        act.wait_ge(turned.handle, turned.after(("n", l, s - 2)))
                    w = k1 - k0 + CTX
                    nc.scalar.activation(probs_n[:, s % 2, 0:w], ps[:, s % 3, 0:w], ACT.Exp, bias=neg_max[:, s % 4:s % 4 + 1],
                                         accum_out=total[:, s % 4:s % 4 + 1]).then_inc(exp_made.handle, exp_made.made(("n", l, s)))

                def turn_out_n(s):
                    i, hh = subs[s]
                    tiles = nitems[i][5]
                    act.wait_ge(turned.handle, turned.after(("n", l, s)))
                    if s >= 2:
                        act.wait_ge(pv_made.handle, pv_made.after(("pvn", l, s - 2)))
                    bank = 4 + s % 2
                    half = tiles[0][2] == 64
                    if half:
                        nc.scalar.copy(probsT_n[0:64, s % 2, 0, :], ps[0:64, bank, 0:P]).then_inc(turn_a.handle, turn_a.made())
                    f = 1 if half else 0
                    nc.scalar.copy(probsT_n[:, s % 2, f:len(tiles), :], ps[:, bank, f * P:len(tiles) * P]
                                   ).then_inc(turn_a.handle, turn_a.made(("n", l, s)))

                def o_hi_n(i):
                    c, q0 = nitems[i][:2]
                    act.wait_ge(turned.handle, turned.after(("oTn", l, i)))
                    nc.scalar.activation(o_hi[:, c, q0:q0 + P], ps[:, 7, 0:P], ACT.Copy
                                         ).then_inc(act_hi.handle, act_hi.made(("on", l, i)))

                for s in range(len(subs) + 4):
                    if s < len(subs):
                        exp_n(s)
                    if 1 <= s <= len(subs):
                        turn_out_n(s - 1)
                    if s >= 4 and s % 2 == 0:
                        o_hi_n((s - 4) // 2)
                gates("branch2")
                stream("in_p", l, None)

                for g in range(WC):
                    act.wait_ge(pool_made.handle, pool_made.after((l, g)))
                    if g == 0:
                        pass
                    b = 2048 + 1024 * (g % 2)
                    nc.scalar.activation(ob_hi[:, g, 0:n], psf[:, b:b + n], ACT.Identity,
                                         scale=vecs[:, P_SC + WC * l + g:P_SC + WC * l + g + 1]
                                         ).then_inc(act_hi.handle, act_hi.made(("ob", l, g)))
                gates("branch1")
                stream("out", l, None)
                norm_act(l, 1, n)
                for g in range(4):
                    u0, t0 = FIRST[f"up{g}", l], TILE[f"up{g}", l]
                    hf = hid[g % 2][2]
                    for j in range(8):
                        split_hi(u0 + j + 3)
                        act.wait_ge(tile_made.handle, t0 + j + 1)
                        nc.scalar.activation(hf[:, j, 0:n], tile_ps(t0 + j, n), ACT.Relu
                                             ).then_inc(tile_a.handle, tile_a.made(("tile", t0 + j)))
                    stream(f"down{g}", l, None)
            norm_act(DEPTH, 2, SEQ)

        @block.tensor
        def _(pe):
            def product(tau, s, hi, lo, n, kc=KC, col=0, width=P, ready=None):
                for c in range(kc):
                    if ready:
                        ready(c)
                    wh = w_hi[:, s, c * width + col:c * width + col + P]
                    wl = w_lo[:, s, c * width + col:c * width + col + P]
                    for step, (w, act_) in enumerate(((wh, hi), (wh, lo), (wl, hi))):
                        for t0, t1 in segs(n):
                            m = pe.matmul(psf[:, 1024 * (tau % 2) + t0:1024 * (tau % 2) + t1], lhsT=w, rhs=act_[:, c, t0:t1],
                                          start=c == 0 and step == 0, stop=c == kc - 1 and step == 2)
                return m

            def tile(tau, u, *args, **kw):
                wait_taken(pe, tau)
                pe.wait_ge(lo_made.handle, u + 1)
                product(tau, u % RING, *args, **kw).then_inc(tile_made.handle, tile_made.made(("tile", tau)))

            def phase_loop(name, l, n_tok, hi, lo, ready, peel=RING):
                n = dict(((a_, b_), c_) for a_, b_, c_ in plan)[name, l]
                u0, t0 = FIRST[name, l], TILE[name, l]
                for j in range(min(peel, n)):
                    tile(t0 + j, u0 + j, hi, lo, n_tok if not callable(n_tok) else n_tok(j), ready=ready if j == 0 else None)
                if n <= peel:
                    return
                tk = taker[t0 + peel - 2]
                v0 = tk.after(("tile", t0 + peel - 2))
                by = max(1, tk.after(("tile", t0 + peel - 1)) - v0)
                for j in range(peel, n):
                    tile_made.made(("tile", t0 + j))
                with pe.Fori(0, (n - peel) // RING) as i:
                    for s in range(RING):
                        pe.wait_ge(tk.handle, i * (RING * by) + (v0 + s * by))
                        pe.wait_ge(lo_made.handle, i * RING + (u0 + peel + s + 1))
                        product(t0 + peel + s, (u0 + peel + s) % RING, hi, lo,
                                n_tok if not callable(n_tok) else n_tok(peel)).then_inc(tile_made.handle, 1)

            pe.wait_ge(vecs_in.handle, 16 * 8)
            pe.wait_ge(consts_in.handle, 48)
            pe.transpose(ps[:, 5, 64:64 + 66], vec_rows[0:66, 0, :], ident[0:66, 0:66]).then_inc(turned.handle, turned.made("vec0"))
            pe.transpose(ps[:, 5, 192:192 + 96], vec_rows[0:96, 1, :], ident[0:96, 0:96]).then_inc(turned.handle, turned.made("vec1"))
            pe.wait_ge(setup.handle, setup.after("lam_pr"))
            pe.matmul(ps[:, 6, 0:2 * DEPTH], lhsT=ones[0:DH, :], rhs=lam_pr[0:DH, :, :].rearrange("p a b -> p (a b)"), start=True, stop=True
                      ).then_inc(turned.handle, turned.made("lam"))
            pe.wait_ge(setup.handle, setup.after("cond"))
            with pe.Fori(0, 2 * 24 // 6) as i:
                for j in range(6):
                    pe.wait_ge(ada_in[j].handle, i * 16 + 16)
                    for e in range(2):
                        for c in range(KC):
                            m = pe.matmul(ps[:, 4, bass.ds(i * 24 + (4 * j + 2 * e), 2)], lhsT=ada_ring[:, j, c, P * e:P * e + P], rhs=cond[:, c, :],
                                          start=c == 0, stop=c == KC - 1)
                    m.then_inc(ada_used.handle, 1)
            ada_used.made("all", 48)

            pe.wait_ge(x_in.handle, 16 * (4 * ROWS + 2))
            for c in range(KC):
                if c >= 2:
                    pe.wait_ge(turn_v.handle, turn_v.after(("x", c - 2)))
                for i in range(6):
                    m = pe.transpose(psf[:, 1024 * (c % 2) + P * i:1024 * (c % 2) + P * i + P], x_rows[:, i, P * c:P * c + P], ident[:, :])
                m.then_inc(turned.handle, turned.made(("x", c)))

            def mean_squares(l, which, n):
                for c in range(KC):
                    pe.wait_ge(squared.handle, squared.after(("sq", l, which, c)))
                    if c == 0 and l == 0 and which == 0:
                        pe.wait_ge(setup.handle, setup.after("vecs"))
                    for t0, t1 in segs(n):
                        m = pe.matmul(psf[:, 3072 + t0:3072 + t1], lhsT=ones[:, :], rhs=square[:, c % 2, t0:t1], start=c == 0, stop=c == KC - 1)
                    m.then_inc(stat_made.handle, stat_made.made(("sq", l, which, c)))

            def h_ready(l, which):
                def ready(c):
                    pe.wait_ge(act_lo.handle, act_lo.after(("h", l, which, c)))
                return ready

            def values(l, tiles, key):
                for j, (t0, nk) in enumerate(tiles):
                    if j < 2:
                        last = taker[TILE[key, l] + 11]
                        pe.wait_ge(last.handle, last.after(("tile", TILE[key, l] + 11)))
                    else:
                        pe.wait_ge(turn_v.handle, turn_v.after((key, l, j - 2)))
                    for c in range(WC):
                        m = pe.transpose(ps[0:nk, 4 + j % 2, P * c:P * c + P], v_f[:, c, t0:t0 + nk], ident[:, :])
                    m.then_inc(turned.handle, turned.made((key, l, j)))

            for l in range(DEPTH):
                n = toks(l)
                mean_squares(l, 0, TOK)
                phase_loop("in_a", l, TOK if n == TOK else (lambda j: n if j < WC else TOK), h_hi, h_lo, h_ready(l, 0))
                values(l, V_TILES_A, "in_a")

                items = diff_items(l)

                def scores_a(i):
                    h, q0, (k0, k1) = items[i]
                    for m in range(2):
                        if i:
                            pe.wait_ge(exp_made.handle, exp_made.after(("a", l, i - 1, m)))
                        lo_, hi_ = DH * m, DH * m + DH
                        for t0, t1 in ([(0, SEQ)] if k0 == 0 else []) + [(SEQ, TOK)]:
                            mm = pe.matmul(psf[:, 1024 * m + t0 - k0:1024 * m + t1 - k0], lhsT=q[lo_:hi_, h, q0:q0 + P],
                                           rhs=k[lo_:hi_, h, t0:t1], start=True, stop=True)
                        mm.then_inc(scores_made.handle, scores_made.made(("a", l, i, m)))

                def weighted_a(i):
                    h, q0, (k0, k1) = items[i]
                    nb = (k1 - k0) // P
                    pe.wait_ge(probs_made.handle, probs_made.after(("a", l, i)))
                    if i:
                        pe.wait_ge(turn_a.handle, turn_a.after(("a", l, i - 1)))
                        if items[i - 1][2][0] == 0:
                            pe.wait_ge(turn_v.handle, turn_v.after(("a", l, i - 1)))
                    else:
                        pe.wait_ge(turn_v.handle, turn_v.after(("in_a", l, 5)))
                    for b in range(nb):
                        mm = pe.transpose(ps[:, 4 + b // 3, P * (b % 3):P * (b % 3) + P], probs_a[:, i % 2, 0, P * b:P * b + P], ident[:, :])
                        if b == min(nb, 3) - 1:
                            mm.then_inc(turned.handle, turned.made(("a4", l, i)))
                            turned.seen["a", l, i] = turned.count
                        if b == 5:
                            mm.then_inc(turned.handle, turned.made(("a", l, i)))
                    pe.wait_ge(turn_a.handle, turn_a.after(("a", l, i)))
                    if nb > 3:
                        pe.wait_ge(turn_v.handle, turn_v.after(("a", l, i)))
                    if i >= 2:
                        pe.wait_ge(o_out.handle, o_out.after(("a", l, i - 2)))
                    for b in range(nb):
                        mm = pe.matmul(ps[:, 6 + i % 2, 0:P], lhsT=probsT_a[:, i % 2, b, :],
                                       rhs=v[:, k0 // P + b, P * h:P * h + P], start=b == 0, stop=b == nb - 1)
                    mm.then_inc(pv_made.handle, pv_made.made(("pv", l, i)))

                for i in range(len(items) + 1):
                    if i < len(items):
                        scores_a(i)
                    if i:
                        weighted_a(i - 1)
                pv_made.seen["pv", l, "last_a"] = pv_made.count
                for h in range(HEADS):
                    b0 = 2048 + 1024 * (h % 2)
                    if h >= 2:
                        pe.wait_ge(turn_a.handle, turn_a.after(("oT", l, h - 2)))
                    blocks = [i for i in range(len(items)) if items[i][0] == h]
                    for i in blocks:
                        pe.wait_ge(o_scaled.handle, o_scaled.after((l, i)))
                        q0 = items[i][1]
                        mm = pe.transpose(psf[:, b0 + q0:b0 + q0 + P], o_rows[:, i, :], ident[:, :])
                    mm.then_inc(turned.handle, turned.made(("oT", l, h)))

                def branch(name, hi, lo, ready):
                    u0, t0 = FIRST[name, l], TILE[name, l]
                    for half in range(2):
                        for j in range(4):
                            tile(t0 + 8 * half + j, u0 + 6 * half + j, h_hi, h_lo, n)
                        for j in range(2):
                            u = u0 + 6 * half + 4 + j
                            for e in range(2):
                                tile(t0 + 8 * half + 4 + 2 * j + e, u, hi, lo, n, kc=WC, col=P * e, width=2 * P,
                                     ready=ready if half + j + e == 0 else None)

                branch("branch0", o_hi, o_lo, lambda c: pe.wait_ge(act_lo.handle, act_lo.after(("o", l, c))))
                phase_loop("in_n", l, TOK if n == TOK else (lambda j: n if j < WC else TOK), h_hi, h_lo, None)
                values(l, V_TILES_N, "in_n")

                nitems = nat_items(l)
                subs = [(i, hh) for i in range(len(nitems)) for hh in range(2)]

                def scores_n(s):
                    i, hh = subs[s]
                    c, q0, kind, k0, k1, tiles = nitems[i]
                    if s >= 3:
                        pe.wait_ge(exp_made.handle, exp_made.after(("n", l, s - 3)))
                    lo_, hi_ = DH * hh, DH * hh + DH
                    loc = k1 - k0
                    if loc:
                        pe.matmul(ps[:, s % 3, 0:loc], lhsT=q[lo_:hi_, c, q0:q0 + P], rhs=k[lo_:hi_, c, k0:k1], start=True, stop=True)
                    pe.matmul(ps[:, s % 3, loc:loc + CTX], lhsT=q[lo_:hi_, c, q0:q0 + P], rhs=k[lo_:hi_, c, SEQ:TOK],
                              start=True, stop=True).then_inc(scores_made.handle, scores_made.made(("n", l, s)))

                def weighted_n(s):
                    i, hh = subs[s]
                    c, q0, kind, k0, k1, tiles = nitems[i]
                    pe.wait_ge(exp_made.handle, exp_made.after(("n", l, s)))
                    if s >= 2:
                        pe.wait_ge(turn_a.handle, turn_a.after(("n", l, s - 2)))
                    else:
                        pe.wait_ge(turn_v.handle, turn_v.after(("in_n", l, 6)))
                    bank = 4 + s % 2
                    for b, (j, off_, nk) in enumerate(tiles):
                        mm = pe.transpose(ps[0:nk, bank, P * b:P * b + P], probs_n[:, s % 2, off_:off_ + nk], ident[:, :])
                    mm.then_inc(turned.handle, turned.made(("n", l, s)))
                    pe.wait_ge(turn_a.handle, turn_a.after(("n", l, s)))
                    if i >= 2 and hh == 0:
                        pe.wait_ge(o_out.handle, o_out.after(("n", l, i - 2)))
                    h = 2 * c + hh
                    for b, (j, off_, nk) in enumerate(tiles):
                        mm = pe.matmul(ps[:, o_bank(i), DH * hh:DH * hh + DH], lhsT=probsT_n[0:nk, s % 2, b, :],
                                       rhs=v[0:nk, j, DH * h:DH * h + DH], start=b == 0, stop=b == len(tiles) - 1)
                    mm.then_inc(pv_made.handle, pv_made.made(("pvn", l, s)))

                def turn_o(i):
                    pe.wait_ge(o_out.handle, o_out.after(("n", l, i)))
                    if i:
                        pe.wait_ge(act_lo.handle, act_lo.after(("on", l, i - 1)))
                    pe.transpose(ps[:, 7, 0:P], o_rows_n[:, i % 2, :], ident[:, :]
                                 ).then_inc(turned.handle, turned.made(("oTn", l, i)))

                for s in range(len(subs) + 2):
                    if s < len(subs):
                        scores_n(s)
                    if 1 <= s <= len(subs):
                        weighted_n(s - 1)
                    if s >= 3 and s % 2 == 1:
                        turn_o((s - 3) // 2)
                per_c = len(nitems) // WC
                branch("branch2", o_hi, o_lo, lambda c: pe.wait_ge(act_lo.handle, act_lo.after(("on", l, per_c * c + per_c - 1))))
                phase_loop("in_p", l, n, h_hi, h_lo, None)
                pe.wait_ge(pw_in.handle, 16 * (l + 1))
                for g in range(WC):
                    pe.wait_ge(pooled_s.handle, pooled_s.after((l, g, "p")))
                    if g >= 2:
                        pe.wait_ge(act_lo.handle, act_lo.after(("ob", l, g - 2)))
                    b = 2048 + 1024 * (g % 2)
                    for t0, t1 in segs(n):
                        mm = pe.matmul(psf[:, b + t0:b + t1], lhsT=pool_w[:, g, :], rhs=pooled[:, g, t0:t1], start=True, stop=True)
                    mm.then_inc(pool_made.handle, pool_made.made((l, g)))
                branch("branch1", ob_hi, o_lo, lambda c: pe.wait_ge(act_lo.handle, act_lo.after(("ob", l, c))))
                phase_loop("out", l, n, m_hi, m_lo, lambda c: pe.wait_ge(act_lo.handle, act_lo.after(("m", l, c))))
                mean_squares(l, 1, n)
                for g in range(4):
                    hh_, hl_, _ = hid[g % 2]
                    phase_loop(f"up{g}", l, n, h_hi, h_lo, h_ready(l, 1) if g == 0 else None, peel=RING)
                    phase_loop(f"down{g}", l, n, hh_, hl_, lambda c: pe.wait_ge(act_lo.handle, act_lo.after(("hid", l, g, c))))
            mean_squares(DEPTH, 2, SEQ)
            for i in range(4):
                for e in range(2):
                    if i * 2 + e >= 2:
                        pi, pe_ = divmod(i * 2 + e - 2, 2)
                        pe.wait_ge(turn_v.handle, turn_v.after(("y", pi, pe_)))
                    for c in range(4 * e, 4 * e + 4):
                        pe.wait_ge(normed.handle, normed.after(("fin", c)))
                        mm = pe.transpose(ps[:, 4 + e, P * (c % 4):P * (c % 4) + P], x[:, c, P * i:P * i + P], ident[:, :])
                    mm.then_inc(turned.handle, turned.made(("y", i, e)))

        @block.vector
        def _(dve):
            V = nc.vector
            V.memset(ones[:, :], 1.0).then_inc(setup.handle, setup.made())
            V.memset(eps[:, :], EPS).then_inc(setup.handle, setup.made("ones"))
            dve.wait_ge(lam_loaded.handle, 64)
            lin = lam_in[0:DH, :, :].rearrange("p l (b t) -> p l b t", t=2)
            V.tensor_tensor(lam_pr[0:DH, :, :], lin[:, :, :, 0], lin[:, :, :, 1], ALU.mult).then_inc(setup.handle, setup.made("lam_pr"))
            dve.wait_ge(turned.handle, turned.after("vec1"))
            V.tensor_copy(vecs[:, :], ps[:, 5, 64:130]).then_inc(setup.handle, setup.made("vecs0"))
            dve.wait_ge(turned.handle, turned.after("lam"))
            V.memset(ones[:, :], 1.0 / D).then_inc(setup.handle, setup.made("vecs"))
            dve.wait_ge(silu_t.handle, 1)
            cv = vecs[:, COND:COND + 16].rearrange("p (s k) -> p k s", s=2)
            V.scalar_tensor_tensor(out=cond_t[:, :, :], in0=cond_t[:, :, :], scalar=1.0, in1=cv, op0=ALU.add, op1=ALU.mult
                                   ).then_inc(setup.handle, setup.made("silu"))
            dve.wait_ge(setup.handle, setup.after("silu"))
            V.tensor_scalar(cond[:, :, :], cond_t[:, :, :], 0.5, None, ALU.mult).then_inc(setup.handle, setup.made("cond"))
            dve.wait_ge(lam_exp.handle, 1)
            for l in range(DEPTH):
                lam_init = 0.8 - 0.6 * math.exp(-0.3 * l)
                V.scalar_tensor_tensor(out=neg_lam[:, l:l + 1], in0=lam_e[:, l, 1:2], scalar=-lam_init, in1=lam_e[:, l, 0:1],
                                       op0=ALU.add, op1=ALU.subtract).then_inc(setup.handle, setup.made())
                V.tensor_scalar(g_sub[:, l:l + 1], vecs[:, G_SUB + l:G_SUB + l + 1], 1.0 - lam_init, None, ALU.mult
                                ).then_inc(setup.handle, setup.made("lam"))

            for c in range(KC):
                dve.wait_ge(turned.handle, turned.after(("x", c)))
                V.tensor_copy(x[:, c, :], psf[:, 1024 * (c % 2):1024 * (c % 2) + TOK]).then_inc(turn_v.handle, turn_v.made(("x", c)))
            dve.wait_ge(ada_used.handle, 48)
            for s in range(2):
                V.tensor_copy(mods[:, :, :, :, s].rearrange("p l i k -> p (l i k)"), ps[:, 5, 192:288]).then_inc(setup.handle, setup.made("b"))
            dve.wait_ge(setup.handle, setup.after("b"))
            mf = mods[:, :, :, :, :].rearrange("p l i k s -> p (l i k s)")
            V.tensor_tensor(mf, ps[:, 4, 0:192], mf, ALU.add).then_inc(setup.handle, setup.made("mods"))
            dve.wait_ge(setup.handle, setup.after("mods"))
            for l in range(DEPTH):
                for w in range(2):
                    g0 = (G_MIX if w == 0 else G_MLP) + KC * l
                    for s in range(2):
                        V.scalar_tensor_tensor(out=coef[:, l, w, :, s], in0=mods[:, l, 3 * w + 1, :, s], scalar=1.0,
                                               in1=vecs[:, g0:g0 + KC], op0=ALU.add, op1=ALU.mult).then_inc(setup.handle, setup.made())
                V.tensor_scalar(mods[:, l, 2, :, :], mods[:, l, 2, :, :], 0.5, None, ALU.mult).then_inc(setup.handle, setup.made("coef"))
            dve.wait_ge(setup.handle, setup.after("coef"))

            def norm_v(l, which, n):
                dve.wait_ge(root.handle, root.after((l, which)))
                V.reciprocal(rstd[:, 0:n], rstd[:, 0:n]).then_inc(rstd_v.handle, rstd_v.made((l, which)))
                dve.wait_ge(rstd_v.handle, rstd_v.after((l, which)))
                if which == 2:
                    for c in range(KC):
                        V.scalar_tensor_tensor(out=x[:, c, 0:n], in0=x[:, c, 0:n], scalar=vecs[:, G_FIN + c:G_FIN + c + 1],
                                               in1=rstd[:, 0:n], op0=ALU.mult, op1=ALU.mult).then_inc(normed.handle, normed.made(("fin", c)))
                    return

                def lo(c):
                    dve.wait_ge(act_hi.handle, act_hi.after(("h", l, which, c)))
                    V.tensor_tensor(h_lo[:, c, 0:n], h_f[:, c, 0:n], h_hi[:, c, 0:n], ALU.subtract
                                    ).then_inc(act_lo.handle, act_lo.made(("h", l, which, c)))
                for c in range(KC):
                    V.tensor_tensor(h_f[:, c, 0:n], x[:, c, 0:n], rstd[:, 0:n], ALU.mult).then_inc(normed.handle, normed.made((l, which, c)))
                    if c >= 2:
                        lo(c - 2)
                lo(KC - 2)
                lo(KC - 1)

            def plain(tau, dst, n, scale=None):
                dve.wait_ge(tile_made.handle, tau + 1)
                if scale is None:
                    V.tensor_copy(dst, tile_ps(tau, n)).then_inc(tile_v.handle, tile_v.made(("tile", tau)))
                else:
                    V.tensor_scalar(dst, tile_ps(tau, n), scale, None, ALU.mult).then_inc(tile_v.handle, tile_v.made(("tile", tau)))

            def rope(tau, dst, n, scale, s):
                dve.wait_ge(tile_made.handle, tau + 1)
                z = tile_ps(tau, SEQ)
                V.stream_shuffle(rope_t[:, s % 2, :], z, [(i + 16) % 32 for i in range(32)]).then_inc(rope_s.handle, rope_s.made(("sh", tau)))
                V.scalar_tensor_tensor(out=dst[:, 0:SEQ], in0=z, scalar=scale, in1=cos[:, :], op0=ALU.mult, op1=ALU.mult
                                       ).then_inc(rope_s.handle, rope_s.made())
                dve.wait_ge(rope_s.handle, rope_s.after(("sh", tau)))
                V.scalar_tensor_tensor(out=rope_t[:, s % 2, :], in0=rope_t[:, s % 2, :], scalar=scale, in1=sin[:, :], op0=ALU.mult,
                                       op1=ALU.mult).then_inc(rope_s.handle, rope_s.made(("sin", tau)))
                if n > SEQ:
                    V.tensor_scalar(dst[:, SEQ:n], tile_ps(tau, n, SEQ), scale, None, ALU.mult).then_inc(rope_s.handle, rope_s.made(("c", tau)))
                    dve.wait_ge(rope_s.handle, rope_s.after(("c", tau)))
                else:
                    dve.wait_ge(rope_s.handle, rope_s.after(("sin", tau)))
                V.tensor_tensor(dst[:, 0:SEQ], dst[:, 0:SEQ], rope_t[:, s % 2, :], ALU.add).then_inc(tile_v.handle, tile_v.made(("tile", tau)))

            def values_v(l, tiles, key):
                for j, (t0, nk) in enumerate(tiles):
                    dve.wait_ge(turned.handle, turned.after((key, l, j)))
                    V.tensor_copy(v[0:nk, j, :], ps[0:nk, 4 + j % 2, :]).then_inc(turn_v.handle, turn_v.made((key, l, j)))

            for l in range(DEPTH):
                n = toks(l)
                norm_v(l, 0, TOK)
                t0 = TILE["in_a", l]
                dve.wait_ge(rope_in.handle, 32 * (l + 1))
                for j in range(12):
                    nt = n if j < WC else TOK
                    if j < 8:
                        rope(t0 + j, (q if j < 4 else k)[:, j % 4, :], nt, SCALE if j < 4 else 1.0, j)
                    else:
                        plain(t0 + j, v_f[:, j - 8, 0:nt], nt)
                values_v(l, V_TILES_A, "in_a")

                items = diff_items(l)

                def max_a(i):
                    h, q0, (k0, k1) = items[i]
                    for m in range(2):
                        s = (2 * i + m) % 4
                        dve.wait_ge(scores_made.handle, scores_made.after(("a", l, i, m)))
                        V.tensor_reduce(neg_max[:, s:s + 1], psf[:, 1024 * m:1024 * m + k1 - k0], AX_X, ALU.max, negate=True
                                        ).then_inc(max_made.handle, max_made.made(("a", l, i, m)))

                def combine(i):
                    h, q0, (k0, k1) = items[i]
                    w, s = k1 - k0, (2 * i) % 4
                    dve.wait_ge(exp_made.handle, exp_made.after(("a", l, i, 1)))
                    V.reciprocal(rtotal[:, s:s + 2], total[:, s:s + 2]).then_inc(rsum.handle, rsum.made(("a", l, i)))
                    dve.wait_ge(rsum.handle, rsum.after(("a", l, i)))
                    V.tensor_scalar(rtotal[:, s + 1:s + 2], rtotal[:, s + 1:s + 2], neg_lam[:, l:l + 1], None, ALU.mult
                                    ).then_inc(rsum.handle, rsum.made())
                    V.tensor_scalar(probs_a[:, i % 2, 0, 0:w], probs_a[:, i % 2, 0, 0:w], rtotal[:, s:s + 1], None, ALU.mult
                                    ).then_inc(rsum.handle, rsum.made(("a0", l, i)))
                    dve.wait_ge(rsum.handle, rsum.after(("a0", l, i)))
                    V.scalar_tensor_tensor(out=probs_a[:, i % 2, 0, 0:w], in0=probs_a[:, i % 2, 1, 0:w], scalar=rtotal[:, s + 1:s + 2],
                                           in1=probs_a[:, i % 2, 0, 0:w], op0=ALU.mult, op1=ALU.add
                                           ).then_inc(probs_made.handle, probs_made.made(("a", l, i)))

                def turn_out_v(i):
                    h, q0, (k0, k1) = items[i]
                    if k0 == 0:
                        dve.wait_ge(turned.handle, turned.after(("a", l, i)))
                        if i >= 2:
                            dve.wait_ge(pv_made.handle, pv_made.after(("pv", l, i - 2)))
                        V.tensor_copy(probsT_a[:, i % 2, 3:6, :], ps[:, 5, 0:3 * P]).then_inc(turn_v.handle, turn_v.made(("a", l, i)))

                def o_out_a(i):
                    dve.wait_ge(pv_made.handle, pv_made.after(("pv", l, i)))
                    V.tensor_copy(o_rows[:, i, :], ps[:, 6 + i % 2, 0:P]).then_inc(o_out.handle, o_out.made(("a", l, i)))

                for i in range(len(items) + 2):
                    if i < len(items):
                        max_a(i)
                    if 1 <= i <= len(items):
                        turn_out_v(i - 1)
                    if i < len(items):
                        combine(i)
                    if i >= 2:
                        o_out_a(i - 2)
                ni = len(items)
                dve.wait_ge(root.handle, root.after(("o", l)))
                V.reciprocal(rms_o[:, 0:ni], rms_o[:, 0:ni]).then_inc(rsum.handle, rsum.made(("o", l)))
                dve.wait_ge(rsum.handle, rsum.after(("o", l)))
                dve.wait_ge(o_out.handle, o_out.after(("a", l, ni - 1)))
                order = sorted(range(ni), key=lambda i: items[i][0])
                for i in order:
                    V.tensor_scalar(o_rows[:, i, :], o_rows[:, i, :], rms_o[:, i:i + 1], None, ALU.mult
                                    ).then_inc(o_scaled.handle, o_scaled.made((l, i)))
                for h in range(HEADS):
                    dve.wait_ge(act_hi.handle, act_hi.after(("oa", l, h)))
                    V.tensor_tensor(o_lo[:, h, 0:n], o_f[:, h, 0:n], o_hi[:, h, 0:n], ALU.subtract
                                    ).then_inc(act_lo.handle, act_lo.made(("o", l, h)))

                def mix(name, b):
                    t0 = TILE[name, l]

                    def lo(c):
                        dve.wait_ge(act_hi.handle, act_hi.after(("m", l, c)))
                        V.tensor_tensor(m_lo[:, c, 0:n], m_f[:, c, 0:n], m_hi[:, c, 0:n], ALU.subtract
                                        ).then_inc(act_lo.handle, act_lo.made(("m", l, c)))
                    for c in range(KC):
                        half, j = divmod(c, 4)
                        tau = t0 + 8 * half + 4 + j
                        dve.wait_ge(tile_made.handle, tau + 1)
                        dve.wait_ge(tile_a.handle, tile_a.after(("tile", t0 + 8 * half + j)))
                        first = name == "branch0"
                        dst = m_f[:, c, 0:n] if first else gate[:, j, 0:n]
                        V.scalar_tensor_tensor(out=dst, in0=gate[:, j, 0:n], scalar=1.0, in1=tile_ps(tau, n), op0=ALU.add,
                                               op1=ALU.mult).then_inc(tile_v.handle, tile_v.made(("tile", tau)))
                        if not first:
                            dve.wait_ge(tile_v.handle, tile_v.after(("tile", tau)))
                            V.tensor_tensor(m_f[:, c, 0:n], m_f[:, c, 0:n], gate[:, j, 0:n], ALU.add
                                            ).then_inc(mixed.handle, mixed.made(("m", l, b, c)))
                        if b == 1 and c:
                            lo(c - 1)
                    if b == 1:
                        lo(KC - 1)

                mix("branch0", 0)

                t0 = TILE["in_n", l]
                dve.wait_ge(tile_v.handle, tile_v.after(("tile", TILE["branch0", l] + 15)))
                V.memset(bias_raw[:, :, :, :], 0.0).then_inc(biased.handle, biased.made(("clear", l)))
                for j in range(12):
                    nt = n if j < WC else TOK
                    dst = (q, k, v_f)[j // 4]
                    plain(t0 + j, dst[:, j % 4, 0:nt], nt, SCALE if j < 4 else None)
                values_v(l, V_TILES_N, "in_n")

                nitems = nat_items(l)
                subs = [(i, hh) for i in range(len(nitems)) for hh in range(2)]
                dve.wait_ge(bias_in.handle, 16 * 16 * (l + 1))

                def bias_of(c):
                    for hh in range(2):
                        for t, c0 in enumerate((8, 0, 0)):
                            w = MASKW[t] // 8
                            o = MASKO[t]
                            V.tensor_tensor(bias[:, hh, o:o + MASKW[t]].rearrange("p (c r) -> p c r", r=8),
                                            bias_raw[:, ::-1, 2 * c + hh, c0:c0 + w].rearrange("p r c -> p c r"),
                                            mask[:, o:o + MASKW[t]].rearrange("p (c r) -> p c r", r=8), ALU.add
                                            ).then_inc(biased.handle, biased.made(("bm", l, c)))

                def max_n(s):
                    i, hh = subs[s]
                    c, q0, kind, k0, k1, tiles = nitems[i]
                    loc = k1 - k0
                    dve.wait_ge(scores_made.handle, scores_made.after(("n", l, s)))
                    if loc:
                        if s % (len(subs) // WC) == 0:
                            dve.wait_ge(biased.handle, biased.after(("bm", l, c)))
                        V.tensor_tensor(ps[:, s % 3, 0:loc], ps[:, s % 3, 0:loc], bias[:, hh, MASKO[kind]:MASKO[kind] + loc], ALU.add
                                        ).then_inc(biased.handle, biased.made(("s", l, s)))
                        dve.wait_ge(biased.handle, biased.after(("s", l, s)))
                    V.tensor_reduce(neg_max[:, s % 4:s % 4 + 1], ps[:, s % 3, 0:loc + CTX], AX_X, ALU.max, negate=True
                                    ).then_inc(max_made.handle, max_made.made(("n", l, s)))

                def o_out_n(i):
                    dve.wait_ge(exp_made.handle, exp_made.after(("n", l, 2 * i + 1)))
                    r0 = 2 * i % 4
                    V.reciprocal(rtotal[:, r0:r0 + 2], total[:, r0:r0 + 2]).then_inc(rsum.handle, rsum.made(("n", l, i)))
                    dve.wait_ge(rsum.handle, rsum.after(("n", l, i)))
                    dve.wait_ge(pv_made.handle, pv_made.after(("pvn", l, 2 * i + 1)))
                    if i >= 2:
                        dve.wait_ge(turned.handle, turned.after(("oTn", l, i - 2)))
                    for hh in range(2):
                        V.tensor_scalar(o_rows_n[:, i % 2, DH * hh:DH * hh + DH], ps[:, o_bank(i), DH * hh:DH * hh + DH],
                                        rtotal[:, r0 + hh:r0 + hh + 1], None, ALU.mult).then_inc(o_out.handle, o_out.made(("n", l, i)))

                def o_lo_n(i):
                    c, q0 = nitems[i][:2]
                    dve.wait_ge(act_hi.handle, act_hi.after(("on", l, i)))
                    V.tensor_tensor(o_lo[:, c, q0:q0 + P], ps[:, 7, 0:P], o_hi[:, c, q0:q0 + P], ALU.subtract
                                    ).then_inc(act_lo.handle, act_lo.made(("on", l, i)))

                ns = len(subs)
                for s in range(ns + 2):
                    if s < ns:
                        if s % (ns // WC) == 0:
                            bias_of(s // (ns // WC))
                        max_n(s)
                    if s >= 3 and s % 2 == 1:
                        o_out_n((s - 3) // 2)
                    if s >= 5 and s % 2 == 1:
                        o_lo_n((s - 5) // 2)
                o_lo_n(len(nitems) - 1)
                mix("branch2", 2)

                t0 = TILE["in_p", l]
                dve.wait_ge(tile_made.handle, t0)
                for g in range(WC):
                    for z0 in (0, UPAD + SEQ, UPAD + SEQ + UPAD, UW - UPAD):
                        V.memset(u_pad[:, g, z0:z0 + UPAD], 0.0).then_inc(pooled_s.handle, pooled_s.made(("zero", l)))
                offs = [(0, UPAD, SEQ), (SEQ, SEQ + 3 * UPAD, CTX)][:len(segs(n))]
                for g in range(WC):
                    tau = t0 + g
                    dve.wait_ge(tile_made.handle, tau + 1)
                    if n > SEQ:
                        V.tensor_copy(u_pad[:, g, SEQ + 3 * UPAD:SEQ + 3 * UPAD + CTX], tile_ps(tau, TOK, SEQ)
                                      ).then_inc(pooled_s.handle, pooled_s.made())
                    V.tensor_copy(u_pad[:, g, UPAD:UPAD + SEQ].rearrange("p (r c) -> p c r", r=ROWS),
                                  tile_ps(tau, SEQ).rearrange("p (c r) -> p c r", r=ROWS)
                                  ).then_inc(tile_v.handle, tile_v.made(("tile", tau)))
                    dve.wait_ge(tile_v.handle, tile_v.after(("tile", tau)))
                    if n > SEQ or g == 0:
                        dve.wait_ge(pooled_s.handle, pooled_s.after(("zero", l)) + (g + 1 if n > SEQ and False else 0))
                    w = 2 << g
                    src = u_pad[:, g, :]
                    for e in range(g + 1):
                        reach = 1 << (g - e) >> 0
                        d_ = (1, 1, 2, 4)[e]
                        lo_ = 1 if e == 0 else None
                        dst = win[:, e % 2, :]
                        if n > SEQ or e:
                            dve.wait_ge(pooled_s.handle, pooled_s.after(("u", l, g, e - 1)))
                        for t_, b_, len_ in offs:
                            m_ = (7, 6, 4, 0)[e]
                            a0, a1 = b_ - m_, b_ + len_ + m_
                            if e == 0:
                                i0, i1 = src[:, a0 - 1:a1 - 1], src[:, a0:a1]
                            else:
                                i0, i1 = src[:, a0 - d_:a1 - d_], src[:, a0 + d_:a1 + d_]
                            V.tensor_tensor(dst[:, a0:a1], i0, i1, ALU.add).then_inc(pooled_s.handle, pooled_s.made(("u", l, g, e)))
                        src = dst
                        if e == 0:
                            pass
                    dve.wait_ge(pooled_s.handle, pooled_s.after(("u", l, g, g)))
                    for t_, b_, len_ in offs:
                        V.tensor_tensor(src[:, b_:b_ + w // 2], src[:, b_:b_ + w // 2], edge[:, g, 0, 0:w // 2], ALU.mult
                                        ).then_inc(pooled_s.handle, pooled_s.made())
                        if w > 2:
                            e0, e1 = b_ + len_ - w // 2 + 1, b_ + len_
                            V.tensor_tensor(src[:, e0:e1], src[:, e0:e1], edge[:, g, 1, 0:w // 2 - 1], ALU.mult
                                            ).then_inc(pooled_s.handle, pooled_s.made())
                    pooled_s.seen["e", l, g] = pooled_s.count
                    dve.wait_ge(pooled_s.handle, pooled_s.after(("e", l, g)))
                    if n > SEQ:
                        o = SEQ + 3 * UPAD
                        V.scalar_tensor_tensor(out=pooled[:, g, SEQ:TOK], in0=src[:, o:o + CTX], scalar=1.0 / w, in1=u_pad[:, g, o:o + CTX],
                                               op0=ALU.mult, op1=ALU.subtract).then_inc(pooled_s.handle, pooled_s.made())
                    V.scalar_tensor_tensor(out=pooled[:, g, 0:SEQ].rearrange("p (c r) -> p c r", r=ROWS),
                                           in0=src[:, UPAD:UPAD + SEQ].rearrange("p (r c) -> p c r", r=ROWS), scalar=1.0 / w,
                                           in1=u_pad[:, g, UPAD:UPAD + SEQ].rearrange("p (r c) -> p c r", r=ROWS),
                                           op0=ALU.mult, op1=ALU.subtract).then_inc(pooled_s.handle, pooled_s.made((l, g, "p")))
                    dve.wait_ge(pooled_s.handle, pooled_s.after((l, g, "p")))
                for g in range(WC):
                    b = 2048 + 1024 * (g % 2)
                    dve.wait_ge(act_hi.handle, act_hi.after(("ob", l, g)))
                    V.scalar_tensor_tensor(out=o_lo[:, g, 0:n], in0=psf[:, b:b + n], scalar=vecs[:, P_SC + WC * l + g:P_SC + WC * l + g + 1],
                                           in1=ob_hi[:, g, 0:n], op0=ALU.mult, op1=ALU.subtract
                                           ).then_inc(act_lo.handle, act_lo.made(("ob", l, g)))
                mix("branch1", 1)

                def residual(name, six):
                    t0 = TILE[name, l]
                    for c in range(KC):
                        dve.wait_ge(tile_made.handle, t0 + c + 1)
                        for s, (a0, a1) in enumerate(segs(n)):
                            V.scalar_tensor_tensor(out=x[:, c, a0:a1], in0=tile_ps(t0 + c, a1, a0), scalar=mods[:, l, six, c, s:s + 1],
                                                   in1=x[:, c, a0:a1], op0=ALU.mult, op1=ALU.add
                                                   ).then_inc(tile_v.handle, tile_v.made(("tile", t0 + c)))

                residual("out", 2)
                dve.wait_ge(tile_v.handle, tile_v.after(("tile", TILE["out", l] + 7)))
                norm_v(l, 1, n)
                for g in range(4):
                    hh_, hl_, hf_ = hid[g % 2]
                    for c in range(KC):
                        dve.wait_ge(tile_a.handle, tile_a.after(("tile", TILE[f"up{g}", l] + c)))
                        V.tensor_tensor(hf_[:, c, 0:n], hf_[:, c, 0:n], hf_[:, c, 0:n], ALU.mult).then_inc(hid_s.handle, hid_s.made(("sq", l, g, c)))
                        dve.wait_ge(hid_s.handle, hid_s.after(("sq", l, g, c)))
                        V.tensor_copy(hh_[:, c, 0:n], hf_[:, c, 0:n]).then_inc(hid_s.handle, hid_s.made(("hi", l, g, c)))
                        dve.wait_ge(hid_s.handle, hid_s.after(("hi", l, g, c)))
                        V.tensor_tensor(hl_[:, c, 0:n], hf_[:, c, 0:n], hh_[:, c, 0:n], ALU.subtract
                                        ).then_inc(act_lo.handle, act_lo.made(("hid", l, g, c)))
                    residual(f"down{g}", 5)
                    dve.wait_ge(tile_v.handle, tile_v.after(("tile", TILE[f"down{g}", l] + 7)))
            norm_v(DEPTH, 2, SEQ)
            for i in range(4):
                for e in range(2):
                    dve.wait_ge(turned.handle, turned.after(("y", i, e)))
                    V.tensor_copy(x_rows[:, i, 512 * e:512 * e + 512], ps[:, 4 + e, :]).then_inc(turn_v.handle, turn_v.made(("y", i, e)))

        return count.counted()


def load_ada_l(sp, a, ring, l, t, j):
    return sp.dma_start(ring[:, j, :, :], a["w_ada"][l].rearrange("(k p) n -> p k n", p=P)[:, :, bass.ts(t, 256)])


_FLAT = ("b_ada", "g_mix", "g_mlp", "g_final", "pool_scale", "g_subln", "c", "c_ctx")
_INS = ("x", "c", "ctx", "c_ctx", "w_ada", "b_ada", "g_mix", "g_mlp", "w_in", "lambda_q1", "lambda_k1", "lambda_q2", "lambda_k2",
        "g_subln", "pool_w", "pool_scale", "nat_rpb", "w_branch", "w_out", "w_mlp1", "w_mlp2", "g_final")


def shape_constants():
    import numpy as np

    t = np.arange(SEQ)
    row, col = t % ROWS, t // ROWS
    nf = 16
    inv = np.float32(10000.0) ** (-np.arange(nf, dtype=np.float32) / np.float32(nf))
    p = np.arange(P)
    pos = np.where(((p // 32) % 2 == 0)[:, None], row[None, :], col[None, :]).astype(np.float32)
    ang = pos * inv[p % 16][:, None]
    sign = np.where((p % 32) < 16, -1.0, 1.0).astype(np.float32)[:, None]
    mask = np.full((P, 640), -1e30, np.float32)
    for kind, g, o, c0 in ((0, 0, MASKO[0], 0), (1, 1, MASKO[1], 8), (2, 3, MASKO[2], 40)):
        for part in range(P):
            cq = 16 * g + part // 8
            w0 = min(max(cq - 8, 0), COLS - 16)
            for j in range(MASKW[kind]):
                if w0 <= c0 + j // 8 < w0 + 16:
                    mask[part, o + j] = 0.0
    edge = np.ones((4, 2, 8), np.float32)
    for g in range(4):
        w = 2 << g
        for i in range(w // 2):
            edge[g, 0, i] = w / (i + w // 2)
            if i < w // 2 - 1:
                edge[g, 1, i] = w / (w // 2 - 1 - i + w // 2)
    return {"c_ident": np.eye(P, dtype=np.float32), "c_mask": mask, "c_cos": np.cos(ang).astype(np.float32),
            "c_sin": (np.sin(ang) * sign).astype(np.float32), "c_edge": np.ascontiguousarray(np.broadcast_to(edge, (P, 4, 2, 8)))}


def kernel(**inputs):
    import numpy as np
    import concourse.bacc as bacc
    from concourse.bass_utils import run_bass_kernel_spmd

    arrays = dict(shape_constants())
    for name in _INS:
        v = np.ascontiguousarray(inputs[name])
        if name == "nat_rpb":
            v = np.ascontiguousarray(v[:, :, ::-1].transpose(0, 2, 1, 3))
        arrays[name] = v.reshape(-1) if name in _FLAT else v.reshape(v.shape[-2:]) if name in ("x", "ctx") else v

    def build(known):
        nc = bacc.Bacc("TRN2", target_bir_lowering=False, num_devices=1, dynamic_dma_scratch_size=64)
        a = {n: nc.dram_tensor(f"in_{n}", v.shape, mybir.dt.from_np(v.dtype), kind="ExternalInput").ap() for n, v in arrays.items()}
        out = nc.dram_tensor("out_0", (SEQ, D), F32, kind="ExternalOutput").ap()
        return nc, hybrid_block(nc, a, out, known)

    _, counted = build({})
    nc, again = build(counted)
    assert again == counted
    r = run_bass_kernel_spmd(nc, [{f"in_{n}": v for n, v in arrays.items()}], core_ids=[0])
    return r.results[0]["out_0"].reshape(1, SEQ, D)
```

```python
import math
from contextlib import ExitStack

import concourse.bass as bass
from concourse import mybir

ALU = mybir.AluOpType
ACT = mybir.ActivationFunctionType
F32 = mybir.dt.float32
F32R = mybir.dt.float32r
AX_X = mybir.AxisListType.X

P = 128
DEPTH = 2
D = 1024
KC = D // P
SEQ, CTX = 512, 256
TOK = SEQ + CTX
ROWS, COLS = 8, 64
DH, DW = 64, 512
WC = DW // P
HEADS = 4
IN_A, IN_P, IN_N, IN_G = 0, 3 * DW, 4 * DW, 7 * DW
DFF = 4 * D
EPS = 1e-6
SCALE = DH ** -0.5
RING = 4
UNIT = 1024
ADA_UNITS = 6 * D // P
ADA_FIRST = 20
X_TURN = 10
MASKW = (192, 256, 192)
MASKO = (0, 192, 448)
UPAD = 8
UW = SEQ + 2 * UPAD + CTX + 2 * UPAD


class Signal:

    def __init__(self, handle, known):
        self.handle, self.known, self.count, self.seen = handle, known, 0, {}

    def made(self, key=None, by=1):
        self.count += by
        self.seen[key] = self.count
        return by

    def after(self, key):
        return self.known.get(key, 1)


class Counter:

    def __init__(self, nc, ctx, known):
        self.nc, self.ctx, self.known, self.signals = nc, ctx, known, {}

    def __call__(self, name):
        s = Signal(self.ctx.enter_context(self.nc.semaphore(name)), self.known.get(name, {}))
        self.signals[name] = s
        return s

    def counted(self):
        return {n: dict(s.seen) for n, s in self.signals.items()}


class Plan:

    def __init__(self):
        self.phases = [("ada", 0, "a" * ADA_FIRST)]
        for l in range(DEPTH):
            two = "aagg" if l == 0 else "gg"
            self.phases += [("in_a", l, two * 6), ("branch0", l, "ggggbb" * 2), ("in_n", l, two * 6),
                            ("branch2", l, "ggggbb" * 2), ("in_p", l, two * 2), ("branch1", l, "ggggbb" * 2), ("out", l, "g" * 8)]
            for g in range(4):
                self.phases += [(f"up{g}", l, two * 4), (f"down{g}", l, (two if g < 2 else "gg") * 4)]
        self.first, self.tile0, self.ada0, self.event0, self.kinds = {}, {}, {}, {}, {}
        self.tile_event, self.tile_unit, self.unit_event = [], [], []
        ada = event = 0
        for name, l, kinds in self.phases:
            at = name, l
            self.first[at], self.tile0[at], self.ada0[at], self.event0[at] = len(self.unit_event), len(self.tile_event), ada, event
            self.kinds[at] = kinds
            for kind in kinds:
                for _ in range(2 if kind == "b" else 1):
                    event += 1
                    if kind != "a":
                        self.tile_event.append(event)
                        self.tile_unit.append(len(self.unit_event))
                ada += kind == "a"
                self.unit_event.append(event)
        self.units = len(self.unit_event)
        assert ada == DEPTH * ADA_UNITS and not self.units % RING


def hybrid_block(nc, a, out, known):
    plan = Plan()
    FIRST, TILE, UNITS = plan.first, plan.tile0, plan.units
    with ExitStack() as ctx:
        base = (nc.sbuf_base + 31) // 32 * 32
        X0 = base
        H0 = X0 + KC * TOK * 4
        RAW0 = H0 + 2 * KC * TOK * 4
        WH0 = RAW0 + RING * UNIT * 4
        WL0 = WH0 + RING * UNIT * 4
        QK0 = WL0 + RING * UNIT * 4
        M0 = QK0 + 2 * WC * TOK * 4
        V0 = M0 + KC * TOK * 4
        OL0 = V0 + 7 * DW * 4
        WK0 = OL0 + WC * TOK * 4
        C0 = WK0 + 24576

        def at(name, shape, dt, off):
            return nc.alloc_sbuf_tensor_at(name, [P] + shape, dt, offset=off)

        x = at("x", [KC, TOK], F32, X0)
        h_hi = at("h_hi", [KC, TOK], F32R, H0)
        h_lo = at("h_lo", [KC, TOK], F32R, H0 + KC * TOK * 4)
        h_f = at("h_f", [KC, TOK], F32, H0 + KC * TOK * 4)
        raw = at("raw", [RING, UNIT], F32, RAW0)
        w_hi = at("w_hi", [RING, UNIT], F32R, WH0)
        w_lo = at("w_lo", [RING, UNIT], F32R, WL0)
        q = at("q", [WC, TOK], F32, QK0)
        k = at("k", [WC, TOK], F32, QK0 + WC * TOK * 4)
        x_rows = at("x_rows", [6, D], F32, QK0)
        u_pad = at("u_pad", [WC, UW], F32, QK0)
        win = at("win", [2, UW], F32, QK0 + WC * UW * 4)
        o_hi = at("o_hi", [WC, TOK], F32R, QK0)
        m_hi = at("m_hi", [KC, TOK], F32R, QK0)
        m_f = at("m_f", [KC, TOK], F32, M0)
        m_lo = at("m_lo", [KC, TOK], F32R, M0)
        cos = at("cos", [SEQ], F32, M0)
        sin = at("sin", [SEQ], F32, M0 + 4 * SEQ)
        rope_t = at("rope_t", [2, SEQ], F32, M0 + 8 * SEQ)
        rms_o = at("rms_o", [HEADS, TOK], F32, WK0 + 16 * TOK)
        o_mean = [at("o_mean0", [2, TOK], F32, V0), at("o_mean1", [2, TOK], F32, V0 + 8 * TOK)]
        v = at("v", [7, DW], F32, V0)
        v_f = at("v_f", [WC, TOK], F32, OL0)
        o_f = at("o_f", [WC, TOK], F32, OL0)
        o_lo = at("o_lo", [WC, TOK], F32R, OL0)
        pooled = at("pooled", [WC, TOK], F32, OL0)
        probs_a = at("probs_a", [2, 2, TOK], F32, WK0)
        probsT_a = at("probsT_a", [2, 6, 2 * P], F32, WK0 + 16 * TOK)
        probs_n = at("probs_n", [3, 512], F32, WK0)
        probsT_n = at("probsT_n", [2, 4, P], F32, WK0 + 6144)
        bias_raw = at("bias_raw", [8, 8, 32], F32, WK0 + 10240)
        bias = at("bias", [2, 640], F32, WK0 + 18432)
        gate = at("gate", [4, TOK], F32, WK0)
        ob_hi = at("ob_hi", [WC, TOK], F32R, WK0 + 4 * TOK * 4)
        pool_w = at("pool_w", [WC, P], F32, WK0)
        square, square_sum, rstd, newton = ([at(f"{name}{i}", shape, F32, o + 4 * TOK * j) for i, o in enumerate((M0 + 16 * SEQ, WK0))]
                                            for name, shape, j in (("square", [2, TOK], 0), ("square_sum", [TOK], 2),
                                                                   ("rstd", [TOK], 3), ("newton", [TOK], 4)))
        ada_rows = at("ada_rows", [2, P], F32, C0 - 8 * P)
        vec_rows = at("vec_rows", [2, P], F32, WK0 + 20 * TOK)
        hid = [(at(f"hid_hi{i}", [KC, TOK], F32R, o), at(f"hid_lo{i}", [KC, TOK], F32R, o + KC * TOK * 4),
                at(f"hid_f{i}", [KC, TOK], F32, o + KC * TOK * 4)) for i, o in enumerate((QK0, V0))]
        off = [C0]

        def const(name, shape, dt=F32):
            n = 1
            for s in shape:
                n *= s
            t = at(name, shape, dt, off[0])
            off[0] += (n * 4 + 31) // 32 * 32
            return t

        ident = const("ident", [P])
        ones = const("ones", [P])
        mask = const("mask", [640])
        mods = const("mods", [DEPTH, 6, KC, 2])
        coef = const("coef", [DEPTH, 2, KC, 2])
        vecs = const("vecs", [66])
        edge = const("edge", [4, 2, 8])
        cond_hl = const("cond_hl", [KC, 4], F32R)
        cond_t = const("cond_t", [KC, 2])
        ada_cols = const("ada_cols", [ADA_FIRST, 4])
        eps = const("eps", [1])
        lam_in = const("lam_in", [DEPTH, 4])
        lam_pr = const("lam_pr", [DEPTH, 2])
        lam_e = const("lam_e", [DEPTH, 2])
        neg_lam = const("neg_lam", [DEPTH])
        g_sub = const("g_sub", [DEPTH])
        softmax_stats = const("softmax_stats", [3, 4])
        neg_max, total, rtotal = (softmax_stats[:, i, :] for i in range(3))
        assert off[0] <= nc.sbuf_usable_end, (off[0], nc.sbuf_usable_end)
        G_MIX, G_MLP, G_FIN, P_SC, G_SUB, COND = 0, 16, 32, 40, 48, 50

        ps = ctx.enter_context(nc.psum_tensor("ps", [P, 8, 512], F32))
        psf = ps[:, :, :].rearrange("p b n -> p (b n)")

        count = Counter(nc, ctx, known)
        consts_in = count("consts_in")
        x_in = count("x_in")
        vecs_in = count("vecs_in")
        lam_loaded = count("lam_loaded")
        setup = count("setup")
        ada_taken = count("ada_taken")
        ada_turned = count("ada_turned")
        ada_out = count("ada_out")
        collected = count("collected")
        first_lo = count("first_lo")
        silu_t = count("silu_t")
        lam_exp = count("lam_exp")
        rope_in = count("rope_in")
        bias_in = count("bias_in")
        pw_in = count("pw_in")
        unit_in = [count(f"unit_in{i}") for i in range(RING)]
        hi_made = count("hi_made")
        lo_made = count("lo_made")
        tile_made = count("tile_made")
        turned = count("turned")
        stat_made = count("stat_made")
        scores_made = count("scores_made")
        pv_made = count("pv_made")
        pool_made = count("pool_made")
        tile_v = count("tile_v")
        tile_a = count("tile_a")
        turn_v = count("turn_v")
        turn_a = count("turn_a")
        rope_s = count("rope_s")
        squared = count("squared")
        root = count("root")
        rstd_v = count("rstd_v")
        normed = count("normed")
        affine = count("affine")
        act_hi = count("act_hi")
        act_lo = count("act_lo")
        biased = count("biased")
        max_made = count("max_made")
        exp_made = count("exp_made")
        rsum = count("rsum")
        probs_made = count("probs_made")
        o_out = count("o_out")
        o_sq = count("o_sq")
        square_v = count("square_v")
        rsq_v = count("rsq_v")
        mixed = count("mixed")
        pooled_s = count("pooled_s")
        hid_s = count("hid_s")
        stored = count("stored")
        block = ctx.enter_context(nc.Block())

        def toks(l):
            return TOK if l + 1 < DEPTH else SEQ

        def segs(n):
            return [(0, SEQ)] + ([(SEQ, TOK)] if n > SEQ else [])

        def tile_ps(tau, n=TOK, lo=0):
            b = 1024 * (tau % 2)
            return psf[:, b + lo:b + n]

        taker = {}
        for name, l, kinds in plan.phases:
            n_tiles = len(kinds.replace("a", "").replace("b", "bb"))
            for j in range(n_tiles):
                by_act = name.startswith("up") or (name.startswith("branch") and j % 8 < 4)
                taker[TILE[name, l] + j] = tile_a if by_act else tile_v

        def wait_tile(eng, tau):
            eng.wait_ge(tile_made.handle, plan.tile_event[tau])

        def wait_lo(eng, u, i=None):
            sem, v0 = (first_lo, u + 1) if u < ADA_FIRST else (lo_made, u + 1 - ADA_FIRST)
            eng.wait_ge(sem.handle, v0 if i is None else i * RING + v0)

        def wait_taken(eng, tau):
            if tau >= 2:
                eng.wait_ge(taker[tau - 2].handle, taker[tau - 2].after(("tile", tau - 2)))

        def diff_items(l):
            items = [(h, P * b, (0, TOK)) for h in range(HEADS) for b in range(SEQ // P)]
            if toks(l) > SEQ:
                items += [(h, SEQ + P * b, (SEQ, TOK)) for h in range(HEADS) for b in range(CTX // P)]
            return items

        def nat_items(l):
            items = []
            for c in range(WC):
                for g in range(4):
                    kind = 0 if g == 0 else 2 if g == 3 else 1
                    k0, k1 = max(0, P * g - 64), min(SEQ, P * g + 192)
                    tiles = {0: [(0, 0, 64), (1, 64, 128)], 2: [(4, 128, 64), (3, 0, 128)],
                             1: [(g, 0, 128), (g + 1, 128, 128)]}[kind]
                    loc = k1 - k0
                    items.append((c, P * g, kind, k0, k1, tiles + [(5, loc, 128), (6, loc + 128, 128)]))
                if toks(l) > SEQ:
                    for b in range(2):
                        items.append((c, SEQ + P * b, None, 0, 0, [(5, 0, 128), (6, 128, 128)]))
            return items

        def o_bank(i):
            return 6 + i % 2

        V_TILES_N = [(0, 64), (64, 128), (192, 128), (320, 128), (448, 64), (512, 128), (640, 128)]
        V_TILES_A = [(P * j, P) for j in range(6)]

        @block.sync
        def _(sp):
            sp.dma_start(ident[:, :], a["c_ident"]).then_inc(consts_in.handle, 16)
            sp.dma_start(mask[:, :], a["c_mask"]).then_inc(consts_in.handle, 16)
            sp.dma_start(edge[:, :, :], a["c_edge"]).then_inc(consts_in.handle, 16)
            rows = [("g_mix", 16), ("g_mlp", 16), ("g_final", 8), ("pool_scale", 8), ("g_subln", 2), ("c", 8), ("c_ctx", 8)]
            r0 = 0
            for name, n in rows:
                sp.dma_start(vec_rows[r0:r0 + n, 0, :], a[name].rearrange("(n p) -> n p", p=P)).then_inc(vecs_in.handle, 16)
                r0 += n
            sp.dma_start(vec_rows[0:96, 1, :], a["b_ada"].rearrange("(n p) -> n p", p=P)).then_inc(vecs_in.handle, 16)
            for i, name in enumerate(("lambda_q1", "lambda_k1", "lambda_q2", "lambda_k2")):
                sp.dma_start(lam_in[0:DH, :, i], a[name].rearrange("l d -> d l"), allow_slow_non_contiguous=True).then_inc(lam_loaded.handle, 16)

            for u in range(RING):
                sp.dma_start(raw[:, u, :].rearrange("p (k n) -> p k n", k=KC),
                             a["w_ada"][0].rearrange("(k p) n -> p k n", p=P)[:, :, P * u:P * u + P]).then_inc(unit_in[u].handle, 16)
            def load_x(r):
                if r < ROWS:
                    sp.dma_start(x_rows[r:P:ROWS, 0:4, :], a["x"][COLS * r:COLS * r + COLS, :].rearrange("(i c) d -> c i d", c=16)
                                 ).then_inc(x_in.handle, 16)
                elif r == ROWS:
                    sp.dma_start(x_rows[:, 4:6, :], a["ctx"].rearrange("(i p) d -> p i d", p=P)).then_inc(x_in.handle, 16)

            load_x(0)
            sp.dma_start(cos[:, :], a["c_cos"]).then_inc(rope_in.handle, 16)
            sp.dma_start(sin[:, :], a["c_sin"]).then_inc(rope_in.handle, 16)

            def load(u, src, rows, i=None):
                wait_lo(sp, u - RING, i)
                dst = raw[:, u % RING, :].rearrange("p (k n) -> p k n", k=rows)
                sp.dma_start(dst, src).then_inc(unit_in[u % RING].handle, 16)

            def cols(w, j, n=P):
                return w.rearrange("(k p) n -> p k n", p=P)[:, :, bass.ts(j, n)]

            for name, l, kinds in plan.phases:
                u0, n = FIRST[name, l], len(kinds)
                w = None
                if name in ("in_a", "in_n", "in_p"):
                    c0 = {"in_a": IN_A, "in_n": IN_N, "in_p": IN_P}[name]
                    w = a["w_in"][l][:, c0:c0 + kinds.count("g") * P]
                elif name == "out":
                    w = a["w_out"][l]
                elif name.startswith("up"):
                    g = int(name[-1])
                    w = a["w_mlp1"][l][:, g * D:(g + 1) * D]
                elif name.startswith("down"):
                    g = int(name[-1])
                    w = a["w_mlp2"][l][g * D:(g + 1) * D, :]
                elif name == "ada":
                    pass
                else:
                    b = int(name[-1])
                    wg = a["w_in"][l][:, IN_G + b * D:IN_G + (b + 1) * D]
                    for half in range(2):
                        for j in range(4):
                            load(u0 + 6 * half + j, cols(wg, 4 * half + j), KC)
                        for j in range(2):
                            load(u0 + 6 * half + 4 + j, cols(a["w_branch"][l, b], 2 * half + j, 256), WC)
                    continue
                if name == "in_a" and l:
                    sp.wait_ge(tile_made.handle, plan.tile_event[TILE["down2", l - 1] + 7])
                    sp.dma_start(cos[:, :], a["c_cos"]).then_inc(rope_in.handle, 16)
                    sp.dma_start(sin[:, :], a["c_sin"]).then_inc(rope_in.handle, 16)
                ada_l, ada_c = divmod(plan.ada0[name, l], ADA_UNITS)
                per = {"a": kinds[:RING].count("a"), "g": kinds[:RING].count("g")}

                def source(j, i=None):
                    kind = kinds[j]
                    c = kinds[:j].count(kind)
                    if kind == "a":
                        return cols(a["w_ada"][ada_l], ada_c + c if i is None else i * per[kind] + (ada_c + c))
                    return w.rearrange("(k p) n -> p k n", p=P)[:, :, bass.ds(P * c if i is None else i * (per[kind] * P) + P * c, P)]

                f = RING if u0 < ADA_FIRST + RING else 0
                if u0 == ADA_FIRST:
                    for j in range(f):
                        load(u0 + j, source(j), KC)
                if name == "ada":
                    for j in range(f, n):
                        load(u0 + j, source(j), KC)
                        load_x(j - f + 1)
                    continue
                with sp.Fori(0, (n - f) // RING) as i:
                    for j in range(f, f + RING):
                        load(u0 + j, source(j, i), KC, i)
                if name == "in_n":
                    sp.wait_ge(biased.handle, biased.after(("clear", l)))
                    for cl in range(16):
                        k0, k1 = max(0, cl - 7), min(32, cl + 24)
                        src = bass.AP(a["nat_rpb"].tensor, a["nat_rpb"].offset + l * 8 * 15 * 31 + k0 + 7 - cl,
                                      [[8 * 31, 8], [31, 64], [1, k1 - k0]])
                        sp.dma_start(bias_raw[8 * cl:8 * cl + 8, :, :, k0:k1].rearrange("p r h c -> p (r h) c"), src).then_inc(bias_in.handle, 16)
                if name == "in_p":
                    sp.wait_ge(tile_v.handle, tile_v.after(("tile", TILE["branch2", l] + 15)))
                    sp.dma_start(pool_w[:, :, :], a["pool_w"][l].rearrange("g c e -> c g e")).then_inc(pw_in.handle, 16)

            for i in range(4):
                sp.wait_ge(turn_v.handle, turn_v.after(("y", i, 1)))
                for r in range(ROWS):
                    sp.dma_start(out[COLS * r + 16 * i:COLS * r + 16 * i + 16, :], x_rows[r:P:ROWS, i, :]).then_inc(stored.handle, 16)
            sp.wait_ge(stored.handle, 16 * 4 * ROWS)

        @block.gpsimd
        def _(pool):
            with pool.Fori(0, (UNITS - ADA_FIRST) // RING) as i:
                for s in range(RING):
                    pool.wait_ge(hi_made.handle, i * RING + (ADA_FIRST + s + 1))
                    nc.gpsimd.tensor_tensor(w_lo[:, s, :], raw[:, s, :], w_hi[:, s, :], ALU.subtract).then_inc(lo_made.handle, 1)

        @block.scalar
        def _(act):
            def split_hi(u, tiles=None):
                if isinstance(u, int):
                    if u >= UNITS:
                        return
                    act.wait_ge(unit_in[u % RING].handle, 16 * (u // RING + 1))
                    if u >= RING:
                        act.wait_ge(tile_made.handle, plan.unit_event[u - RING])
                    s = u % RING
                nc.scalar.activation(w_hi[:, s, :], raw[:, s, :], ACT.Copy).then_inc(hi_made.handle, 1)

            def split_hi_loop(i, u, t):
                s = u % RING
                act.wait_ge(unit_in[s].handle, i * 16 + 16 * (u // RING + 1))
                act.wait_ge(tile_made.handle, i * RING + t)
                nc.scalar.activation(w_hi[:, s, :], raw[:, s, :], ACT.Copy).then_inc(hi_made.handle, 1)

            def take_ada(u, A, i=None):
                act.wait_ge(tile_made.handle, plan.unit_event[u] if i is None else i * RING + plan.unit_event[u])
                if A >= 2:
                    act.wait_ge(ada_turned.handle, A - 1 if i is None else i * 2 + (A - 1))
                nc.scalar.copy(ada_rows[0:4, A % 2, :], ps[0:4, 4 + A % 2, 0:P]).then_inc(ada_taken.handle, 1)

            def stream(name, l, body, begun=False):
                kinds = plan.kinds[name, l]
                n, u0, t0, A0 = len(kinds), FIRST[name, l], plan.event0[name, l], plan.ada0[name, l]
                if body is None and u0 and u0 + n + 3 <= UNITS:
                    j0 = RING if begun else 0
                    for j in range(j0):
                        if j:
                            split_hi(u0 + j + 3)
                        if kinds[j] == "a":
                            take_ada(u0 + j, A0 + kinds[:j].count("a"))
                    with act.Fori(0, (n - j0) // RING) as i:
                        for j in range(j0, j0 + RING):
                            split_hi_loop(i, u0 + j + 3, t0 + j)
                            if kinds[j] == "a":
                                take_ada(u0 + j, A0 + kinds[:j].count("a"), i)
                    return
                for j in range(n):
                    if j or not begun:
                        split_hi(u0 + j + 3)
                    if kinds[j] == "a":
                        take_ada(u0 + j, A0 + kinds[:j].count("a"))
                        if name == "ada" and 0 <= j - X_TURN < KC:
                            squares(0, 0, TOK, [j - X_TURN])
                    elif body:
                        body(kinds[:j].count("g"))

            def squares(l, which, n, chunks):
                for c in chunks:
                    if which == 0 and l == 0:
                        act.wait_ge(turn_v.handle, turn_v.after(("x", c)))
                    else:
                        act.wait_ge(tile_v.handle, tile_v.after(("tile", (TILE["out", l] if which == 1 else TILE["down3", l - 1]) + c)))
                    if c >= 2:
                        act.wait_ge(square_v.handle, square_v.after((l, which, c - 2)))
                    nc.scalar.activation(square[which % 2][:, c % 2, 0:n], x[:, c, 0:n], ACT.Square).then_inc(squared.handle, squared.made(("sq", l, which, c)))

            def rsqrt_act(mean, dst, scale=1.0):
                nc.scalar.activation(dst, mean, ACT.Ln, bias=eps[:, 0:1], scale=scale).then_inc(root.handle, root.made())
                act.wait_ge(root.handle, root.count)
                return nc.scalar.activation(dst, dst, ACT.Exp, scale=-0.5)

            def norm_act(l, which, n):
                act.wait_ge(stat_made.handle, stat_made.after(("sq", l, which)))
                rsqrt_act(psf[:, 3072:3072 + n], rstd[which % 2][:, 0:n]).then_inc(root.handle, root.made((l, which)))
                if which == 2:
                    return
                split_hi(FIRST[("in_a", "up0")[which], l] + 3)
                for c in range(KC):
                    act.wait_ge(normed.handle, normed.after((l, which, c)))
                    for s, (t0, t1) in enumerate(segs(n)):
                        nc.scalar.activation(h_hi[:, c, t0:t1], h_f[:, c, t0:t1], ACT.Identity, bias=mods[:, l, 3 * which, c, s:s + 1]
                                             ).then_inc(act_hi.handle, act_hi.made(("h", l, which, c)))

            act.wait_ge(setup.handle, setup.after("vecs"))
            nc.scalar.activation(cond_t[:, :, :], vecs[:, COND:COND + 16].rearrange("p (s k) -> p k s", s=2), ACT.Tanh,
                                 scale=0.5).then_inc(silu_t.handle, silu_t.made("tanh"))
            act.wait_ge(turned.handle, turned.after("lam"))
            nc.scalar.activation(lam_e[:, :, :], psf[:, 3072:3072 + 2 * DEPTH], ACT.Exp).then_inc(lam_exp.handle, lam_exp.made("exp"))
            for u in range(3):
                split_hi(u)
            act.wait_ge(setup.handle, setup.after("cond"))
            stream("ada", 0, None)

            for l in range(DEPTH):
                n = toks(l)
                norm_act(l, 0, TOK)
                stream("in_a", l, None, begun=True)

                items = diff_items(l)

                def exp_a(i):
                    h, q0, (k0, k1) = items[i]
                    for m in range(2):
                        act.wait_ge(max_made.handle, max_made.after(("a", l, i, m)))
                        if i >= 2:
                            act.wait_ge(turned.handle, turned.after(("a", l, i - 2)))
                        s = (2 * i + m) % 4
                        nc.scalar.activation(probs_a[:, i % 2, m, 0:k1 - k0], psf[:, 1024 * m:1024 * m + k1 - k0], ACT.Exp,
                                             bias=neg_max[:, s:s + 1], accum_out=total[:, s:s + 1]
                                             ).then_inc(exp_made.handle, exp_made.made(("a", l, i, m)))

                def turn_out_a(i):
                    h, q0, (k0, k1) = items[i]
                    act.wait_ge(turned.handle, turned.after(("a4", l, i)))
                    if i >= 4:
                        act.wait_ge(pv_made.handle, pv_made.after(("pv", l, i // 2 - 2)))
                    nb = min(4, (k1 - k0) // P)
                    e = P * (i % 2)
                    nc.scalar.copy(probsT_a[:, i // 2 % 2, 0:nb, e:e + P], ps[:, 4, 0:nb * P]).then_inc(turn_a.handle, turn_a.made(("a", l, i)))

                def take_oa(p):
                    h, q0, _ = items[2 * p]
                    act.wait_ge(pv_made.handle, pv_made.after(("pv", l, p)))
                    nc.scalar.copy(o_f[:, h, q0:q0 + 2 * P], ps[:, 6, 0:2 * P]).then_inc(o_out.handle, o_out.made(("a", l, p)))

                for i in range(len(items) + 3):
                    if i < len(items):
                        exp_a(i)
                    if 1 <= i <= len(items):
                        turn_out_a(i - 1)
                    p, odd = divmod(i - 3, 2)
                    if not odd and 0 <= p < len(items) // 2:
                        take_oa(p)
                assert (len(items) + 2 - 3) // 2 >= len(items) // 2 - 1
                act.wait_ge(o_out.handle, o_out.after(("a", l, len(items) // 2 - 1)))
                for h in range(HEADS):
                    if h >= 2:
                        act.wait_ge(stat_made.handle, stat_made.after(("o", l, h - 2)))
                    nc.scalar.activation(square[0][:, h % 2, 0:n], o_f[:, h, 0:n], ACT.Square).then_inc(o_sq.handle, o_sq.made((l, h)))
                for h in range(HEADS):
                    act.wait_ge(stat_made.handle, stat_made.after(("o", l, h)))
                    b = 2048 + 1024 * (h % 2)
                    nc.scalar.activation(rms_o[:, h, 0:n], psf[:, b:b + n], ACT.Ln, bias=eps[:, 0:1], scale=float(D // P)
                                         ).then_inc(root.handle, root.made(("ln", l, h)))
                for h in range(HEADS):
                    act.wait_ge(root.handle, root.after(("ln", l, h)))
                    nc.scalar.activation(rms_o[:, h, 0:n], rms_o[:, h, 0:n], ACT.Exp, scale=-0.5).then_inc(root.handle, root.made(("o", l, h)))

                def hi_oa(h):
                    act.wait_ge(rsq_v.handle, rsq_v.after(("o", l, h)))
                    nc.scalar.activation(o_hi[:, h, 0:n], o_f[:, h, 0:n], ACT.Copy).then_inc(act_hi.handle, act_hi.made(("oa", l, h)))

                def gates(name):
                    u0, t0 = FIRST[name, l], TILE[name, l]
                    for half in range(2):
                        for j in range(4):
                            split_hi(u0 + 6 * half + j + 3)
                            tau = t0 + 8 * half + j
                            wait_tile(act, tau)
                            if half:
                                act.wait_ge(tile_v.handle, tile_v.after(("tile", t0 + 4 + j)))
                                if name != "branch0":
                                    act.wait_ge(mixed.handle, mixed.after(("m", l, int(name[-1]), j)))
                            nc.scalar.activation(gate[:, j, 0:n], tile_ps(tau, n), ACT.Tanh, scale=0.5
                                                 ).then_inc(tile_a.handle, tile_a.made(("tile", tau)))
                            if name == "branch0" and half == 0:
                                hi_oa(j)
                        for j in range(2):
                            split_hi(u0 + 6 * half + 4 + j + 3)
                            if name == "branch1":
                                for e in range(2):
                                    c = 4 * half + 2 * j + e
                                    act.wait_ge(mixed.handle, mixed.after(("m", l, 1, c)))
                                    nc.scalar.activation(m_hi[:, c, 0:n], m_f[:, c, 0:n], ACT.Copy
                                                         ).then_inc(act_hi.handle, act_hi.made(("m", l, c)))

                gates("branch0")
                stream("in_n", l, None)

                nitems = nat_items(l)
                subs = [(i, hh) for i in range(len(nitems)) for hh in range(2)]

                def exp_n(s):
                    i, hh = subs[s]
                    c, q0, kind, k0, k1, tiles = nitems[i]
                    act.wait_ge(max_made.handle, max_made.after(("n", l, s)))
                    if s >= 3:
                        act.wait_ge(turned.handle, turned.after(("n", l, s - 3)))
                    w = k1 - k0 + CTX
                    nc.scalar.activation(probs_n[:, s % 3, 0:w], ps[:, s % 3, 0:w], ACT.Exp, bias=neg_max[:, s % 4:s % 4 + 1],
                                         accum_out=total[:, s % 4:s % 4 + 1]).then_inc(exp_made.handle, exp_made.made(("n", l, s)))

                def turn_out_n(s):
                    i, hh = subs[s]
                    tiles = nitems[i][5]
                    act.wait_ge(turned.handle, turned.after(("n", l, s)))
                    if s >= 2:
                        act.wait_ge(pv_made.handle, pv_made.after(("pvn", l, s - 2)))
                    nc.scalar.copy(probsT_n[:, s % 2, 0:len(tiles), :], ps[:, 4 + s % 2, 0:len(tiles) * P]
                                   ).then_inc(turn_a.handle, turn_a.made(("n", l, s)))

                def o_hi_n(i):
                    c, q0 = nitems[i][:2]
                    act.wait_ge(pv_made.handle, pv_made.after(("pvn", l, 2 * i + 1)))
                    nc.scalar.activation(o_hi[:, c, q0:q0 + P], ps[:, o_bank(i), 0:P], ACT.Copy
                                         ).then_inc(act_hi.handle, act_hi.made(("on", l, i)))

                for s in range(len(subs) + 5):
                    if s < len(subs):
                        exp_n(s)
                    if 2 <= s < len(subs) + 2:
                        turn_out_n(s - 2)
                    if s >= 5 and s % 2 == 1 and (s - 5) // 2 < len(nitems):
                        o_hi_n((s - 5) // 2)
                gates("branch2")
                stream("in_p", l, None)

                for g in range(WC):
                    act.wait_ge(pool_made.handle, pool_made.after((l, g)))
                    if g == 0:
                        pass
                    b = 2048 + 1024 * (g % 2)
                    nc.scalar.activation(ob_hi[:, g, 0:n], psf[:, b:b + n], ACT.Identity,
                                         scale=vecs[:, P_SC + WC * l + g:P_SC + WC * l + g + 1]
                                         ).then_inc(act_hi.handle, act_hi.made(("ob", l, g)))
                gates("branch1")
                stream("out", l, lambda j: squares(l, 1, n, [j - 1] if j else []))
                squares(l, 1, n, [KC - 1])
                norm_act(l, 1, n)
                for g in range(4):
                    t0 = TILE[f"up{g}", l]

                    def relu(j):
                        wait_tile(act, t0 + j)
                        nc.scalar.activation(hid[g % 2][2][:, j, 0:n], tile_ps(t0 + j, n), ACT.Relu
                                             ).then_inc(tile_a.handle, tile_a.made(("tile", t0 + j)))

                    stream(f"up{g}", l, relu, begun=g == 0)
                    nxt = (DEPTH, 2, SEQ) if l == DEPTH - 1 else (l + 1, 0, TOK)
                    stream(f"down{g}", l, (lambda j: squares(*nxt, [j - 1] if j else [])) if g == 3 else None)
                squares(*nxt, [KC - 1])
            norm_act(DEPTH, 2, SEQ)

        @block.tensor
        def _(pe):
            def product(tau, s, hi, lo, n, kc=KC, col=0, width=P, ready=None):
                for c in range(kc):
                    if ready:
                        ready(c)
                    wh = w_hi[:, s, c * width + col:c * width + col + P]
                    wl = w_lo[:, s, c * width + col:c * width + col + P]
                    for step, (w, act_) in enumerate(((wh, hi), (wh, lo), (wl, hi))):
                        for t0, t1 in segs(n):
                            m = pe.matmul(psf[:, 1024 * (tau % 2) + t0:1024 * (tau % 2) + t1], lhsT=w, rhs=act_[:, c, t0:t1],
                                          start=c == 0 and step == 0, stop=c == kc - 1 and step == 2)
                return m

            def tile(tau, *args, **kw):
                u = plan.tile_unit[tau]
                wait_taken(pe, tau)
                wait_lo(pe, u)
                product(tau, u % RING, *args, **kw).then_inc(tile_made.handle, 1)

            def tile_pair(tau, hi, lo, n, ready):
                for t in (tau, tau + 1):
                    wait_taken(pe, t)
                    wait_lo(pe, plan.tile_unit[t])
                for c in range(KC):
                    ready(c)
                    for t in (tau, tau + 1):
                        s = plan.tile_unit[t] % RING
                        wh, wl = w_hi[:, s, P * c:P * c + P], w_lo[:, s, P * c:P * c + P]
                        for step, (w, act_) in enumerate(((wh, hi), (wh, lo), (wl, hi))):
                            for t0, t1 in segs(n):
                                m = pe.matmul(psf[:, 1024 * (t % 2) + t0:1024 * (t % 2) + t1], lhsT=w, rhs=act_[:, c, t0:t1],
                                              start=c == 0 and step == 0, stop=c == KC - 1 and step == 2)
                        if c == KC - 1:
                            m.then_inc(tile_made.handle, 1)

            def ada(u, A, i=None):
                if A >= 2:
                    pe.wait_ge(ada_taken.handle, A - 1 if i is None else i * 2 + (A - 1))
                wait_lo(pe, u, i)
                s, bank = u % RING, 4 + A % 2
                for c in range(KC):
                    pe.matmul(ps[0:4, bank, 0:P], lhsT=cond_hl[:, c, :], rhs=w_hi[:, s, P * c:P * c + P], start=c == 0, stop=False)
                    m = pe.matmul(ps[0:2, bank, 0:P], lhsT=cond_hl[:, c, 0:2], rhs=w_lo[:, s, P * c:P * c + P], start=False, stop=c == KC - 1)
                m.then_inc(tile_made.handle, 1)

            def ada_turnable(A, i=None):
                pe.wait_ge(ada_taken.handle, A + 1 if i is None else i * 2 + (A + 1))
                if A >= 2:
                    pe.wait_ge(ada_out.handle, A - 1 if i is None else i * 2 + (A - 1))

            def turn_ada(A):
                pe.transpose(ps[:, 6 + A % 2, 0:4], ada_rows[0:4, A % 2, :], ident[0:4, 0:4]).then_inc(ada_turned.handle, 1)

            def phase_loop(name, l, n_tok, hi, lo, ready, pair=False):
                kinds = plan.kinds[name, l]
                n, u0, t0, A0 = len(kinds), FIRST[name, l], TILE[name, l], plan.ada0[name, l]
                per, a_per = kinds[:RING].count("g"), kinds[:RING].count("a")
                tok = n_tok if callable(n_tok) else lambda j: n_tok
                peel = RING if per == RING else 2 * RING
                for j in range(peel):
                    g, A = kinds[:j].count("g"), kinds[:j].count("a")
                    if kinds[j] == "a":
                        ada(u0 + j, A0 + A)
                    else:
                        if not pair or g > 1:
                            tile(t0 + g, hi, lo, tok(g), ready=ready if g == 0 else None)
                        elif g:
                            tile_pair(t0, hi, lo, tok(0), ready)
                        for t in range(0 if pair and g == 1 else g, g + 1) if a_per and not (pair and g == 0) else ():
                            ada_turnable(A0 + t)
                            turn_ada(A0 + t)
                if n <= peel:
                    return
                tk = taker[t0 + WC - 2]
                v0 = tk.after(("tile", t0 + WC - 2))
                by = max(1, tk.after(("tile", t0 + WC - 1)) - v0)
                with pe.Fori(0, (n - peel) // RING) as i:
                    for j in range(peel, peel + RING):
                        g, A = kinds[:j].count("g"), kinds[:j].count("a")
                        if kinds[j] == "a":
                            ada(u0 + j, A0 + A, i)
                        else:
                            pe.wait_ge(tk.handle, i * (per * by) + (v0 + (g - WC) * by))
                            wait_lo(pe, u0 + j, i)
                            product(t0 + g, (u0 + j) % RING, hi, lo, tok(g),
                                    ready=(lambda c: ada_turnable(A0 + g, i) if c == KC - 1 else None) if a_per else None
                                    ).then_inc(tile_made.handle, 1)
                            if a_per:
                                turn_ada(A0 + g)

            pe.wait_ge(vecs_in.handle, 16 * 8)
            pe.wait_ge(consts_in.handle, 48)
            pe.transpose(ps[:, 5, 64:64 + 66], vec_rows[0:66, 0, :], ident[0:66, 0:66]).then_inc(turned.handle, turned.made("vec0"))
            pe.transpose(ps[:, 5, 192:192 + 96], vec_rows[0:96, 1, :], ident[0:96, 0:96]).then_inc(turned.handle, turned.made("vec1"))
            pe.wait_ge(setup.handle, setup.after("lam_pr"))
            pe.matmul(ps[:, 6, 0:2 * DEPTH], lhsT=ones[0:DH, :], rhs=lam_pr[0:DH, :, :].rearrange("p a b -> p (a b)"), start=True, stop=True
                      ).then_inc(turned.handle, turned.made("lam"))
            pe.wait_ge(setup.handle, setup.after("cond"))
            for A in range(ADA_FIRST):
                ada(A, A)
                if A:
                    ada_turnable(A - 1)
                    turn_ada(A - 1)
                if A == X_TURN:
                    pe.wait_ge(x_in.handle, 16 * (ROWS + 1))
                    for c in range(KC):
                        if c >= 2:
                            pe.wait_ge(turn_v.handle, turn_v.after(("x", c - 2)))
                        for i in range(6):
                            m = pe.transpose(psf[:, 1024 * (c % 2) + P * i:1024 * (c % 2) + P * i + P], x_rows[:, i, P * c:P * c + P], ident[:, :])
                        m.then_inc(turned.handle, turned.made(("x", c)))
            ada_turnable(ADA_FIRST - 1)
            turn_ada(ADA_FIRST - 1)

            def mean_squares(l, which, n):
                pe.wait_ge(square_v.handle, square_v.after((l, which, KC - 1)))
                if l == 0 and which == 0:
                    pe.wait_ge(ada_out.handle, ADA_FIRST)
                for t0, t1 in segs(n):
                    m = pe.matmul(psf[:, 3072 + t0:3072 + t1], lhsT=ones[:, :], rhs=square_sum[which % 2][:, t0:t1], start=True, stop=True)
                m.then_inc(stat_made.handle, stat_made.made(("sq", l, which)))

            def h_ready(l, which):
                def ready(c):
                    pe.wait_ge(act_lo.handle, act_lo.after(("h", l, which, c)))
                return ready

            def values(l, tiles, key):
                for j, (t0, nk) in enumerate(tiles):
                    if j < 2:
                        last = taker[TILE[key, l] + 11]
                        pe.wait_ge(last.handle, last.after(("tile", TILE[key, l] + 11)))
                    else:
                        pe.wait_ge(turn_v.handle, turn_v.after((key, l, j - 2)))
                    for c in range(WC):
                        m = pe.transpose(ps[0:nk, 4 + j % 2, P * c:P * c + P], v_f[:, c, t0:t0 + nk], ident[:, :])
                    m.then_inc(turned.handle, turned.made((key, l, j)))

            for l in range(DEPTH):
                n = toks(l)
                mean_squares(l, 0, TOK)
                phase_loop("in_a", l, TOK if n == TOK else (lambda j: n if j < WC else TOK), h_hi, h_lo, h_ready(l, 0), pair=True)
                values(l, V_TILES_A, "in_a")

                items = diff_items(l)

                def scores_a(i):
                    h, q0, (k0, k1) = items[i]
                    for m in range(2):
                        if i:
                            pe.wait_ge(exp_made.handle, exp_made.after(("a", l, i - 1, m)))
                        lo_, hi_ = DH * m, DH * m + DH
                        for t0, t1 in ([(0, SEQ)] if k0 == 0 else []) + [(SEQ, TOK)]:
                            mm = pe.matmul(psf[:, 1024 * m + t0 - k0:1024 * m + t1 - k0], lhsT=q[lo_:hi_, h, q0:q0 + P],
                                           rhs=k[lo_:hi_, h, t0:t1], start=True, stop=True)
                        mm.then_inc(scores_made.handle, scores_made.made(("a", l, i, m)))

                def turn_pa(i):
                    h, q0, (k0, k1) = items[i]
                    nb = (k1 - k0) // P
                    pe.wait_ge(probs_made.handle, probs_made.after(("a", l, i)))
                    if i:
                        pe.wait_ge(turn_a.handle, turn_a.after(("a", l, i - 1)))
                        if items[i - 1][2][0] == 0:
                            pe.wait_ge(turn_v.handle, turn_v.after(("a", l, i - 1)))
                    else:
                        pe.wait_ge(turn_v.handle, turn_v.after(("in_a", l, 5)))
                    for b in range(nb):
                        mm = pe.transpose(ps[:, 4 + b // 4, P * (b % 4):P * (b % 4) + P], probs_a[:, i % 2, 0, P * b:P * b + P], ident[:, :])
                        if b == min(nb, 4) - 1:
                            mm.then_inc(turned.handle, turned.made(("a4", l, i)))
                            turned.seen["a", l, i] = turned.count
                        if b == 5:
                            mm.then_inc(turned.handle, turned.made(("a", l, i)))

                def weighted_a(p):
                    h, q0, (k0, k1) = items[2 * p]
                    nb = (k1 - k0) // P
                    pe.wait_ge(turn_a.handle, turn_a.after(("a", l, 2 * p + 1)))
                    if nb > 4:
                        pe.wait_ge(turn_v.handle, turn_v.after(("a", l, 2 * p + 1)))
                    if p:
                        pe.wait_ge(o_out.handle, o_out.after(("a", l, p - 1)))
                    elif l == 0:
                        pe.wait_ge(ada_out.handle, plan.ada0["in_a", 0] + plan.kinds["in_a", 0].count("a"))
                    for b in range(nb):
                        mm = pe.matmul(ps[:, 6, 0:2 * P], lhsT=v[:, k0 // P + b, P * h:P * h + P], rhs=probsT_a[:, p % 2, b, :],
                                       start=b == 0, stop=b == nb - 1)
                    mm.then_inc(pv_made.handle, pv_made.made(("pv", l, p)))

                def square_mean_o(h):
                    pe.wait_ge(o_sq.handle, o_sq.after((l, h)))
                    if h < 2:
                        pe.wait_ge(o_out.handle, o_out.after(("a", l, len(items) // 2 - 1)))
                    else:
                        pe.wait_ge(rsq_v.handle, rsq_v.after(("o1", l, h - 2)))
                    b = 2048 + 1024 * (h % 2)
                    for t0, t1 in segs(n):
                        mm = pe.matmul(psf[:, b + t0:b + t1], lhsT=ones[:, :], rhs=square[0][:, h % 2, t0:t1], start=True, stop=True)
                    mm.then_inc(stat_made.handle, stat_made.made(("o", l, h)))

                for i in range(len(items) + 5):
                    if i < len(items):
                        scores_a(i)
                    if 1 <= i <= len(items):
                        turn_pa(i - 1)
                    p, odd = divmod(i - 3, 2)
                    if not odd and 0 <= p < len(items) // 2:
                        weighted_a(p)

                def branch(name, hi, lo, ready):
                    t0 = TILE[name, l]
                    for half in range(2):
                        for j in range(4):
                            if name == "branch0" and half == 0 and j < 2:
                                square_mean_o(2 * j)
                                square_mean_o(2 * j + 1)
                            tile(t0 + 8 * half + j, h_hi, h_lo, n)
                        for j in range(2):
                            for e in range(2):
                                tile(t0 + 8 * half + 4 + 2 * j + e, hi, lo, n, kc=WC, col=P * e, width=2 * P,
                                     ready=ready if half + j + e == 0 else None)

                branch("branch0", o_hi, o_lo, lambda c: pe.wait_ge(act_lo.handle, act_lo.after(("o", l, c))))
                phase_loop("in_n", l, TOK if n == TOK else (lambda j: n if j < WC else TOK), h_hi, h_lo, None)
                values(l, V_TILES_N, "in_n")

                nitems = nat_items(l)
                subs = [(i, hh) for i in range(len(nitems)) for hh in range(2)]

                def scores_n(s):
                    i, hh = subs[s]
                    c, q0, kind, k0, k1, tiles = nitems[i]
                    if s >= 3:
                        pe.wait_ge(exp_made.handle, exp_made.after(("n", l, s - 3)))
                    lo_, hi_ = DH * hh, DH * hh + DH
                    loc = k1 - k0
                    if loc:
                        pe.matmul(ps[:, s % 3, 0:loc], lhsT=q[lo_:hi_, c, q0:q0 + P], rhs=k[lo_:hi_, c, k0:k1], start=True, stop=True)
                    pe.matmul(ps[:, s % 3, loc:loc + CTX], lhsT=q[lo_:hi_, c, q0:q0 + P], rhs=k[lo_:hi_, c, SEQ:TOK],
                              start=True, stop=True).then_inc(scores_made.handle, scores_made.made(("n", l, s)))

                def turn_pn(s):
                    i, hh = subs[s]
                    tiles = nitems[i][5]
                    pe.wait_ge(probs_made.handle, probs_made.after(("n", l, s)))
                    if s >= 2:
                        pe.wait_ge(turn_a.handle, turn_a.after(("n", l, s - 2)))
                    else:
                        pe.wait_ge(turn_v.handle, turn_v.after(("in_n", l, 6)))
                    for b, (j, off_, nk) in enumerate(tiles):
                        mm = pe.transpose(ps[0:nk, 4 + s % 2, P * b:P * b + P], probs_n[:, s % 3, off_:off_ + nk], ident[:, :])
                    mm.then_inc(turned.handle, turned.made(("n", l, s)))

                def weighted_n(s):
                    i, hh = subs[s]
                    c, q0, kind, k0, k1, tiles = nitems[i]
                    pe.wait_ge(turn_a.handle, turn_a.after(("n", l, s)))
                    if i >= 2 and hh == 0:
                        pe.wait_ge(act_lo.handle, act_lo.after(("on", l, i - 2)))
                    if s == 0 and l == 0:
                        pe.wait_ge(ada_out.handle, plan.ada0["in_n", 0] + plan.kinds["in_n", 0].count("a"))
                    h = 2 * c + hh
                    for b, (j, off_, nk) in enumerate(tiles):
                        mm = pe.matmul(ps[DH * hh:DH * hh + DH, o_bank(i), 0:P], lhsT=v[0:nk, j, DH * h:DH * h + DH],
                                       rhs=probsT_n[0:nk, s % 2, b, :], start=b == 0, stop=b == len(tiles) - 1)
                    mm.then_inc(pv_made.handle, pv_made.made(("pvn", l, s)))

                for s in range(len(subs) + 3):
                    if s < len(subs):
                        scores_n(s)
                    if 2 <= s < len(subs) + 2:
                        turn_pn(s - 2)
                    if s >= 3:
                        weighted_n(s - 3)
                per_c = len(nitems) // WC
                branch("branch2", o_hi, o_lo, lambda c: pe.wait_ge(act_lo.handle, act_lo.after(("on", l, per_c * c + per_c - 1))))
                phase_loop("in_p", l, n, h_hi, h_lo, None)
                pe.wait_ge(pw_in.handle, 16 * (l + 1))
                for g in range(WC):
                    pe.wait_ge(pooled_s.handle, pooled_s.after((l, g, "p")))
                    if g >= 2:
                        pe.wait_ge(act_lo.handle, act_lo.after(("ob", l, g - 2)))
                    if g == 1 and l == 0:
                        pe.wait_ge(ada_out.handle, plan.ada0["in_p", 0] + plan.kinds["in_p", 0].count("a"))
                    b = 2048 + 1024 * (g % 2)
                    for t0, t1 in segs(n):
                        mm = pe.matmul(psf[:, b + t0:b + t1], lhsT=pool_w[:, g, :], rhs=pooled[:, g, t0:t1], start=True, stop=True)
                    mm.then_inc(pool_made.handle, pool_made.made((l, g)))
                branch("branch1", ob_hi, o_lo, lambda c: pe.wait_ge(act_lo.handle, act_lo.after(("ob", l, c))))
                phase_loop("out", l, n, m_hi, m_lo, lambda c: pe.wait_ge(act_lo.handle, act_lo.after(("m", l, c))))
                mean_squares(l, 1, n)
                for g in range(4):
                    hh_, hl_, _ = hid[g % 2]
                    phase_loop(f"up{g}", l, n, h_hi, h_lo, h_ready(l, 1) if g == 0 else None, pair=g == 0)
                    phase_loop(f"down{g}", l, n, hh_, hl_, lambda c: pe.wait_ge(act_lo.handle, act_lo.after(("hid", l, g, c))))
            mean_squares(DEPTH, 2, SEQ)
            for i in range(4):
                for e in range(2):
                    if i * 2 + e >= 2:
                        pi, pe_ = divmod(i * 2 + e - 2, 2)
                        pe.wait_ge(turn_v.handle, turn_v.after(("y", pi, pe_)))
                    for c in range(4 * e, 4 * e + 4):
                        pe.wait_ge(normed.handle, normed.after(("fin", c)))
                        mm = pe.transpose(ps[:, 4 + e, P * (c % 4):P * (c % 4) + P], x[:, c, P * i:P * i + P], ident[:, :])
                    mm.then_inc(turned.handle, turned.made(("y", i, e)))

        @block.vector
        def _(dve):
            V = nc.vector
            V.memset(ones[:, :], 1.0).then_inc(setup.handle, setup.made())
            V.memset(eps[:, :], EPS).then_inc(setup.handle, setup.made("ones"))
            dve.wait_ge(lam_loaded.handle, 64)
            lin = lam_in[0:DH, :, :].rearrange("p l (b t) -> p l b t", t=2)
            V.tensor_tensor(lam_pr[0:DH, :, :], lin[:, :, :, 0], lin[:, :, :, 1], ALU.mult).then_inc(setup.handle, setup.made("lam_pr"))
            dve.wait_ge(turned.handle, turned.after("vec1"))
            V.tensor_copy(vecs[:, :], ps[:, 5, 64:130]).then_inc(setup.handle, setup.made("vecs0"))
            dve.wait_ge(turned.handle, turned.after("lam"))
            V.memset(ones[:, :], 1.0 / D).then_inc(setup.handle, setup.made("vecs"))
            dve.wait_ge(silu_t.handle, 1)
            cv = vecs[:, COND:COND + 16].rearrange("p (s k) -> p k s", s=2)
            V.scalar_tensor_tensor(out=cond_t[:, :, :], in0=cond_t[:, :, :], scalar=1.0, in1=cv, op0=ALU.add, op1=ALU.mult
                                   ).then_inc(setup.handle, setup.made("silu"))
            dve.wait_ge(setup.handle, setup.after("silu"))
            V.tensor_scalar(cond_t[:, :, :], cond_t[:, :, :], 0.5, None, ALU.mult).then_inc(setup.handle, setup.made("cond_f"))
            dve.wait_ge(setup.handle, setup.after("cond_f"))
            V.tensor_copy(cond_hl[:, :, 0:2], cond_t[:, :, :]).then_inc(setup.handle, setup.made("cond_hi"))
            dve.wait_ge(setup.handle, setup.after("cond_hi"))
            V.tensor_tensor(cond_hl[:, :, 2:4], cond_t[:, :, :], cond_hl[:, :, 0:2], ALU.subtract).then_inc(setup.handle, setup.made("cond"))
            dve.wait_ge(lam_exp.handle, 1)
            for l in range(DEPTH):
                lam_init = 0.8 - 0.6 * math.exp(-0.3 * l)
                V.scalar_tensor_tensor(out=neg_lam[:, l:l + 1], in0=lam_e[:, l, 1:2], scalar=-lam_init, in1=lam_e[:, l, 0:1],
                                       op0=ALU.add, op1=ALU.subtract).then_inc(setup.handle, setup.made())
                V.tensor_scalar(g_sub[:, l:l + 1], vecs[:, G_SUB + l:G_SUB + l + 1], 1.0 - lam_init, None, ALU.mult
                                ).then_inc(setup.handle, setup.made("lam"))

            def lo_first(u):
                dve.wait_ge(hi_made.handle, u + 1)
                V.tensor_tensor(w_lo[:, u % RING, :], raw[:, u % RING, :], w_hi[:, u % RING, :], ALU.subtract).then_inc(first_lo.handle, 1)

            def take_ada(A, j):
                dve.wait_ge(ada_turned.handle, A + 1)
                V.tensor_copy(ada_cols[:, j, :], ps[:, 6 + A % 2, 0:4]).then_inc(ada_out.handle, 1)

            def square_add(l, which, c, n):
                dve.wait_ge(squared.handle, squared.after(("sq", l, which, c)))
                if c == 0:
                    V.tensor_copy(square_sum[which % 2][:, 0:n], square[which % 2][:, 0, 0:n]).then_inc(square_v.handle, square_v.made((l, which, c)))
                    return
                dve.wait_ge(square_v.handle, square_v.after((l, which, c - 1)))
                V.tensor_tensor(square_sum[which % 2][:, 0:n], square_sum[which % 2][:, 0:n], square[which % 2][:, c % 2, 0:n], ALU.add
                                ).then_inc(square_v.handle, square_v.made((l, which, c)))

            for s in range(2):
                V.tensor_copy(mods[:, :, :, :, s].rearrange("p l i k -> p (l i k)"), ps[:, 5, 192:288]).then_inc(setup.handle, setup.made("b"))
            for u in range(X_TURN + 1):
                lo_first(u)
                if u >= 3:
                    take_ada(u - 3, u - 3)
            for c in range(KC):
                dve.wait_ge(turned.handle, turned.after(("x", c)))
                V.tensor_copy(x[:, c, :], psf[:, 1024 * (c % 2):1024 * (c % 2) + TOK]).then_inc(turn_v.handle, turn_v.made(("x", c)))
            for u in range(X_TURN + 1, ADA_FIRST + 3):
                if u < ADA_FIRST:
                    lo_first(u)
                take_ada(u - 3, u - 3)
                if u > X_TURN + 1 and u - X_TURN - 2 < KC:
                    square_add(0, 0, u - X_TURN - 2, TOK)
            mf = mods[:, :, :, :, :].rearrange("p l i k s -> p (l i k) s")

            def collect(name, l):
                A0, n = plan.ada0[name, l], plan.kinds[name, l].count("a")
                dve.wait_ge(ada_out.handle, A0 + n)
                got = ada_cols[:, 0:n, :]
                dst = mf[:, A0:A0 + n, :]
                if A0 == 0:
                    dve.wait_ge(setup.handle, setup.after("b"))
                V.tensor_tensor(dst, got[:, :, 0:2], dst, ALU.add).then_inc(collected.handle, collected.made())
                dve.wait_ge(collected.handle, collected.count)
                V.tensor_tensor(dst, got[:, :, 2:4], dst, ALU.add).then_inc(collected.handle, collected.made((name, l)))
                dve.wait_ge(collected.handle, collected.count)

            def take_ada_of(name, l, j):
                if "a" in plan.kinds[name, l]:
                    take_ada(plan.ada0[name, l] + j, j)

            def coefficients(l, w):
                g0 = (G_MIX if w == 0 else G_MLP) + KC * l
                for s in range(2):
                    V.scalar_tensor_tensor(out=coef[:, l, w, :, s], in0=mods[:, l, 3 * w + 1, :, s], scalar=1.0,
                                           in1=vecs[:, g0:g0 + KC], op0=ALU.add, op1=ALU.mult).then_inc(setup.handle, setup.made())
                dve.wait_ge(setup.handle, setup.count)

            def half_gate(l):
                V.tensor_scalar(mods[:, l, 2, :, :], mods[:, l, 2, :, :], 0.5, None, ALU.mult).then_inc(setup.handle, setup.made())
                dve.wait_ge(setup.handle, setup.count)

            collect("ada", 0)
            coefficients(0, 0)

            def rsqrt_v(y, mean, t, key, scale=1.0):
                V.scalar_tensor_tensor(out=t, in0=mean, scalar=EPS / scale, in1=y, op0=ALU.add, op1=ALU.mult
                                       ).then_inc(rsq_v.handle, rsq_v.made((key[0] + "1", *key[1:])))
                dve.wait_ge(rsq_v.handle, rsq_v.count)
                V.scalar_tensor_tensor(out=t, in0=t, scalar=-0.5 * scale, in1=y, op0=ALU.mult, op1=ALU.mult).then_inc(rsq_v.handle, rsq_v.made())
                dve.wait_ge(rsq_v.handle, rsq_v.count)
                V.scalar_tensor_tensor(out=y, in0=t, scalar=1.5, in1=y, op0=ALU.add, op1=ALU.mult).then_inc(rsq_v.handle, rsq_v.made())
                dve.wait_ge(rsq_v.handle, rsq_v.count)

            def norm_v(l, which, n):
                dve.wait_ge(root.handle, root.after((l, which)))
                rsqrt_v(rstd[which % 2][:, 0:n], psf[:, 3072:3072 + n], newton[which % 2][:, 0:n], ("norm", l, which))
                if which == 2:
                    for c in range(KC):
                        V.scalar_tensor_tensor(out=x[:, c, 0:n], in0=x[:, c, 0:n], scalar=vecs[:, G_FIN + c:G_FIN + c + 1],
                                               in1=rstd[which % 2][:, 0:n], op0=ALU.mult, op1=ALU.mult).then_inc(normed.handle, normed.made(("fin", c)))
                    return

                def lo(c):
                    dve.wait_ge(act_hi.handle, act_hi.after(("h", l, which, c)))
                    for s, (t0, t1) in enumerate(segs(n)):
                        V.scalar_tensor_tensor(out=h_lo[:, c, t0:t1], in0=h_f[:, c, t0:t1], scalar=mods[:, l, 3 * which, c, s:s + 1],
                                               in1=h_hi[:, c, t0:t1], op0=ALU.add, op1=ALU.subtract
                                               ).then_inc(act_lo.handle, act_lo.made(("h", l, which, c)))
                for c in range(KC):
                    for s, (t0, t1) in enumerate(segs(n)):
                        V.scalar_tensor_tensor(out=h_f[:, c, t0:t1], in0=x[:, c, t0:t1], scalar=coef[:, l, which, c, s:s + 1],
                                               in1=rstd[which % 2][:, t0:t1], op0=ALU.mult, op1=ALU.mult
                                               ).then_inc(normed.handle, normed.made((l, which, c)))
                    if c >= 1:
                        lo(c - 1)
                lo(KC - 1)

            def plain(tau, dst, n, scale=None):
                wait_tile(dve, tau)
                if scale is None:
                    V.tensor_copy(dst, tile_ps(tau, n)).then_inc(tile_v.handle, tile_v.made(("tile", tau)))
                else:
                    V.tensor_scalar(dst, tile_ps(tau, n), scale, None, ALU.mult).then_inc(tile_v.handle, tile_v.made(("tile", tau)))

            def rope(tau, dst, n, scale, s):
                wait_tile(dve, tau)
                z = tile_ps(tau, SEQ)
                V.stream_shuffle(rope_t[:, s % 2, :], z, [(i + 16) % 32 for i in range(32)]).then_inc(rope_s.handle, rope_s.made(("sh", tau)))
                V.scalar_tensor_tensor(out=dst[:, 0:SEQ], in0=z, scalar=scale, in1=cos[:, :], op0=ALU.mult, op1=ALU.mult
                                       ).then_inc(rope_s.handle, rope_s.made())
                dve.wait_ge(rope_s.handle, rope_s.after(("sh", tau)))
                V.scalar_tensor_tensor(out=rope_t[:, s % 2, :], in0=rope_t[:, s % 2, :], scalar=scale, in1=sin[:, :], op0=ALU.mult,
                                       op1=ALU.mult).then_inc(rope_s.handle, rope_s.made(("sin", tau)))
                if n > SEQ:
                    V.tensor_scalar(dst[:, SEQ:n], tile_ps(tau, n, SEQ), scale, None, ALU.mult).then_inc(rope_s.handle, rope_s.made(("c", tau)))
                    dve.wait_ge(rope_s.handle, rope_s.after(("c", tau)))
                else:
                    dve.wait_ge(rope_s.handle, rope_s.after(("sin", tau)))
                V.tensor_tensor(dst[:, 0:SEQ], dst[:, 0:SEQ], rope_t[:, s % 2, :], ALU.add).then_inc(tile_v.handle, tile_v.made(("tile", tau)))

            def values_v(l, tiles, key):
                for j, (t0, nk) in enumerate(tiles):
                    dve.wait_ge(turned.handle, turned.after((key, l, j)))
                    V.tensor_copy(v[0:nk, j, :], ps[0:nk, 4 + j % 2, :]).then_inc(turn_v.handle, turn_v.made((key, l, j)))

            for l in range(DEPTH):
                n = toks(l)
                norm_v(l, 0, TOK)
                t0 = TILE["in_a", l]
                dve.wait_ge(rope_in.handle, 32 * (l + 1))
                for j in range(12):
                    nt = n if j < WC else TOK
                    if j < 8:
                        rope(t0 + j, (q if j < 4 else k)[:, j % 4, :], nt, SCALE if j < 4 else 1.0, j)
                    else:
                        plain(t0 + j, v_f[:, j - 8, 0:nt], nt)
                    take_ada_of("in_a", l, j)
                values_v(l, V_TILES_A, "in_a")
                if l == 0:
                    collect("in_a", 0)

                items = diff_items(l)

                def max_a(i):
                    h, q0, (k0, k1) = items[i]
                    for m in range(2):
                        s = (2 * i + m) % 4
                        dve.wait_ge(scores_made.handle, scores_made.after(("a", l, i, m)))
                        V.tensor_reduce(neg_max[:, s:s + 1], psf[:, 1024 * m:1024 * m + k1 - k0], AX_X, ALU.max, negate=True
                                        ).then_inc(max_made.handle, max_made.made(("a", l, i, m)))

                def combine(i):
                    h, q0, (k0, k1) = items[i]
                    w, s = k1 - k0, (2 * i) % 4
                    dve.wait_ge(exp_made.handle, exp_made.after(("a", l, i, 1)))
                    V.reciprocal(rtotal[:, s:s + 2], total[:, s:s + 2]).then_inc(rsum.handle, rsum.made(("a", l, i)))
                    dve.wait_ge(rsum.handle, rsum.after(("a", l, i)))
                    V.tensor_scalar(rtotal[:, s + 1:s + 2], rtotal[:, s + 1:s + 2], neg_lam[:, l:l + 1], None, ALU.mult
                                    ).then_inc(rsum.handle, rsum.made())
                    V.tensor_scalar(probs_a[:, i % 2, 0, 0:w], probs_a[:, i % 2, 0, 0:w], rtotal[:, s:s + 1], None, ALU.mult
                                    ).then_inc(rsum.handle, rsum.made(("a0", l, i)))
                    dve.wait_ge(rsum.handle, rsum.after(("a0", l, i)))
                    V.scalar_tensor_tensor(out=probs_a[:, i % 2, 0, 0:w], in0=probs_a[:, i % 2, 1, 0:w], scalar=rtotal[:, s + 1:s + 2],
                                           in1=probs_a[:, i % 2, 0, 0:w], op0=ALU.mult, op1=ALU.add
                                           ).then_inc(probs_made.handle, probs_made.made(("a", l, i)))

                def turn_out_v(i):
                    h, q0, (k0, k1) = items[i]
                    if k0 == 0:
                        dve.wait_ge(turned.handle, turned.after(("a", l, i)))
                        if i >= 4:
                            dve.wait_ge(pv_made.handle, pv_made.after(("pv", l, i // 2 - 2)))
                        e = P * (i % 2)
                        V.tensor_copy(probsT_a[:, i // 2 % 2, 4:6, e:e + P], ps[:, 5, 0:2 * P].rearrange("p (b q) -> p b q", b=2)
                                      ).then_inc(turn_v.handle, turn_v.made(("a", l, i)))

                for i in range(len(items) + 1):
                    if i < len(items):
                        max_a(i)
                    if i:
                        turn_out_v(i - 1)
                    if i < len(items):
                        combine(i)

                def lo_oa(h):
                    dve.wait_ge(act_hi.handle, act_hi.after(("oa", l, h)))
                    V.tensor_tensor(o_lo[:, h, 0:n], o_f[:, h, 0:n], o_hi[:, h, 0:n], ALU.subtract
                                    ).then_inc(act_lo.handle, act_lo.made(("o", l, h)))

                for h in range(HEADS):
                    b = 2048 + 1024 * (h % 2)
                    dve.wait_ge(root.handle, root.after(("ln", l, h)))
                    V.tensor_scalar(o_mean[h // 2][:, h % 2, 0:n], psf[:, b:b + n], EPS * P / D, None, ALU.add).then_inc(rsq_v.handle, rsq_v.made(("o1", l, h)))
                for h in range(HEADS):
                    y, t = rms_o[:, h, 0:n], o_mean[h // 2][:, h % 2, 0:n]
                    dve.wait_ge(root.handle, root.after(("o", l, h)))
                    dve.wait_ge(rsq_v.handle, rsq_v.count)
                    V.tensor_tensor(t, t, y, ALU.mult).then_inc(rsq_v.handle, rsq_v.made())
                    dve.wait_ge(rsq_v.handle, rsq_v.count)
                    V.scalar_tensor_tensor(out=t, in0=t, scalar=-0.5 * D / P, in1=y, op0=ALU.mult, op1=ALU.mult).then_inc(rsq_v.handle, rsq_v.made())
                    dve.wait_ge(rsq_v.handle, rsq_v.count)
                    V.scalar_tensor_tensor(out=y, in0=t, scalar=1.5, in1=y, op0=ALU.add, op1=ALU.mult).then_inc(rsq_v.handle, rsq_v.made())
                    dve.wait_ge(rsq_v.handle, rsq_v.count)
                    V.scalar_tensor_tensor(out=o_f[:, h, 0:n], in0=o_f[:, h, 0:n], scalar=g_sub[:, l:l + 1], in1=y, op0=ALU.mult,
                                           op1=ALU.mult).then_inc(rsq_v.handle, rsq_v.made(("o", l, h)))
                    if h:
                        lo_oa(h - 1)
                lo_oa(HEADS - 1)

                def mix(name, b):
                    t0 = TILE[name, l]

                    def lo(c):
                        dve.wait_ge(act_hi.handle, act_hi.after(("m", l, c)))
                        V.tensor_tensor(m_lo[:, c, 0:n], m_f[:, c, 0:n], m_hi[:, c, 0:n], ALU.subtract
                                        ).then_inc(act_lo.handle, act_lo.made(("m", l, c)))
                    for c in range(KC):
                        half, j = divmod(c, 4)
                        tau = t0 + 8 * half + 4 + j
                        wait_tile(dve, tau)
                        dve.wait_ge(tile_a.handle, tile_a.after(("tile", t0 + 8 * half + j)))
                        first = name == "branch0"
                        dst = m_f[:, c, 0:n] if first else gate[:, j, 0:n]
                        V.scalar_tensor_tensor(out=dst, in0=gate[:, j, 0:n], scalar=1.0, in1=tile_ps(tau, n), op0=ALU.add,
                                               op1=ALU.mult).then_inc(tile_v.handle, tile_v.made(("tile", tau)))
                        if not first:
                            dve.wait_ge(tile_v.handle, tile_v.after(("tile", tau)))
                            V.tensor_tensor(m_f[:, c, 0:n], m_f[:, c, 0:n], gate[:, j, 0:n], ALU.add
                                            ).then_inc(mixed.handle, mixed.made(("m", l, b, c)))
                        if b == 1 and c:
                            lo(c - 1)
                    if b == 1:
                        lo(KC - 1)

                mix("branch0", 0)

                t0 = TILE["in_n", l]
                dve.wait_ge(tile_v.handle, tile_v.after(("tile", TILE["branch0", l] + 15)))
                V.memset(bias_raw[:, :, :, :], 0.0).then_inc(biased.handle, biased.made(("clear", l)))
                for j in range(12):
                    nt = n if j < WC else TOK
                    dst = (q, k, v_f)[j // 4]
                    plain(t0 + j, dst[:, j % 4, 0:nt], nt, SCALE if j < 4 else None)
                    take_ada_of("in_n", l, j)
                values_v(l, V_TILES_N, "in_n")
                if l == 0:
                    collect("in_n", 0)

                nitems = nat_items(l)
                subs = [(i, hh) for i in range(len(nitems)) for hh in range(2)]
                dve.wait_ge(bias_in.handle, 16 * 16 * (l + 1))

                def bias_of(c, kinds):
                    for t in kinds:
                        c0 = (8, 0, 0)[t]
                        for hh in range(2):
                            w = MASKW[t] // 8
                            o = MASKO[t]
                            V.tensor_tensor(bias[:, hh, o:o + MASKW[t]].rearrange("p (c r) -> p c r", r=8),
                                            bias_raw[:, ::-1, 2 * c + hh, c0:c0 + w].rearrange("p r c -> p c r"),
                                            mask[:, o:o + MASKW[t]].rearrange("p (c r) -> p c r", r=8), ALU.add
                                            ).then_inc(biased.handle, biased.made(("bm", l, c, t)))

                def max_n(s):
                    i, hh = subs[s]
                    c, q0, kind, k0, k1, tiles = nitems[i]
                    loc = k1 - k0
                    dve.wait_ge(scores_made.handle, scores_made.after(("n", l, s)))
                    if loc:
                        if hh == 0 and q0 != 2 * P:
                            dve.wait_ge(biased.handle, biased.after(("bm", l, c, kind)))
                        V.tensor_tensor(ps[:, s % 3, 0:loc], ps[:, s % 3, 0:loc], bias[:, hh, MASKO[kind]:MASKO[kind] + loc], ALU.add
                                        ).then_inc(biased.handle, biased.made(("s", l, s)))
                        dve.wait_ge(biased.handle, biased.after(("s", l, s)))
                    V.tensor_reduce(neg_max[:, s % 4:s % 4 + 1], ps[:, s % 3, 0:loc + CTX], AX_X, ALU.max, negate=True
                                    ).then_inc(max_made.handle, max_made.made(("n", l, s)))

                def divide_n(s):
                    i, hh = subs[s]
                    c, q0, kind, k0, k1, tiles = nitems[i]
                    w = k1 - k0 + CTX
                    dve.wait_ge(exp_made.handle, exp_made.after(("n", l, s)))
                    V.reciprocal(rtotal[:, s % 4:s % 4 + 1], total[:, s % 4:s % 4 + 1]).then_inc(rsum.handle, rsum.made(("n", l, s)))
                    dve.wait_ge(rsum.handle, rsum.after(("n", l, s)))
                    V.tensor_scalar(probs_n[:, s % 3, 0:w], probs_n[:, s % 3, 0:w], rtotal[:, s % 4:s % 4 + 1], None, ALU.mult
                                    ).then_inc(probs_made.handle, probs_made.made(("n", l, s)))

                def o_lo_n(i):
                    c, q0 = nitems[i][:2]
                    dve.wait_ge(act_hi.handle, act_hi.after(("on", l, i)))
                    V.tensor_tensor(o_lo[:, c, q0:q0 + P], ps[:, o_bank(i), 0:P], o_hi[:, c, q0:q0 + P], ALU.subtract
                                    ).then_inc(act_lo.handle, act_lo.made(("on", l, i)))

                ns = len(subs)
                bias_of(0, (0, 1, 2))
                for s in range(ns + 5):
                    if s < ns:
                        c, at_ = divmod(s, ns // WC)
                        if at_ in (2, 6) and c + 1 < WC:
                            bias_of(c + 1, (at_ // 4,))
                        if at_ == 0 and c:
                            bias_of(c, (2,))
                        max_n(s)
                    if 1 <= s <= ns:
                        divide_n(s - 1)
                    if s >= 5 and s % 2 == 1 and (s - 5) // 2 < len(nitems):
                        o_lo_n((s - 5) // 2)
                mix("branch2", 2)

                t0 = TILE["in_p", l]
                wait_tile(dve, t0 - 1)
                for g in range(WC):
                    for z0 in (0, UPAD + SEQ, UPAD + SEQ + UPAD, UW - UPAD):
                        V.memset(u_pad[:, g, z0:z0 + UPAD], 0.0).then_inc(pooled_s.handle, pooled_s.made(("zero", l)))
                offs = [(0, UPAD, SEQ), (SEQ, SEQ + 3 * UPAD, CTX)][:len(segs(n))]
                for g in range(WC):
                    tau = t0 + g
                    wait_tile(dve, tau)
                    if n > SEQ:
                        V.tensor_copy(u_pad[:, g, SEQ + 3 * UPAD:SEQ + 3 * UPAD + CTX], tile_ps(tau, TOK, SEQ)
                                      ).then_inc(pooled_s.handle, pooled_s.made())
                    V.tensor_copy(u_pad[:, g, UPAD:UPAD + SEQ].rearrange("p (r c) -> p c r", r=ROWS),
                                  tile_ps(tau, SEQ).rearrange("p (c r) -> p c r", r=ROWS)
                                  ).then_inc(tile_v.handle, tile_v.made(("tile", tau)))
                    take_ada_of("in_p", l, g)
                    dve.wait_ge(tile_v.handle, tile_v.after(("tile", tau)))
                    if n > SEQ or g == 0:
                        dve.wait_ge(pooled_s.handle, pooled_s.after(("zero", l)) + (g + 1 if n > SEQ and False else 0))
                    w = 2 << g
                    src = u_pad[:, g, :]
                    for e in range(g + 1):
                        reach = 1 << (g - e) >> 0
                        d_ = (1, 1, 2, 4)[e]
                        lo_ = 1 if e == 0 else None
                        dst = win[:, e % 2, :]
                        if n > SEQ or e:
                            dve.wait_ge(pooled_s.handle, pooled_s.after(("u", l, g, e - 1)))
                        for t_, b_, len_ in offs:
                            m_ = (7, 6, 4, 0)[e]
                            a0, a1 = b_ - m_, b_ + len_ + m_
                            if e == 0:
                                i0, i1 = src[:, a0 - 1:a1 - 1], src[:, a0:a1]
                            else:
                                i0, i1 = src[:, a0 - d_:a1 - d_], src[:, a0 + d_:a1 + d_]
                            V.tensor_tensor(dst[:, a0:a1], i0, i1, ALU.add).then_inc(pooled_s.handle, pooled_s.made(("u", l, g, e)))
                        src = dst
                        if e == 0:
                            pass
                    dve.wait_ge(pooled_s.handle, pooled_s.after(("u", l, g, g)))
                    for t_, b_, len_ in offs:
                        V.tensor_tensor(src[:, b_:b_ + w // 2], src[:, b_:b_ + w // 2], edge[:, g, 0, 0:w // 2], ALU.mult
                                        ).then_inc(pooled_s.handle, pooled_s.made())
                        if w > 2:
                            e0, e1 = b_ + len_ - w // 2 + 1, b_ + len_
                            V.tensor_tensor(src[:, e0:e1], src[:, e0:e1], edge[:, g, 1, 0:w // 2 - 1], ALU.mult
                                            ).then_inc(pooled_s.handle, pooled_s.made())
                    pooled_s.seen["e", l, g] = pooled_s.count
                    dve.wait_ge(pooled_s.handle, pooled_s.after(("e", l, g)))
                    if n > SEQ:
                        o = SEQ + 3 * UPAD
                        V.scalar_tensor_tensor(out=pooled[:, g, SEQ:TOK], in0=src[:, o:o + CTX], scalar=1.0 / w, in1=u_pad[:, g, o:o + CTX],
                                               op0=ALU.mult, op1=ALU.subtract).then_inc(pooled_s.handle, pooled_s.made())
                    V.scalar_tensor_tensor(out=pooled[:, g, 0:SEQ].rearrange("p (c r) -> p c r", r=ROWS),
                                           in0=src[:, UPAD:UPAD + SEQ].rearrange("p (r c) -> p c r", r=ROWS), scalar=1.0 / w,
                                           in1=u_pad[:, g, UPAD:UPAD + SEQ].rearrange("p (r c) -> p c r", r=ROWS),
                                           op0=ALU.mult, op1=ALU.subtract).then_inc(pooled_s.handle, pooled_s.made((l, g, "p")))
                    dve.wait_ge(pooled_s.handle, pooled_s.after((l, g, "p")))
                if l == 0:
                    collect("in_p", 0)
                    half_gate(0)
                    coefficients(0, 1)
                for g in range(WC):
                    b = 2048 + 1024 * (g % 2)
                    dve.wait_ge(act_hi.handle, act_hi.after(("ob", l, g)))
                    V.scalar_tensor_tensor(out=o_lo[:, g, 0:n], in0=psf[:, b:b + n], scalar=vecs[:, P_SC + WC * l + g:P_SC + WC * l + g + 1],
                                           in1=ob_hi[:, g, 0:n], op0=ALU.mult, op1=ALU.subtract
                                           ).then_inc(act_lo.handle, act_lo.made(("ob", l, g)))
                mix("branch1", 1)

                def residual(name, six, norm=None):
                    t0 = TILE[name, l]
                    for c in range(KC):
                        if norm and c:
                            square_add(*norm[:2], c - 1, norm[2])
                        wait_tile(dve, t0 + c)
                        for s, (a0, a1) in enumerate(segs(n)):
                            V.scalar_tensor_tensor(out=x[:, c, a0:a1], in0=tile_ps(t0 + c, a1, a0), scalar=mods[:, l, six, c, s:s + 1],
                                                   in1=x[:, c, a0:a1], op0=ALU.mult, op1=ALU.add
                                                   ).then_inc(tile_v.handle, tile_v.made(("tile", t0 + c)))
                        take_ada_of(name, l, c)

                residual("out", 2, (l, 1, n))
                square_add(l, 1, KC - 1, n)
                norm_v(l, 1, n)
                for g in range(4):
                    hh_, hl_, hf_ = hid[g % 2]
                    for c in range(KC):
                        dve.wait_ge(tile_a.handle, tile_a.after(("tile", TILE[f"up{g}", l] + c)))
                        V.tensor_tensor(hf_[:, c, 0:n], hf_[:, c, 0:n], hf_[:, c, 0:n], ALU.mult).then_inc(hid_s.handle, hid_s.made(("sq", l, g, c)))
                        dve.wait_ge(hid_s.handle, hid_s.after(("sq", l, g, c)))
                        V.tensor_copy(hh_[:, c, 0:n], hf_[:, c, 0:n]).then_inc(hid_s.handle, hid_s.made(("hi", l, g, c)))
                        dve.wait_ge(hid_s.handle, hid_s.after(("hi", l, g, c)))
                        V.tensor_tensor(hl_[:, c, 0:n], hf_[:, c, 0:n], hh_[:, c, 0:n], ALU.subtract
                                        ).then_inc(act_lo.handle, act_lo.made(("hid", l, g, c)))
                        take_ada_of(f"up{g}", l, c)
                    if l == 0:
                        collect(f"up{g}", 0)
                    norm = None if g < 3 else (l + 1, 0, TOK) if l + 1 < DEPTH else (DEPTH, 2, SEQ)
                    residual(f"down{g}", 5, norm)
                    if norm:
                        square_add(*norm[:2], KC - 1, norm[2])
                    dve.wait_ge(tile_v.handle, tile_v.after(("tile", TILE[f"down{g}", l] + 7)))
                    if l == 0 and g < 2:
                        collect(f"down{g}", 0)
                    if l == 0 and g == 2:
                        half_gate(1)
                        coefficients(1, 0)
                        coefficients(1, 1)
            norm_v(DEPTH, 2, SEQ)
            for i in range(4):
                for e in range(2):
                    dve.wait_ge(turned.handle, turned.after(("y", i, e)))
                    V.tensor_copy(x_rows[:, i, 512 * e:512 * e + 512], ps[:, 4 + e, :]).then_inc(turn_v.handle, turn_v.made(("y", i, e)))

        return count.counted()


_FLAT = ("b_ada", "g_mix", "g_mlp", "g_final", "pool_scale", "g_subln", "c", "c_ctx")
_INS = ("x", "c", "ctx", "c_ctx", "w_ada", "b_ada", "g_mix", "g_mlp", "w_in", "lambda_q1", "lambda_k1", "lambda_q2", "lambda_k2",
        "g_subln", "pool_w", "pool_scale", "nat_rpb", "w_branch", "w_out", "w_mlp1", "w_mlp2", "g_final")


def shape_constants():
    import numpy as np

    t = np.arange(SEQ)
    row, col = t % ROWS, t // ROWS
    nf = 16
    inv = np.float32(10000.0) ** (-np.arange(nf, dtype=np.float32) / np.float32(nf))
    p = np.arange(P)
    pos = np.where(((p // 32) % 2 == 0)[:, None], row[None, :], col[None, :]).astype(np.float32)
    ang = pos * inv[p % 16][:, None]
    sign = np.where((p % 32) < 16, -1.0, 1.0).astype(np.float32)[:, None]
    mask = np.full((P, 640), -1e30, np.float32)
    for kind, g, o, c0 in ((0, 0, MASKO[0], 0), (1, 1, MASKO[1], 8), (2, 3, MASKO[2], 40)):
        for part in range(P):
            cq = 16 * g + part // 8
            w0 = min(max(cq - 8, 0), COLS - 16)
            for j in range(MASKW[kind]):
                if w0 <= c0 + j // 8 < w0 + 16:
                    mask[part, o + j] = 0.0
    edge = np.ones((4, 2, 8), np.float32)
    for g in range(4):
        w = 2 << g
        for i in range(w // 2):
            edge[g, 0, i] = w / (i + w // 2)
            if i < w // 2 - 1:
                edge[g, 1, i] = w / (w // 2 - 1 - i + w // 2)
    return {"c_ident": np.eye(P, dtype=np.float32), "c_mask": mask, "c_cos": np.cos(ang).astype(np.float32),
            "c_sin": (np.sin(ang) * sign).astype(np.float32), "c_edge": np.ascontiguousarray(np.broadcast_to(edge, (P, 4, 2, 8)))}


def kernel(**inputs):
    import numpy as np
    import concourse.bacc as bacc
    from concourse.bass_utils import run_bass_kernel_spmd

    arrays = dict(shape_constants())
    for name in _INS:
        v = np.ascontiguousarray(inputs[name])
        if name == "nat_rpb":
            v = np.ascontiguousarray(v[:, :, ::-1].transpose(0, 2, 1, 3))
        arrays[name] = v.reshape(-1) if name in _FLAT else v.reshape(v.shape[-2:]) if name in ("x", "ctx") else v

    def build(known):
        nc = bacc.Bacc("TRN2", target_bir_lowering=False, num_devices=1, dynamic_dma_scratch_size=64)
        a = {n: nc.dram_tensor(f"in_{n}", v.shape, mybir.dt.from_np(v.dtype), kind="ExternalInput").ap() for n, v in arrays.items()}
        out = nc.dram_tensor("out_0", (SEQ, D), F32, kind="ExternalOutput").ap()
        return nc, hybrid_block(nc, a, out, known)

    _, counted = build({})
    nc, again = build(counted)
    assert again == counted
    r = run_bass_kernel_spmd(nc, [{f"in_{n}": v for n, v in arrays.items()}], core_ids=[0])
    return r.results[0]["out_0"].reshape(1, SEQ, D)
```

```python
import math
from contextlib import ExitStack

import concourse.bass as bass
from concourse import mybir

ALU = mybir.AluOpType
ACT = mybir.ActivationFunctionType
F32 = mybir.dt.float32
F32R = mybir.dt.float32r
AX_X = mybir.AxisListType.X

P = 128
DEPTH = 2
D = 1024
KC = D // P
SEQ, CTX = 512, 256
TOK = SEQ + CTX
ROWS, COLS = 8, 64
DH, DW = 64, 512
WC = DW // P
HEADS = 4
IN_A, IN_P, IN_N, IN_G = 0, 3 * DW, 4 * DW, 7 * DW
EPS = 1e-6
SCALE = DH ** -0.5
RING = 4
UNIT = 1024
ADA_UNITS = 6 * D // P
ADA_FIRST = 20
X_TURN = 8
MASKW = (192, 256, 192)
MASKO = (0, 192, 448)
UPAD = 8
UW = SEQ + 2 * UPAD + CTX + 2 * UPAD


class Signal:

    def __init__(self, handle, known):
        self.handle, self.known, self.count, self.seen = handle, known, 0, {}

    def made(self, key=None, by=1):
        self.count += by
        self.seen[key] = self.count
        return by

    def after(self, key):
        return self.known.get(key, 1)


class Counter:

    def __init__(self, nc, ctx, known):
        self.nc, self.ctx, self.known, self.signals = nc, ctx, known, {}

    def __call__(self, name):
        s = Signal(self.ctx.enter_context(self.nc.semaphore(name)), self.known.get(name, {}))
        self.signals[name] = s
        return s

    def counted(self):
        return {n: dict(s.seen) for n, s in self.signals.items()}


class Plan:

    def __init__(self):
        self.phases = [("ada", 0, "a" * ADA_FIRST)]
        for l in range(DEPTH):
            two = "aagg" if l == 0 else "gg"
            self.phases += [("in_a", l, two * 6), ("branch0", l, "ggggbb" * 2), ("in_n", l, two * 6),
                            ("branch2", l, "ggggbb" * 2), ("in_p", l, two * 2), ("branch1", l, "ggggbb" * 2), ("out", l, "g" * 8)]
            for g in range(4):
                self.phases += [(f"up{g}", l, two * 4), (f"down{g}", l, (two if g < 2 else "gg") * 4)]
        self.first, self.tile0, self.ada0, self.event0, self.kinds = {}, {}, {}, {}, {}
        self.tile_event, self.tile_unit, self.unit_event = [], [], []
        ada = event = 0
        for name, l, kinds in self.phases:
            at = name, l
            self.first[at], self.tile0[at], self.ada0[at], self.event0[at] = len(self.unit_event), len(self.tile_event), ada, event
            self.kinds[at] = kinds
            for kind in kinds:
                for _ in range(2 if kind == "b" else 1):
                    event += 1
                    if kind != "a":
                        self.tile_event.append(event)
                        self.tile_unit.append(len(self.unit_event))
                ada += kind == "a"
                self.unit_event.append(event)
        self.units = len(self.unit_event)
        assert ada == DEPTH * ADA_UNITS and not self.units % RING


def hybrid_block(nc, a, out, known):
    plan = Plan()
    FIRST, TILE, UNITS = plan.first, plan.tile0, plan.units
    with ExitStack() as ctx:
        base = (nc.sbuf_base + 31) // 32 * 32
        X0 = base
        H0 = X0 + KC * TOK * 4
        RAW0 = H0 + 2 * KC * TOK * 4
        WH0 = RAW0 + RING * UNIT * 4
        WL0 = WH0 + RING * UNIT * 4
        QK0 = WL0 + RING * UNIT * 4
        M0 = QK0 + 2 * WC * TOK * 4
        V0 = M0 + KC * TOK * 4
        OL0 = V0 + 7 * DW * 4
        WK0 = OL0 + WC * TOK * 4
        C0 = WK0 + 24576

        def at(name, shape, dt, off):
            return nc.alloc_sbuf_tensor_at(name, [P] + shape, dt, offset=off)

        x = at("x", [KC, TOK], F32, X0)
        h_hi = at("h_hi", [KC, TOK], F32R, H0)
        h_lo = at("h_lo", [KC, TOK], F32R, H0 + KC * TOK * 4)
        h_f = at("h_f", [KC, TOK], F32, H0 + KC * TOK * 4)
        raw = at("raw", [RING, UNIT], F32, RAW0)
        w_hi = at("w_hi", [RING, UNIT], F32R, WH0)
        w_lo = at("w_lo", [RING, UNIT], F32R, WL0)
        q = at("q", [WC, TOK], F32, QK0)
        k = at("k", [WC, TOK], F32, QK0 + WC * TOK * 4)
        k_lo = at("k_lo", [WC, TOK], F32R, QK0 + WC * TOK * 4)
        x_rows = at("x_rows", [6, D], F32, QK0)
        u_pad = at("u_pad", [WC, UW], F32, QK0)
        win = at("win", [2, UW], F32, QK0 + WC * UW * 4)
        o_hi = at("o_hi", [WC, TOK], F32R, QK0)
        m_hi = at("m_hi", [KC, TOK], F32R, QK0)
        m_f = at("m_f", [KC, TOK], F32, M0)
        m_lo = at("m_lo", [KC, TOK], F32R, M0)
        cos = at("cos", [SEQ], F32, M0)
        sin = at("sin", [SEQ], F32, M0 + 4 * SEQ)
        rope_t = at("rope_t", [2, SEQ], F32, M0 + 8 * SEQ)
        q_two = [at(f"q_two{i}", [2, TOK], F32R, M0 + 16 * TOK * (1 - i)) for i in range(2)]
        k_two = [at(f"k_two{i}", [2, TOK], F32R, M0 + 16 * TOK * (1 - i) + 8 * TOK) for i in range(2)]
        rms_o = at("rms_o", [HEADS, TOK], F32, WK0 + 16 * TOK)
        o_mean = [at("o_mean0", [2, TOK], F32, V0), at("o_mean1", [2, TOK], F32, V0 + 8 * TOK)]
        v = at("v", [7, DW], F32, V0)
        v_f = at("v_f", [WC, TOK], F32, OL0)
        o_f = at("o_f", [WC, TOK], F32, OL0)
        o_lo = at("o_lo", [WC, TOK], F32R, OL0)
        pooled = at("pooled", [WC, TOK], F32, OL0)
        probs_0 = at("probs_0", [3, TOK], F32, WK0)
        probs_1 = at("probs_1", [2, TOK], F32, WK0 + 12 * TOK)
        probsT_a = at("probsT_a", [3, 6, P], F32, WK0 + 20 * TOK)
        probs_n = [at("probs_n0", [2, 512], F32, WK0), at("probs_n1", [2, 512], F32, WH0 + 3 * UNIT * 4)]
        assert all((FIRST["branch2", l] + 3) % RING == 3 for l in range(DEPTH))
        probsT_n = at("probsT_n", [2, 4, P], F32, WK0 + 6144)
        bias_raw = at("bias_raw", [8, 8, 32], F32, WK0 + 10240)
        bias = at("bias", [2, 640], F32, WK0 + 18432)
        gate = at("gate", [4, TOK], F32, WK0)
        ob_hi = at("ob_hi", [WC, TOK], F32R, WK0 + 4 * TOK * 4)
        pool_w = at("pool_w", [WC, P], F32, V0)
        square, square_sum, rstd, newton = ([at(f"{name}{i}", shape, F32, o + 4 * TOK * j) for i, o in enumerate((M0 + 16 * SEQ, WK0))]
                                            for name, shape, j in (("square", [2, TOK], 0), ("square_sum", [TOK], 2),
                                                                   ("rstd", [TOK], 3), ("newton", [TOK], 4)))
        ada_rows = at("ada_rows", [2, P], F32, C0 - 8 * P)
        vec_rows = at("vec_rows", [2, P], F32, WK0 + 20 * TOK)
        hid = [(at(f"hid_hi{i}", [KC, TOK], F32R, o), at(f"hid_lo{i}", [KC, TOK], F32R, o + KC * TOK * 4),
                at(f"hid_f{i}", [KC, TOK], F32, o + KC * TOK * 4)) for i, o in enumerate((QK0, V0))]
        off = [C0]

        def const(name, shape, dt=F32):
            n = 1
            for s in shape:
                n *= s
            t = at(name, shape, dt, off[0])
            off[0] += (n * 4 + 31) // 32 * 32
            return t

        ident = const("ident", [P])
        ones = const("ones", [P])
        mask = const("mask", [640])
        mods = const("mods", [DEPTH, 6, KC, 2])
        coef = const("coef", [DEPTH, 2, KC, 2])
        vecs = const("vecs", [66])
        edge = const("edge", [4, 2, 8])
        cond_hl = const("cond_hl", [KC, 4], F32R)
        cond_t = const("cond_t", [KC, 2])
        ada_cols = const("ada_cols", [ADA_FIRST, 4])
        eps = const("eps", [1])
        lam_in = const("lam_in", [DEPTH, 4])
        lam_pr = const("lam_pr", [DEPTH, 2])
        lam_e = const("lam_e", [DEPTH, 2])
        neg_lam = const("neg_lam", [DEPTH])
        g_sub = const("g_sub", [DEPTH])
        softmax_stats = const("softmax_stats", [3, 4])
        neg_max, total, rtotal = (softmax_stats[:, i, :] for i in range(3))
        assert off[0] <= nc.sbuf_usable_end, (off[0], nc.sbuf_usable_end)
        G_MIX, G_MLP, G_FIN, P_SC, G_SUB, COND = 0, 16, 32, 40, 48, 50

        ps = ctx.enter_context(nc.psum_tensor("ps", [P, 8, 512], F32))
        psf = ps[:, :, :].rearrange("p b n -> p (b n)")

        count = Counter(nc, ctx, known)
        ident_in = count("ident_in")
        consts_in = count("consts_in")
        x_in = count("x_in")
        vecs_in = count("vecs_in")
        lam_loaded = count("lam_loaded")
        setup = count("setup")
        ada_taken = count("ada_taken")
        ada_turned = count("ada_turned")
        ada_out = count("ada_out")
        collected = count("collected")
        first_lo = count("first_lo")
        silu_tanh = count("silu_tanh")
        lam_exp = count("lam_exp")
        rope_in = count("rope_in")
        bias_in = count("bias_in")
        pw_in = count("pw_in")
        unit_in = [count(f"unit_in{i}") for i in range(RING)]
        hi_made = count("hi_made")
        lo_made = count("lo_made")
        tile_made = count("tile_made")
        turned = count("turned")
        stat_made = count("stat_made")
        scores_made = count("scores_made")
        pv_made = count("pv_made")
        pool_made = count("pool_made")
        tile_v = count("tile_v")
        tile_a = count("tile_a")
        turn_v = count("turn_v")
        turn_a = count("turn_a")
        rope_s = count("rope_s")
        split_qk = count("split_qk")
        two_made = count("two_made")
        split_v = count("split_v")
        squared = count("squared")
        root = count("root")
        normed = count("normed")
        act_hi = count("act_hi")
        act_lo = count("act_lo")
        biased = count("biased")
        max_made = count("max_made")
        exp_made = count("exp_made")
        rsum = count("rsum")
        probs_made = count("probs_made")
        o_out = count("o_out")
        o_sq = count("o_sq")
        square_v = count("square_v")
        rsq_v = count("rsq_v")
        mixed = count("mixed")
        pooled_s = count("pooled_s")
        hid_s = count("hid_s")
        stored = count("stored")
        block = ctx.enter_context(nc.Block())

        def toks(l):
            return TOK if l + 1 < DEPTH else SEQ

        def segs(n):
            return [(0, SEQ)] + ([(SEQ, TOK)] if n > SEQ else [])

        def tile_ps(tau, n=TOK, lo=0):
            b = 1024 * (tau % 2)
            return psf[:, b + lo:b + n]

        taker = {}
        for name, l, kinds in plan.phases:
            n_tiles = len(kinds.replace("a", "").replace("b", "bb"))
            for j in range(n_tiles):
                by_act = name.startswith("up") or (name.startswith("branch") and j % 8 < 4)
                taker[TILE[name, l] + j] = tile_a if by_act else tile_v

        def wait_tile(eng, tau):
            eng.wait_ge(tile_made.handle, plan.tile_event[tau])

        def wait_lo(eng, u, i=None):
            sem, v0 = (first_lo, u + 1) if u < ADA_FIRST else (lo_made, u + 1 - ADA_FIRST)
            eng.wait_ge(sem.handle, v0 if i is None else i * RING + v0)

        def wait_taken(eng, tau):
            if tau >= 2:
                eng.wait_ge(taker[tau - 2].handle, taker[tau - 2].after(("tile", tau - 2)))

        def diff_items(l):
            items = []
            for h in range(HEADS):
                items += [(h, P * b, (0, TOK)) for b in range(SEQ // P)]
                if toks(l) > SEQ:
                    items += [(h, SEQ + P * b, (SEQ, TOK)) for b in range(CTX // P)]
            return items

        def map_rows(m):
            return slice(DH * m, DH * m + DH), slice(DH * (1 - m), DH * (1 - m) + DH)

        def nat_items(l):
            items = []
            for c in range(WC):
                for g in range(4):
                    kind = 0 if g == 0 else 2 if g == 3 else 1
                    k0, k1 = max(0, P * g - 64), min(SEQ, P * g + 192)
                    tiles = {0: [(0, 0, 64), (1, 64, 128)], 2: [(4, 128, 64), (3, 0, 128)],
                             1: [(g, 0, 128), (g + 1, 128, 128)]}[kind]
                    loc = k1 - k0
                    items.append((c, P * g, kind, k0, k1, tiles + [(5, loc, 128), (6, loc + 128, 128)]))
                if toks(l) > SEQ:
                    for b in range(2):
                        items.append((c, SEQ + P * b, None, 0, 0, [(5, 0, 128), (6, 128, 128)]))
            return items

        def o_bank(i):
            return 6 + i % 2

        V_TILES_N = [(0, 64), (64, 128), (192, 128), (320, 128), (448, 64), (512, 128), (640, 128)]
        V_TILES_A = [(P * j, P) for j in range(6)]

        @block.sync
        def _(sp):
            sp.dma_start(ident[:, :], a["c_ident"]).then_inc(ident_in.handle, 16)
            rows = [("g_mix", 16), ("g_mlp", 16), ("g_final", 8), ("pool_scale", 8), ("g_subln", 2), ("c", 8), ("c_ctx", 8)]
            r0 = 0
            for name, n in rows:
                sp.dma_start(vec_rows[r0:r0 + n, 0, :], a[name].rearrange("(n p) -> n p", p=P)).then_inc(vecs_in.handle, 16)
                r0 += n
            sp.dma_start(vec_rows[0:96, 1, :], a["b_ada"].rearrange("(n p) -> n p", p=P)).then_inc(vecs_in.handle, 16)
            for i, name in enumerate(("lambda_q1", "lambda_k1", "lambda_q2", "lambda_k2")):
                sp.dma_start(lam_in[0:DH, :, i], a[name].rearrange("l d -> d l"), allow_slow_non_contiguous=True).then_inc(lam_loaded.handle, 16)

            for u in range(RING):
                sp.dma_start(raw[:, u, :].rearrange("p (k n) -> p k n", k=KC),
                             a["w_ada"][0].rearrange("(k p) n -> p k n", p=P)[:, :, P * u:P * u + P]).then_inc(unit_in[u].handle, 16)
            def grid_rows(t, i):
                return bass.AP(t.tensor, t.offset + 16 * i * D, [[D, 16], [COLS * D, ROWS], [1, D]])

            def load_x(i):
                if i < 6:
                    src = grid_rows(a["x"], i) if i < 4 else a["ctx"][P * (i - 4):P * (i - 3), :]
                    sp.dma_start(x_rows[:, i, :], src).then_inc(x_in.handle, 16)

            load_x(0)
            sp.dma_start(mask[:, :], a["c_mask"]).then_inc(consts_in.handle, 16)
            sp.dma_start(edge[:, :, :], a["c_edge"]).then_inc(consts_in.handle, 16)
            sp.dma_start(cos[:, :], a["c_cos"]).then_inc(rope_in.handle, 16)
            sp.dma_start(sin[:, :], a["c_sin"]).then_inc(rope_in.handle, 16)

            def load(u, src, rows, i=None):
                wait_lo(sp, u - RING, i)
                dst = raw[:, u % RING, :].rearrange("p (k n) -> p k n", k=rows)
                sp.dma_start(dst, src).then_inc(unit_in[u % RING].handle, 16)

            def cols(w, j, n=P):
                return w.rearrange("(k p) n -> p k n", p=P)[:, :, bass.ts(j, n)]

            for name, l, kinds in plan.phases:
                u0, n = FIRST[name, l], len(kinds)
                w = None
                if name in ("in_a", "in_n", "in_p"):
                    c0 = {"in_a": IN_A, "in_n": IN_N, "in_p": IN_P}[name]
                    w = a["w_in"][l][:, c0:c0 + kinds.count("g") * P]
                elif name == "out":
                    w = a["w_out"][l]
                elif name.startswith("up"):
                    g = int(name[-1])
                    w = a["w_mlp1"][l][:, g * D:(g + 1) * D]
                elif name.startswith("down"):
                    g = int(name[-1])
                    w = a["w_mlp2"][l][g * D:(g + 1) * D, :]
                elif name.startswith("branch"):
                    b = int(name[-1])
                    wg = a["w_in"][l][:, IN_G + b * D:IN_G + (b + 1) * D]
                    for half in range(2):
                        for j in range(4):
                            load(u0 + 6 * half + j, cols(wg, 4 * half + j), KC)
                        for j in range(2):
                            load(u0 + 6 * half + 4 + j, cols(a["w_branch"][l, b], 2 * half + j, 256), WC)
                    continue
                if name == "in_a" and l:
                    sp.wait_ge(tile_made.handle, plan.tile_event[TILE["down2", l - 1] + 7])
                    sp.dma_start(cos[:, :], a["c_cos"]).then_inc(rope_in.handle, 16)
                    sp.dma_start(sin[:, :], a["c_sin"]).then_inc(rope_in.handle, 16)
                ada_l, ada_c = divmod(plan.ada0[name, l], ADA_UNITS)
                per = {"a": kinds[:RING].count("a"), "g": kinds[:RING].count("g")}

                def source(j, i=None):
                    kind = kinds[j]
                    c = kinds[:j].count(kind)
                    if kind == "a":
                        return cols(a["w_ada"][ada_l], ada_c + c if i is None else i * per[kind] + (ada_c + c))
                    return w.rearrange("(k p) n -> p k n", p=P)[:, :, bass.ds(P * c if i is None else i * (per[kind] * P) + P * c, P)]

                f = RING if u0 < ADA_FIRST + RING else 0
                if u0 == ADA_FIRST:
                    for j in range(f):
                        load(u0 + j, source(j), KC)
                if name == "ada":
                    for j in range(f, n):
                        load(u0 + j, source(j), KC)
                        load_x(j - f + 1)
                    continue
                with sp.Fori(0, (n - f) // RING) as i:
                    for j in range(f, f + RING):
                        load(u0 + j, source(j, i), KC, i)
                if name == "in_n":
                    sp.wait_ge(biased.handle, biased.after(("clear", l)))
                    for cl in range(16):
                        k0, k1 = max(0, cl - 7), min(32, cl + 24)
                        src = bass.AP(a["nat_rpb"].tensor, a["nat_rpb"].offset + l * 8 * 15 * 31 + k0 + 7 - cl,
                                      [[8 * 31, 8], [31, 64], [1, k1 - k0]])
                        sp.dma_start(bias_raw[8 * cl:8 * cl + 8, :, :, k0:k1].rearrange("p r h c -> p (r h) c"), src).then_inc(bias_in.handle, 16)
                if name == "in_p":
                    sp.wait_ge(tile_v.handle, tile_v.after(("tile", TILE["branch2", l] + 15)))
                    sp.dma_start(pool_w[:, :, :], a["pool_w"][l].rearrange("g c e -> c g e")).then_inc(pw_in.handle, 16)

            for i in range(4):
                sp.wait_ge(turn_v.handle, turn_v.after(("y", i)))
                sp.wait_ge(turn_a.handle, turn_a.after(("y", i)))
                sp.dma_start(grid_rows(out, i), x_rows[:, i, :]).then_inc(stored.handle, 16)
            sp.wait_ge(stored.handle, 16 * 4)

        @block.gpsimd
        def _(pool):
            def lo_units(u0, u1):
                n = (u1 - u0) // RING

                def lo(u, i=None):
                    pool.wait_ge(hi_made.handle, u + 1 if i is None else i * RING + (u + 1))
                    s = u % RING
                    nc.gpsimd.tensor_tensor(w_lo[:, s, :], raw[:, s, :], w_hi[:, s, :], ALU.subtract).then_inc(lo_made.handle, 1)
                with pool.Fori(0, n) as i:
                    for u in range(u0, u0 + RING):
                        lo(u, i)
                for u in range(u0 + n * RING, u1):
                    lo(u)

            u0 = ADA_FIRST
            for l in range(DEPTH):
                u1 = FIRST["branch0", l] + 3
                lo_units(u0, u1)
                u0 = u1
                pool.wait_ge(lo_made.handle, u1 - ADA_FIRST)
                for h in range(2, HEADS):
                    b = h % 2
                    pool.wait_ge(split_qk.handle, split_qk.after(("k", l, h)))
                    for m in range(2):
                        own, other = map_rows(m)
                        if two_made.count:
                            pool.wait_ge(two_made.handle, two_made.count)
                        nc.gpsimd.tensor_tensor(k_lo[own, h, :], k[own, h, :], k_two[b][own, m, :], ALU.subtract
                                                ).then_inc(two_made.handle, two_made.made())
                    pool.wait_ge(split_qk.handle, split_qk.after(("q", l, h)))
                    for m in range(2):
                        own, other = map_rows(m)
                        pool.wait_ge(two_made.handle, two_made.count)
                        nc.gpsimd.tensor_tensor(q_two[b][other, m, 0:toks(l)], q[own, h, 0:toks(l)], q_two[b][own, m, 0:toks(l)],
                                                ALU.subtract).then_inc(two_made.handle, two_made.made((l, h)))
                pool.wait_ge(two_made.handle, two_made.count)
            lo_units(u0, UNITS)

        @block.scalar
        def _(act):
            def split_hi(u, tiles=None):
                if isinstance(u, int):
                    if u >= UNITS:
                        return
                    act.wait_ge(unit_in[u % RING].handle, 16 * (u // RING + 1))
                    if u >= RING:
                        act.wait_ge(tile_made.handle, plan.unit_event[u - RING])
                    s = u % RING
                nc.scalar.activation(w_hi[:, s, :], raw[:, s, :], ACT.Copy).then_inc(hi_made.handle, 1)

            def split_hi_loop(i, u, t):
                s = u % RING
                act.wait_ge(unit_in[s].handle, i * 16 + 16 * (u // RING + 1))
                act.wait_ge(tile_made.handle, i * RING + t)
                nc.scalar.activation(w_hi[:, s, :], raw[:, s, :], ACT.Copy).then_inc(hi_made.handle, 1)

            def take_ada(u, A, i=None):
                act.wait_ge(tile_made.handle, plan.unit_event[u] if i is None else i * RING + plan.unit_event[u])
                if A >= 2:
                    act.wait_ge(ada_turned.handle, A - 1 if i is None else i * 2 + (A - 1))
                nc.scalar.copy(ada_rows[0:4, A % 2, :], ps[0:4, 4 + A % 2, 0:P]).then_inc(ada_taken.handle, 1)

            def stream(name, l, body, begun=False):
                kinds = plan.kinds[name, l]
                n, u0, t0, A0 = len(kinds), FIRST[name, l], plan.event0[name, l], plan.ada0[name, l]
                if body is None and u0 and u0 + n + 3 <= UNITS:
                    j0 = RING if begun else 0
                    for j in range(j0):
                        if j:
                            split_hi(u0 + j + 3)
                        if kinds[j] == "a":
                            take_ada(u0 + j, A0 + kinds[:j].count("a"))
                    with act.Fori(0, (n - j0) // RING) as i:
                        for j in range(j0, j0 + RING):
                            split_hi_loop(i, u0 + j + 3, t0 + j)
                            if kinds[j] == "a":
                                take_ada(u0 + j, A0 + kinds[:j].count("a"), i)
                    return
                for j in range(n):
                    if j or not begun:
                        split_hi(u0 + j + 3)
                    if kinds[j] == "a":
                        take_ada(u0 + j, A0 + kinds[:j].count("a"))
                        if name == "ada" and 0 <= j - X_TURN - 2 < KC:
                            squares(0, 0, TOK, [j - X_TURN - 2])
                    elif body:
                        body(kinds[:j].count("g"))

            def squares(l, which, n, chunks):
                for c in chunks:
                    if which == 0 and l == 0:
                        act.wait_ge(turn_v.handle, turn_v.after(("x", c)))
                    else:
                        act.wait_ge(tile_v.handle, tile_v.after(("tile", (TILE["out", l] if which == 1 else TILE["down3", l - 1]) + c)))
                    if c >= 2:
                        act.wait_ge(square_v.handle, square_v.after((l, which, c - 2)))
                    nc.scalar.activation(square[which % 2][:, c % 2, 0:n], x[:, c, 0:n], ACT.Square).then_inc(squared.handle, squared.made(("sq", l, which, c)))

            def rsqrt_act(mean, dst):
                nc.scalar.activation(dst, mean, ACT.Ln, bias=eps[:, 0:1]).then_inc(root.handle, root.made())
                act.wait_ge(root.handle, root.count)
                return nc.scalar.activation(dst, dst, ACT.Exp, scale=-0.5)

            def norm_act(l, which, n):
                act.wait_ge(stat_made.handle, stat_made.after(("sq", l, which)))
                rsqrt_act(psf[:, 3072:3072 + n], rstd[which % 2][:, 0:n]).then_inc(root.handle, root.made((l, which)))
                if which == 2:
                    return
                split_hi(FIRST[("in_a", "up0")[which], l] + 3)
                for c in range(KC):
                    act.wait_ge(normed.handle, normed.after((l, which, c)))
                    for s, (t0, t1) in enumerate(segs(n)):
                        nc.scalar.activation(h_hi[:, c, t0:t1], h_f[:, c, t0:t1], ACT.Identity, bias=mods[:, l, 3 * which, c, s:s + 1]
                                             ).then_inc(act_hi.handle, act_hi.made(("h", l, which, c)))

            act.wait_ge(setup.handle, setup.after("vecs"))
            nc.scalar.activation(cond_t[:, :, :], vecs[:, COND:COND + 16].rearrange("p (s k) -> p k s", s=2), ACT.Tanh,
                                 scale=0.5).then_inc(silu_tanh.handle, silu_tanh.made("tanh"))
            act.wait_ge(turned.handle, turned.after("lam"))
            nc.scalar.activation(lam_e[:, :, :], psf[:, 3072:3072 + 2 * DEPTH], ACT.Exp).then_inc(lam_exp.handle, lam_exp.made("exp"))
            for u in range(3):
                split_hi(u)
            act.wait_ge(setup.handle, setup.after("cond"))
            stream("ada", 0, None)

            def values_act(l, tiles, key):
                for j, (t0, nk) in enumerate(tiles):
                    if j % 2:
                        act.wait_ge(turned.handle, turned.after((key, l, j)))
                        nc.scalar.copy(v[0:nk, j, :], ps[0:nk, 4 + j % 4, :]).then_inc(turn_a.handle, turn_a.made((key, l, j)))

            for l in range(DEPTH):
                n = toks(l)
                norm_act(l, 0, TOK)
                stream("in_a", l, None, begun=True)
                values_act(l, V_TILES_A, "in_a")

                items = diff_items(l)

                def exp_a(i):
                    h, q0, (k0, k1) = items[i]
                    for m in range(2):
                        act.wait_ge(max_made.handle, max_made.after(("a", l, i, m)))
                        if m == 0 and i >= 3:
                            act.wait_ge(turned.handle, turned.after(("a", l, i - 3)))
                        if m == 1 and i >= 2:
                            act.wait_ge(probs_made.handle, probs_made.after(("a", l, i - 2)))
                        s = (2 * i + m) % 4
                        dst = (probs_0[:, i % 3, 0:k1 - k0], probs_1[:, i % 2, 0:k1 - k0])[m]
                        nc.scalar.activation(dst, psf[:, 1024 * m:1024 * m + k1 - k0], ACT.Exp,
                                             bias=neg_max[:, s:s + 1], accum_out=total[:, s:s + 1]
                                             ).then_inc(exp_made.handle, exp_made.made(("a", l, i, m)))

                def split_act(h, part):
                    b = h % 2
                    for m in range(2):
                        own, other = map_rows(m)
                        dst, src = ((k_two[b][own, m, :], k[own, h, :]), (k_two[b][other, m, :], k[own, h, :]),
                                    (q_two[b][own, m, 0:n], q[own, h, 0:n]))[part]
                        key = ("q" if part == 2 else "k", l, h)
                        nc.scalar.activation(dst, src, ACT.Copy).then_inc(split_qk.handle, split_qk.made(key))

                def turn_out_a(i):
                    h, q0, (k0, k1) = items[i]
                    act.wait_ge(turned.handle, turned.after(("a", l, i)))
                    if i >= 3:
                        act.wait_ge(pv_made.handle, pv_made.after(("pv", l, i - 3)))
                    nb = (k1 - k0) // P
                    nc.scalar.copy(probsT_a[:, i % 3, 0:nb, :], psf[:, 2048:2048 + nb * P]).then_inc(turn_a.handle, turn_a.made(("a", l, i)))

                def take_oa(i):
                    h, q0, _ = items[i]
                    act.wait_ge(pv_made.handle, pv_made.after(("pv", l, i)))
                    nc.scalar.copy(o_f[:, h, q0:q0 + P], ps[:, o_bank(i), 0:P]).then_inc(o_out.handle, o_out.made(("a", l, i)))

                per_head = len(items) // HEADS
                for i in range(len(items) + 4):
                    if i < len(items):
                        exp_a(i)
                        h, part = i // per_head + 1, i % per_head
                        if 2 <= h < HEADS and part < 3:
                            split_act(h, part)
                    if 2 <= i < len(items) + 2:
                        turn_out_a(i - 2)
                    if i >= 4:
                        take_oa(i - 4)
                act.wait_ge(o_out.handle, o_out.after(("a", l, len(items) - 1)))
                for h in range(HEADS):
                    if h >= 2:
                        act.wait_ge(stat_made.handle, stat_made.after(("o", l, h - 2)))
                    nc.scalar.activation(square[0][:, h % 2, 0:n], o_f[:, h, 0:n], ACT.Square).then_inc(o_sq.handle, o_sq.made((l, h)))
                for h in range(HEADS):
                    act.wait_ge(stat_made.handle, stat_made.after(("o", l, h)))
                    b = 2048 + 1024 * (h % 2)
                    nc.scalar.activation(rms_o[:, h, 0:n], psf[:, b:b + n], ACT.Ln, bias=eps[:, 0:1], scale=float(D // P)
                                         ).then_inc(root.handle, root.made(("ln", l, h)))
                for h in range(HEADS):
                    act.wait_ge(root.handle, root.after(("ln", l, h)))
                    nc.scalar.activation(rms_o[:, h, 0:n], rms_o[:, h, 0:n], ACT.Exp, scale=-0.5).then_inc(root.handle, root.made(("o", l, h)))

                def hi_oa(h):
                    act.wait_ge(rsq_v.handle, rsq_v.after(("o", l, h)))
                    nc.scalar.activation(o_hi[:, h, 0:n], o_f[:, h, 0:n], ACT.Copy).then_inc(act_hi.handle, act_hi.made(("oa", l, h)))

                def gates(name):
                    u0, t0 = FIRST[name, l], TILE[name, l]
                    for half in range(2):
                        for j in range(4):
                            split_hi(u0 + 6 * half + j + 3)
                            tau = t0 + 8 * half + j
                            wait_tile(act, tau)
                            if half:
                                act.wait_ge(tile_v.handle, tile_v.after(("tile", t0 + 4 + j)))
                                if name != "branch0":
                                    act.wait_ge(mixed.handle, mixed.after(("m", l, int(name[-1]), j)))
                            nc.scalar.activation(gate[:, j, 0:n], tile_ps(tau, n), ACT.Tanh, scale=0.5
                                                 ).then_inc(tile_a.handle, tile_a.made(("tile", tau)))
                            if name == "branch0" and half == 0:
                                hi_oa(j)
                        if name == "branch1" and half == 0:
                            for g in range(WC):
                                act.wait_ge(pool_made.handle, pool_made.after((l, g)))
                                b = 2048 + 1024 * (g % 2)
                                nc.scalar.activation(ob_hi[:, g, 0:n], psf[:, b:b + n], ACT.Identity,
                                                     scale=vecs[:, P_SC + WC * l + g:P_SC + WC * l + g + 1]
                                                     ).then_inc(act_hi.handle, act_hi.made(("ob", l, g)))
                        for j in range(2):
                            split_hi(u0 + 6 * half + 4 + j + 3)
                            if name == "branch1":
                                for e in range(2):
                                    c = 4 * half + 2 * j + e
                                    act.wait_ge(mixed.handle, mixed.after(("m", l, 1, c)))
                                    nc.scalar.activation(m_hi[:, c, 0:n], m_f[:, c, 0:n], ACT.Copy
                                                         ).then_inc(act_hi.handle, act_hi.made(("m", l, c)))

                gates("branch0")
                stream("in_n", l, None)
                values_act(l, V_TILES_N, "in_n")

                nitems = nat_items(l)
                subs = [(i, hh) for i in range(len(nitems)) for hh in range(2)]

                def exp_n(s):
                    i, hh = subs[s]
                    c, q0, kind, k0, k1, tiles = nitems[i]
                    act.wait_ge(max_made.handle, max_made.after(("n", l, s)))
                    if s >= 4:
                        act.wait_ge(turned.handle, turned.after(("n", l, s - 4)))
                    w = k1 - k0 + CTX
                    nc.scalar.activation(probs_n[s // 2 % 2][:, s % 2, 0:w], ps[:, s % 4, 0:w], ACT.Exp, bias=neg_max[:, s % 4:s % 4 + 1],
                                         accum_out=total[:, s % 4:s % 4 + 1]).then_inc(exp_made.handle, exp_made.made(("n", l, s)))

                def turn_out_n(s):
                    i, hh = subs[s]
                    tiles = nitems[i][5]
                    act.wait_ge(turned.handle, turned.after(("n", l, s)))
                    if s >= 2:
                        act.wait_ge(pv_made.handle, pv_made.after(("pvn", l, s - 2)))
                    nc.scalar.copy(probsT_n[:, s % 2, 0:len(tiles), :], ps[:, 4 + s % 2, 0:len(tiles) * P]
                                   ).then_inc(turn_a.handle, turn_a.made(("n", l, s)))

                def o_hi_n(i):
                    c, q0 = nitems[i][:2]
                    act.wait_ge(pv_made.handle, pv_made.after(("pvn", l, 2 * i + 1)))
                    nc.scalar.activation(o_hi[:, c, q0:q0 + P], ps[:, o_bank(i), 0:P], ACT.Copy
                                         ).then_inc(act_hi.handle, act_hi.made(("on", l, i)))

                for s in range(len(subs) + 6):
                    if 3 <= s < len(subs) + 3:
                        turn_out_n(s - 3)
                    if s < len(subs):
                        exp_n(s)
                    if s >= 6 and s % 2 == 0 and (s - 6) // 2 < len(nitems):
                        o_hi_n((s - 6) // 2)
                gates("branch2")
                stream("in_p", l, None)

                gates("branch1")
                stream("out", l, lambda j: squares(l, 1, n, [j - 1] if j else []))
                squares(l, 1, n, [KC - 1])
                norm_act(l, 1, n)
                for g in range(4):
                    t0 = TILE[f"up{g}", l]

                    def relu(j):
                        wait_tile(act, t0 + j)
                        nc.scalar.activation(hid[g % 2][2][:, j, 0:n], tile_ps(t0 + j, n), ACT.Relu
                                             ).then_inc(tile_a.handle, tile_a.made(("tile", t0 + j)))

                    stream(f"up{g}", l, relu, begun=g == 0)
                    nxt = (DEPTH, 2, SEQ) if l == DEPTH - 1 else (l + 1, 0, TOK)
                    stream(f"down{g}", l, (lambda j: squares(*nxt, [j - 1] if j else [])) if g == 3 else None)
                squares(*nxt, [KC - 1])
            norm_act(DEPTH, 2, SEQ)
            for i in range(4):
                act.wait_ge(turned.handle, turned.after(("y", i, 1)))
                nc.scalar.copy(x_rows[:, i, 512:D], ps[:, 5, :]).then_inc(turn_a.handle, turn_a.made(("y", i)))

        @block.tensor
        def _(pe):
            def product(tau, s, hi, lo, n, kc=KC, col=0, width=P, ready=None):
                for c in range(kc):
                    if ready:
                        ready(c)
                    wh = w_hi[:, s, c * width + col:c * width + col + P]
                    wl = w_lo[:, s, c * width + col:c * width + col + P]
                    for step, (w, act_) in enumerate(((wh, hi), (wh, lo), (wl, hi))):
                        for t0, t1 in segs(n):
                            m = pe.matmul(psf[:, 1024 * (tau % 2) + t0:1024 * (tau % 2) + t1], lhsT=w, rhs=act_[:, c, t0:t1],
                                          start=c == 0 and step == 0, stop=c == kc - 1 and step == 2)
                return m

            def tile(tau, *args, **kw):
                u = plan.tile_unit[tau]
                wait_taken(pe, tau)
                wait_lo(pe, u)
                product(tau, u % RING, *args, **kw).then_inc(tile_made.handle, 1)

            def tile_pair(tau, hi, lo, n, ready):
                for t in (tau, tau + 1):
                    wait_taken(pe, t)
                    wait_lo(pe, plan.tile_unit[t])
                for c in range(KC):
                    ready(c)
                    for t in (tau, tau + 1):
                        s = plan.tile_unit[t] % RING
                        wh, wl = w_hi[:, s, P * c:P * c + P], w_lo[:, s, P * c:P * c + P]
                        for step, (w, act_) in enumerate(((wh, hi), (wh, lo), (wl, hi))):
                            for t0, t1 in segs(n):
                                m = pe.matmul(psf[:, 1024 * (t % 2) + t0:1024 * (t % 2) + t1], lhsT=w, rhs=act_[:, c, t0:t1],
                                              start=c == 0 and step == 0, stop=c == KC - 1 and step == 2)
                        if c == KC - 1:
                            m.then_inc(tile_made.handle, 1)

            def ada(u, A, i=None):
                if A >= 2:
                    pe.wait_ge(ada_taken.handle, A - 1 if i is None else i * 2 + (A - 1))
                wait_lo(pe, u, i)
                s, bank = u % RING, 4 + A % 2
                for c in range(KC):
                    pe.matmul(ps[0:4, bank, 0:P], lhsT=cond_hl[:, c, :], rhs=w_hi[:, s, P * c:P * c + P], start=c == 0, stop=False)
                    m = pe.matmul(ps[0:2, bank, 0:P], lhsT=cond_hl[:, c, 0:2], rhs=w_lo[:, s, P * c:P * c + P], start=False, stop=c == KC - 1)
                m.then_inc(tile_made.handle, 1)

            def ada_turnable(A, i=None):
                pe.wait_ge(ada_taken.handle, A + 1 if i is None else i * 2 + (A + 1))
                if A >= 2:
                    pe.wait_ge(ada_out.handle, A - 1 if i is None else i * 2 + (A - 1))

            def turn_ada(A):
                pe.transpose(ps[:, 6 + A % 2, 0:4], ada_rows[0:4, A % 2, :], ident[0:4, 0:4]).then_inc(ada_turned.handle, 1)

            def phase_loop(name, l, n_tok, hi, lo, ready, pair=False):
                kinds = plan.kinds[name, l]
                n, u0, t0, A0 = len(kinds), FIRST[name, l], TILE[name, l], plan.ada0[name, l]
                per, a_per = kinds[:RING].count("g"), kinds[:RING].count("a")
                tok = n_tok if callable(n_tok) else lambda j: n_tok
                peel = RING if per == RING else 2 * RING
                for j in range(peel):
                    g, A = kinds[:j].count("g"), kinds[:j].count("a")
                    if kinds[j] == "a":
                        ada(u0 + j, A0 + A)
                    else:
                        if not pair or g > 1:
                            tile(t0 + g, hi, lo, tok(g), ready=ready if g == 0 else None)
                        elif g:
                            tile_pair(t0, hi, lo, tok(0), ready)
                        for t in range(0 if pair and g == 1 else g, g + 1) if a_per and not (pair and g == 0) else ():
                            ada_turnable(A0 + t)
                            turn_ada(A0 + t)
                if n <= peel:
                    return
                tk = taker[t0 + WC - 2]
                v0 = tk.after(("tile", t0 + WC - 2))
                by = max(1, tk.after(("tile", t0 + WC - 1)) - v0)
                with pe.Fori(0, (n - peel) // RING) as i:
                    for j in range(peel, peel + RING):
                        g, A = kinds[:j].count("g"), kinds[:j].count("a")
                        if kinds[j] == "a":
                            ada(u0 + j, A0 + A, i)
                        else:
                            pe.wait_ge(tk.handle, i * (per * by) + (v0 + (g - WC) * by))
                            wait_lo(pe, u0 + j, i)
                            product(t0 + g, (u0 + j) % RING, hi, lo, tok(g),
                                    ready=(lambda c: ada_turnable(A0 + g, i) if c == KC - 1 else None) if a_per else None
                                    ).then_inc(tile_made.handle, 1)
                            if a_per:
                                turn_ada(A0 + g)

            pe.wait_ge(vecs_in.handle, 16 * 8)
            pe.wait_ge(ident_in.handle, 16)
            pe.transpose(ps[:, 5, 64:64 + 66], vec_rows[0:66, 0, :], ident[0:66, 0:66]).then_inc(turned.handle, turned.made("vec0"))
            pe.transpose(ps[:, 5, 192:192 + 96], vec_rows[0:96, 1, :], ident[0:96, 0:96]).then_inc(turned.handle, turned.made("vec1"))
            pe.wait_ge(setup.handle, setup.after("lam_pr"))
            pe.matmul(ps[:, 6, 0:2 * DEPTH], lhsT=ones[0:DH, :], rhs=lam_pr[0:DH, :, :].rearrange("p a b -> p (a b)"), start=True, stop=True
                      ).then_inc(turned.handle, turned.made("lam"))
            pe.wait_ge(setup.handle, setup.after("cond"))
            for A in range(ADA_FIRST):
                ada(A, A)
                if A:
                    ada_turnable(A - 1)
                    turn_ada(A - 1)
                c = A - X_TURN
                if 0 <= c < KC:
                    if c == 0:
                        pe.wait_ge(x_in.handle, 16 * 6)
                    if c >= 2:
                        pe.wait_ge(turn_v.handle, turn_v.after(("x", c - 2)))
                    for i in range(6):
                        m = pe.transpose(psf[:, 1024 * (c % 2) + P * i:1024 * (c % 2) + P * i + P], x_rows[:, i, P * c:P * c + P], ident[:, :])
                    m.then_inc(turned.handle, turned.made(("x", c)))
            ada_turnable(ADA_FIRST - 1)
            turn_ada(ADA_FIRST - 1)

            def mean_squares(l, which, n):
                pe.wait_ge(square_v.handle, square_v.after((l, which, KC - 1)))
                if l == 0 and which == 0:
                    pe.wait_ge(ada_out.handle, ADA_FIRST)
                for t0, t1 in segs(n):
                    m = pe.matmul(psf[:, 3072 + t0:3072 + t1], lhsT=ones[:, :], rhs=square_sum[which % 2][:, t0:t1], start=True, stop=True)
                m.then_inc(stat_made.handle, stat_made.made(("sq", l, which)))

            def h_ready(l, which):
                def ready(c):
                    pe.wait_ge(act_lo.handle, act_lo.after(("h", l, which, c)))
                return ready

            def values(l, tiles, key):
                for j, (t0, nk) in enumerate(tiles):
                    if j == 0:
                        last = taker[TILE[key, l] + 11]
                        pe.wait_ge(last.handle, last.after(("tile", TILE[key, l] + 11)))
                    if j == 2 and l == 0:
                        pe.wait_ge(ada_out.handle, plan.ada0[key, 0] + plan.kinds[key, 0].count("a"))
                    if j >= 4:
                        took = turn_a if j % 2 else turn_v
                        pe.wait_ge(took.handle, took.after((key, l, j - 4)))
                    for c in range(WC):
                        m = pe.transpose(ps[0:nk, 4 + j % 4, P * c:P * c + P], v_f[:, c, t0:t0 + nk], ident[:, :])
                    m.then_inc(turned.handle, turned.made((key, l, j)))

            for l in range(DEPTH):
                n = toks(l)
                mean_squares(l, 0, TOK)
                phase_loop("in_a", l, TOK if n == TOK else (lambda j: n if j < WC else TOK), h_hi, h_lo, h_ready(l, 0), pair=True)
                values(l, V_TILES_A, "in_a")

                items = diff_items(l)

                def scores_a(i):
                    h, q0, (k0, k1) = items[i]
                    if i % (len(items) // HEADS) == 0:
                        made = split_v if h < 2 else two_made
                        pe.wait_ge(made.handle, made.after((l, h)))
                    for m in range(2):
                        if i:
                            pe.wait_ge(exp_made.handle, exp_made.after(("a", l, i - 1, m)))
                        own, _ = map_rows(m)
                        qt, kt = q_two[h % 2], k_two[h % 2]
                        for part in range(2):
                            for t0, t1 in ([(0, SEQ)] if k0 == 0 else []) + [(SEQ, TOK)]:
                                lhsT, rhs = ((qt[:, m, q0:q0 + P], kt[:, m, t0:t1]), (qt[own, m, q0:q0 + P], k_lo[own, h, t0:t1]))[part]
                                mm = pe.matmul(psf[:, 1024 * m + t0 - k0:1024 * m + t1 - k0], lhsT=lhsT, rhs=rhs,
                                               start=part == 0, stop=part == 1)
                        mm.then_inc(scores_made.handle, scores_made.made(("a", l, i, m)))

                def turn_pa(i):
                    h, q0, (k0, k1) = items[i]
                    nb = (k1 - k0) // P
                    pe.wait_ge(probs_made.handle, probs_made.after(("a", l, i)))
                    if i:
                        pe.wait_ge(turn_a.handle, turn_a.after(("a", l, i - 1)))
                    else:
                        pe.wait_ge(turn_v.handle, turn_v.after(("in_a", l, 4)))
                        pe.wait_ge(turn_a.handle, turn_a.after(("in_a", l, 5)))
                    for b in range(nb):
                        mm = pe.transpose(psf[:, 2048 + P * b:2048 + P * b + P], probs_0[:, i % 3, P * b:P * b + P], ident[:, :])
                    mm.then_inc(turned.handle, turned.made(("a", l, i)))

                def weighted_a(i):
                    h, q0, (k0, k1) = items[i]
                    nb = (k1 - k0) // P
                    pe.wait_ge(turn_a.handle, turn_a.after(("a", l, i)))
                    if i >= 2:
                        pe.wait_ge(o_out.handle, o_out.after(("a", l, i - 2)))
                    elif l == 0:
                        pe.wait_ge(ada_out.handle, plan.ada0["in_a", 0] + plan.kinds["in_a", 0].count("a"))
                    for b in range(nb):
                        mm = pe.matmul(ps[:, o_bank(i), 0:P], lhsT=v[:, k0 // P + b, P * h:P * h + P], rhs=probsT_a[:, i % 3, b, :],
                                       start=b == 0, stop=b == nb - 1)
                    mm.then_inc(pv_made.handle, pv_made.made(("pv", l, i)))

                def square_mean_o(h):
                    pe.wait_ge(o_sq.handle, o_sq.after((l, h)))
                    if h < 2:
                        pe.wait_ge(o_out.handle, o_out.after(("a", l, len(items) - 1)))
                    else:
                        pe.wait_ge(rsq_v.handle, rsq_v.after(("o1", l, h - 2)))
                    b = 2048 + 1024 * (h % 2)
                    for t0, t1 in segs(n):
                        mm = pe.matmul(psf[:, b + t0:b + t1], lhsT=ones[:, :], rhs=square[0][:, h % 2, t0:t1], start=True, stop=True)
                    mm.then_inc(stat_made.handle, stat_made.made(("o", l, h)))

                for i in range(len(items) + 3):
                    if i < len(items):
                        scores_a(i)
                    if 2 <= i < len(items) + 2:
                        turn_pa(i - 2)
                    if i >= 3:
                        weighted_a(i - 3)

                def pool_products():
                    pe.wait_ge(pw_in.handle, 16 * (l + 1))
                    for g in range(WC):
                        pe.wait_ge(pooled_s.handle, pooled_s.after((l, g, "p")))
                        if g >= 2:
                            pe.wait_ge(act_lo.handle, act_lo.after(("ob", l, g - 2)))
                        if g == 1 and l == 0:
                            pe.wait_ge(ada_out.handle, plan.ada0["in_p", 0] + plan.kinds["in_p", 0].count("a"))
                        b = 2048 + 1024 * (g % 2)
                        for t0, t1 in segs(n):
                            mm = pe.matmul(psf[:, b + t0:b + t1], lhsT=pool_w[:, g, :], rhs=pooled[:, g, t0:t1], start=True, stop=True)
                        mm.then_inc(pool_made.handle, pool_made.made((l, g)))

                def branch(name, hi, lo, ready):
                    t0 = TILE[name, l]
                    for half in range(2):
                        for j in range(4):
                            if name == "branch0" and half == 0 and j < 2:
                                square_mean_o(2 * j)
                                square_mean_o(2 * j + 1)
                            tile(t0 + 8 * half + j, h_hi, h_lo, n)
                        if name == "branch1" and half == 0:
                            pool_products()
                        for j in range(2):
                            for e in range(2):
                                tile(t0 + 8 * half + 4 + 2 * j + e, hi, lo, n, kc=WC, col=P * e, width=2 * P,
                                     ready=ready if half + j + e == 0 else None)

                branch("branch0", o_hi, o_lo, lambda c: pe.wait_ge(act_lo.handle, act_lo.after(("o", l, c))))
                phase_loop("in_n", l, TOK if n == TOK else (lambda j: n if j < WC else TOK), h_hi, h_lo, None)
                values(l, V_TILES_N, "in_n")

                nitems = nat_items(l)
                subs = [(i, hh) for i in range(len(nitems)) for hh in range(2)]

                def scores_n(s):
                    i, hh = subs[s]
                    c, q0, kind, k0, k1, tiles = nitems[i]
                    if s >= 4:
                        pe.wait_ge(exp_made.handle, exp_made.after(("n", l, s - 4)))
                    lo_, hi_ = DH * hh, DH * hh + DH
                    loc = k1 - k0
                    if loc:
                        pe.matmul(ps[:, s % 4, 0:loc], lhsT=q[lo_:hi_, c, q0:q0 + P], rhs=k[lo_:hi_, c, k0:k1], start=True, stop=True)
                    pe.matmul(ps[:, s % 4, loc:loc + CTX], lhsT=q[lo_:hi_, c, q0:q0 + P], rhs=k[lo_:hi_, c, SEQ:TOK],
                              start=True, stop=True).then_inc(scores_made.handle, scores_made.made(("n", l, s)))

                def turn_pn(s):
                    i, hh = subs[s]
                    tiles = nitems[i][5]
                    pe.wait_ge(probs_made.handle, probs_made.after(("n", l, s)))
                    if s >= 2:
                        pe.wait_ge(turn_a.handle, turn_a.after(("n", l, s - 2)))
                    else:
                        pe.wait_ge(turn_v.handle, turn_v.after(("in_n", l, 6)))
                        pe.wait_ge(turn_a.handle, turn_a.after(("in_n", l, 5)))
                    for b, (j, off_, nk) in enumerate(tiles):
                        mm = pe.transpose(ps[0:nk, 4 + s % 2, P * b:P * b + P], probs_n[s // 2 % 2][:, s % 2, off_:off_ + nk], ident[:, :])
                    mm.then_inc(turned.handle, turned.made(("n", l, s)))

                def weighted_n(s):
                    i, hh = subs[s]
                    c, q0, kind, k0, k1, tiles = nitems[i]
                    pe.wait_ge(turn_a.handle, turn_a.after(("n", l, s)))
                    if i >= 2 and hh == 0:
                        pe.wait_ge(act_lo.handle, act_lo.after(("on", l, i - 2)))
                    if s == 0 and l == 0:
                        pe.wait_ge(ada_out.handle, plan.ada0["in_n", 0] + plan.kinds["in_n", 0].count("a"))
                    h = 2 * c + hh
                    for b, (j, off_, nk) in enumerate(tiles):
                        mm = pe.matmul(ps[DH * hh:DH * hh + DH, o_bank(i), 0:P], lhsT=v[0:nk, j, DH * h:DH * h + DH],
                                       rhs=probsT_n[0:nk, s % 2, b, :], start=b == 0, stop=b == len(tiles) - 1)
                    mm.then_inc(pv_made.handle, pv_made.made(("pvn", l, s)))

                for s in range(len(subs) + 4):
                    if s < len(subs):
                        scores_n(s)
                    if 3 <= s < len(subs) + 3:
                        turn_pn(s - 3)
                    if s >= 4:
                        weighted_n(s - 4)
                per_c = len(nitems) // WC
                branch("branch2", o_hi, o_lo, lambda c: pe.wait_ge(act_lo.handle, act_lo.after(("on", l, per_c * c + per_c - 1))))
                phase_loop("in_p", l, n, h_hi, h_lo, None)
                branch("branch1", ob_hi, o_lo, lambda c: pe.wait_ge(act_lo.handle, act_lo.after(("ob", l, c))))
                phase_loop("out", l, n, m_hi, m_lo, lambda c: pe.wait_ge(act_lo.handle, act_lo.after(("m", l, c))))
                mean_squares(l, 1, n)
                for g in range(4):
                    hh_, hl_, _ = hid[g % 2]
                    phase_loop(f"up{g}", l, n, h_hi, h_lo, h_ready(l, 1) if g == 0 else None, pair=g == 0)
                    phase_loop(f"down{g}", l, n, hh_, hl_, lambda c: pe.wait_ge(act_lo.handle, act_lo.after(("hid", l, g, c))))
            mean_squares(DEPTH, 2, SEQ)
            for i in range(4):
                for e in range(2):
                    if i:
                        took = turn_a if e else turn_v
                        pe.wait_ge(took.handle, took.after(("y", i - 1)))
                    for c in range(4 * e, 4 * e + 4):
                        pe.wait_ge(normed.handle, normed.after(("fin", c)))
                        mm = pe.transpose(ps[:, 4 + e, P * (c % 4):P * (c % 4) + P], x[:, c, P * i:P * i + P], ident[:, :])
                    mm.then_inc(turned.handle, turned.made(("y", i, e)))

        @block.vector
        def _(dve):
            V = nc.vector
            V.memset(ones[:, :], 1.0).then_inc(setup.handle, setup.made())
            V.memset(eps[:, :], EPS).then_inc(setup.handle, setup.made("ones"))
            dve.wait_ge(lam_loaded.handle, 64)
            lin = lam_in[0:DH, :, :].rearrange("p l (b t) -> p l b t", t=2)
            V.tensor_tensor(lam_pr[0:DH, :, :], lin[:, :, :, 0], lin[:, :, :, 1], ALU.mult).then_inc(setup.handle, setup.made("lam_pr"))
            dve.wait_ge(turned.handle, turned.after("vec1"))
            V.tensor_copy(vecs[:, :], ps[:, 5, 64:130]).then_inc(setup.handle, setup.made("vecs0"))
            dve.wait_ge(turned.handle, turned.after("lam"))
            V.memset(ones[:, :], 1.0 / D).then_inc(setup.handle, setup.made("vecs"))
            dve.wait_ge(silu_tanh.handle, 1)
            cv = vecs[:, COND:COND + 16].rearrange("p (s k) -> p k s", s=2)
            V.scalar_tensor_tensor(out=cond_t[:, :, :], in0=cond_t[:, :, :], scalar=1.0, in1=cv, op0=ALU.add, op1=ALU.mult
                                   ).then_inc(setup.handle, setup.made("silu"))
            dve.wait_ge(setup.handle, setup.after("silu"))
            V.tensor_scalar(cond_t[:, :, :], cond_t[:, :, :], 0.5, None, ALU.mult).then_inc(setup.handle, setup.made("cond_f"))
            dve.wait_ge(setup.handle, setup.after("cond_f"))
            V.tensor_copy(cond_hl[:, :, 0:2], cond_t[:, :, :]).then_inc(setup.handle, setup.made("cond_hi"))
            dve.wait_ge(setup.handle, setup.after("cond_hi"))
            V.tensor_tensor(cond_hl[:, :, 2:4], cond_t[:, :, :], cond_hl[:, :, 0:2], ALU.subtract).then_inc(setup.handle, setup.made("cond"))
            dve.wait_ge(lam_exp.handle, 1)
            for l in range(DEPTH):
                lam_init = 0.8 - 0.6 * math.exp(-0.3 * l)
                V.scalar_tensor_tensor(out=neg_lam[:, l:l + 1], in0=lam_e[:, l, 1:2], scalar=-lam_init, in1=lam_e[:, l, 0:1],
                                       op0=ALU.add, op1=ALU.subtract).then_inc(setup.handle, setup.made())
                V.tensor_scalar(g_sub[:, l:l + 1], vecs[:, G_SUB + l:G_SUB + l + 1], 1.0 - lam_init, None, ALU.mult
                                ).then_inc(setup.handle, setup.made("lam"))

            def lo_first(u):
                dve.wait_ge(hi_made.handle, u + 1)
                V.tensor_tensor(w_lo[:, u % RING, :], raw[:, u % RING, :], w_hi[:, u % RING, :], ALU.subtract).then_inc(first_lo.handle, 1)

            def take_ada(A, j):
                dve.wait_ge(ada_turned.handle, A + 1)
                V.tensor_copy(ada_cols[:, j, :], ps[:, 6 + A % 2, 0:4]).then_inc(ada_out.handle, 1)

            def square_add(l, which, c, n):
                dve.wait_ge(squared.handle, squared.after(("sq", l, which, c)))
                if c == 0:
                    V.tensor_copy(square_sum[which % 2][:, 0:n], square[which % 2][:, 0, 0:n]).then_inc(square_v.handle, square_v.made((l, which, c)))
                    return
                dve.wait_ge(square_v.handle, square_v.after((l, which, c - 1)))
                V.tensor_tensor(square_sum[which % 2][:, 0:n], square_sum[which % 2][:, 0:n], square[which % 2][:, c % 2, 0:n], ALU.add
                                ).then_inc(square_v.handle, square_v.made((l, which, c)))

            for s in range(2):
                V.tensor_copy(mods[:, :, :, :, s].rearrange("p l i k -> p (l i k)"), ps[:, 5, 192:288]).then_inc(setup.handle, setup.made("b"))
            for u in range(ADA_FIRST + 3):
                if u < ADA_FIRST:
                    lo_first(u)
                if u >= 3:
                    take_ada(u - 3, u - 3)
                c = u - X_TURN - 2
                if 0 <= c < KC:
                    dve.wait_ge(turned.handle, turned.after(("x", c)))
                    V.tensor_copy(x[:, c, :], psf[:, 1024 * (c % 2):1024 * (c % 2) + TOK]).then_inc(turn_v.handle, turn_v.made(("x", c)))
                if 0 <= c - 3 < KC:
                    square_add(0, 0, c - 3, TOK)
            assert ADA_FIRST + 3 >= X_TURN + 5 + KC
            mf = mods[:, :, :, :, :].rearrange("p l i k s -> p (l i k) s")

            def collect(name, l):
                A0, n = plan.ada0[name, l], plan.kinds[name, l].count("a")
                dve.wait_ge(ada_out.handle, A0 + n)
                got = ada_cols[:, 0:n, :]
                dst = mf[:, A0:A0 + n, :]
                if A0 == 0:
                    dve.wait_ge(setup.handle, setup.after("b"))
                V.tensor_tensor(dst, got[:, :, 0:2], dst, ALU.add).then_inc(collected.handle, collected.made())
                dve.wait_ge(collected.handle, collected.count)
                V.tensor_tensor(dst, got[:, :, 2:4], dst, ALU.add).then_inc(collected.handle, collected.made((name, l)))
                dve.wait_ge(collected.handle, collected.count)

            def take_ada_of(name, l, j):
                if "a" in plan.kinds[name, l]:
                    take_ada(plan.ada0[name, l] + j, j)

            def coefficients(l, w):
                g0 = (G_MIX if w == 0 else G_MLP) + KC * l
                for s in range(2):
                    V.scalar_tensor_tensor(out=coef[:, l, w, :, s], in0=mods[:, l, 3 * w + 1, :, s], scalar=1.0,
                                           in1=vecs[:, g0:g0 + KC], op0=ALU.add, op1=ALU.mult).then_inc(setup.handle, setup.made())
                dve.wait_ge(setup.handle, setup.count)

            def half_gate(l):
                V.tensor_scalar(mods[:, l, 2, :, :], mods[:, l, 2, :, :], 0.5, None, ALU.mult).then_inc(setup.handle, setup.made())
                dve.wait_ge(setup.handle, setup.count)

            collect("ada", 0)
            coefficients(0, 0)
            dve.wait_ge(consts_in.handle, 32)

            def rsqrt_v(y, mean, t, key):
                V.scalar_tensor_tensor(out=t, in0=mean, scalar=EPS, in1=y, op0=ALU.add, op1=ALU.mult
                                       ).then_inc(rsq_v.handle, rsq_v.made((key[0] + "1", *key[1:])))
                dve.wait_ge(rsq_v.handle, rsq_v.count)
                V.scalar_tensor_tensor(out=t, in0=t, scalar=-0.5, in1=y, op0=ALU.mult, op1=ALU.mult).then_inc(rsq_v.handle, rsq_v.made())
                dve.wait_ge(rsq_v.handle, rsq_v.count)
                V.scalar_tensor_tensor(out=y, in0=t, scalar=1.5, in1=y, op0=ALU.add, op1=ALU.mult).then_inc(rsq_v.handle, rsq_v.made())
                dve.wait_ge(rsq_v.handle, rsq_v.count)

            def norm_v(l, which, n):
                dve.wait_ge(root.handle, root.after((l, which)))
                rsqrt_v(rstd[which % 2][:, 0:n], psf[:, 3072:3072 + n], newton[which % 2][:, 0:n], ("norm", l, which))
                if which == 2:
                    for c in range(KC):
                        V.scalar_tensor_tensor(out=x[:, c, 0:n], in0=x[:, c, 0:n], scalar=vecs[:, G_FIN + c:G_FIN + c + 1],
                                               in1=rstd[which % 2][:, 0:n], op0=ALU.mult, op1=ALU.mult).then_inc(normed.handle, normed.made(("fin", c)))
                    return

                def lo(c):
                    dve.wait_ge(act_hi.handle, act_hi.after(("h", l, which, c)))
                    for s, (t0, t1) in enumerate(segs(n)):
                        V.scalar_tensor_tensor(out=h_lo[:, c, t0:t1], in0=h_f[:, c, t0:t1], scalar=mods[:, l, 3 * which, c, s:s + 1],
                                               in1=h_hi[:, c, t0:t1], op0=ALU.add, op1=ALU.subtract
                                               ).then_inc(act_lo.handle, act_lo.made(("h", l, which, c)))
                for c in range(KC):
                    for s, (t0, t1) in enumerate(segs(n)):
                        V.scalar_tensor_tensor(out=h_f[:, c, t0:t1], in0=x[:, c, t0:t1], scalar=coef[:, l, which, c, s:s + 1],
                                               in1=rstd[which % 2][:, t0:t1], op0=ALU.mult, op1=ALU.mult
                                               ).then_inc(normed.handle, normed.made((l, which, c)))
                    if c >= 1:
                        lo(c - 1)
                lo(KC - 1)

            def plain(tau, dst, n, scale=None):
                wait_tile(dve, tau)
                if scale is None:
                    V.tensor_copy(dst, tile_ps(tau, n)).then_inc(tile_v.handle, tile_v.made(("tile", tau)))
                else:
                    V.tensor_scalar(dst, tile_ps(tau, n), scale, None, ALU.mult).then_inc(tile_v.handle, tile_v.made(("tile", tau)))

            def rope(tau, dst, n, scale, s):
                wait_tile(dve, tau)
                z = tile_ps(tau, SEQ)
                V.stream_shuffle(rope_t[:, s % 2, :], z, [(i + 16) % 32 for i in range(32)]).then_inc(rope_s.handle, rope_s.made(("sh", tau)))
                V.scalar_tensor_tensor(out=dst[:, 0:SEQ], in0=z, scalar=scale, in1=cos[:, :], op0=ALU.mult, op1=ALU.mult
                                       ).then_inc(rope_s.handle, rope_s.made())
                dve.wait_ge(rope_s.handle, rope_s.after(("sh", tau)))
                V.scalar_tensor_tensor(out=rope_t[:, s % 2, :], in0=rope_t[:, s % 2, :], scalar=scale, in1=sin[:, :], op0=ALU.mult,
                                       op1=ALU.mult).then_inc(rope_s.handle, rope_s.made(("sin", tau)))
                if n > SEQ:
                    V.tensor_scalar(dst[:, SEQ:n], tile_ps(tau, n, SEQ), scale, None, ALU.mult).then_inc(rope_s.handle, rope_s.made(("c", tau)))
                    dve.wait_ge(rope_s.handle, rope_s.after(("c", tau)))
                else:
                    dve.wait_ge(rope_s.handle, rope_s.after(("sin", tau)))
                V.tensor_tensor(dst[:, 0:SEQ], dst[:, 0:SEQ], rope_t[:, s % 2, :], ALU.add).then_inc(tile_v.handle, tile_v.made(("tile", tau)))

            def values_v(l, tiles, key):
                for j, (t0, nk) in enumerate(tiles):
                    if j % 2 == 0:
                        dve.wait_ge(turned.handle, turned.after((key, l, j)))
                        V.tensor_copy(v[0:nk, j, :], ps[0:nk, 4 + j % 4, :]).then_inc(turn_v.handle, turn_v.made((key, l, j)))

            for l in range(DEPTH):
                n = toks(l)
                norm_v(l, 0, TOK)
                t0 = TILE["in_a", l]
                dve.wait_ge(rope_in.handle, 32 * (l + 1))
                def split_qk_v(h):
                    for part in range(5):
                        for m in range(2):
                            own, other = map_rows(m)
                            kt, qt = k_two[h][:, m, :], q_two[h][:, m, 0:n]
                            qf = q[own, h, 0:n]
                            if part < 3:
                                dst, src = ((kt[own, :], k[own, h, :]), (kt[other, :], k[own, h, :]), (qt[own, :], qf))[part]
                                V.tensor_copy(dst, src).then_inc(split_v.handle, split_v.made(("hi", l, h)))
                                continue
                            dve.wait_ge(split_v.handle, split_v.after(("hi", l, h)))
                            if part == 3:
                                V.tensor_tensor(k_lo[own, h, :], k[own, h, :], kt[own, :], ALU.subtract
                                                ).then_inc(split_v.handle, split_v.made((l, h)))
                            else:
                                V.tensor_tensor(qt[other, :], qf, qt[own, :], ALU.subtract).then_inc(split_v.handle, split_v.made((l, h)))

                for j in range(12):
                    nt = n if j < WC else TOK
                    if j in (9, 10):
                        dve.wait_ge(tile_v.handle, tile_v.after(("tile", t0 + 7)))
                        split_qk_v(j - 9)
                    if j < 8:
                        rope(t0 + j, (q if j < 4 else k)[:, j % 4, :], nt, SCALE if j < 4 else 1.0, j)
                    else:
                        plain(t0 + j, v_f[:, j - 8, 0:nt], nt)
                    take_ada_of("in_a", l, j)
                values_v(l, V_TILES_A, "in_a")
                if l == 0:
                    collect("in_a", 0)

                items = diff_items(l)

                def max_a(i):
                    h, q0, (k0, k1) = items[i]
                    for m in range(2):
                        s = (2 * i + m) % 4
                        dve.wait_ge(scores_made.handle, scores_made.after(("a", l, i, m)))
                        V.tensor_reduce(neg_max[:, s:s + 1], psf[:, 1024 * m:1024 * m + k1 - k0], AX_X, ALU.max, negate=True
                                        ).then_inc(max_made.handle, max_made.made(("a", l, i, m)))

                def combine(i):
                    h, q0, (k0, k1) = items[i]
                    w, s = k1 - k0, (2 * i) % 4
                    dve.wait_ge(exp_made.handle, exp_made.after(("a", l, i, 1)))
                    V.reciprocal(rtotal[:, s:s + 2], total[:, s:s + 2]).then_inc(rsum.handle, rsum.made(("a", l, i)))
                    dve.wait_ge(rsum.handle, rsum.after(("a", l, i)))
                    V.tensor_scalar(rtotal[:, s + 1:s + 2], rtotal[:, s + 1:s + 2], neg_lam[:, l:l + 1], None, ALU.mult
                                    ).then_inc(rsum.handle, rsum.made())
                    V.tensor_scalar(probs_0[:, i % 3, 0:w], probs_0[:, i % 3, 0:w], rtotal[:, s:s + 1], None, ALU.mult
                                    ).then_inc(rsum.handle, rsum.made(("a0", l, i)))
                    dve.wait_ge(rsum.handle, rsum.after(("a0", l, i)))
                    V.scalar_tensor_tensor(out=probs_0[:, i % 3, 0:w], in0=probs_1[:, i % 2, 0:w], scalar=rtotal[:, s + 1:s + 2],
                                           in1=probs_0[:, i % 3, 0:w], op0=ALU.mult, op1=ALU.add
                                           ).then_inc(probs_made.handle, probs_made.made(("a", l, i)))

                for i in range(len(items) + 1):
                    if i < len(items):
                        max_a(i)
                    if i:
                        combine(i - 1)

                def lo_oa(h):
                    dve.wait_ge(act_hi.handle, act_hi.after(("oa", l, h)))
                    V.tensor_tensor(o_lo[:, h, 0:n], o_f[:, h, 0:n], o_hi[:, h, 0:n], ALU.subtract
                                    ).then_inc(act_lo.handle, act_lo.made(("o", l, h)))

                for h in range(HEADS):
                    b = 2048 + 1024 * (h % 2)
                    dve.wait_ge(root.handle, root.after(("ln", l, h)))
                    V.tensor_scalar(o_mean[h // 2][:, h % 2, 0:n], psf[:, b:b + n], EPS * P / D, None, ALU.add).then_inc(rsq_v.handle, rsq_v.made(("o1", l, h)))
                for h in range(HEADS):
                    y, t = rms_o[:, h, 0:n], o_mean[h // 2][:, h % 2, 0:n]
                    dve.wait_ge(root.handle, root.after(("o", l, h)))
                    dve.wait_ge(rsq_v.handle, rsq_v.count)
                    V.tensor_tensor(t, t, y, ALU.mult).then_inc(rsq_v.handle, rsq_v.made())
                    dve.wait_ge(rsq_v.handle, rsq_v.count)
                    V.scalar_tensor_tensor(out=t, in0=t, scalar=-0.5 * D / P, in1=y, op0=ALU.mult, op1=ALU.mult).then_inc(rsq_v.handle, rsq_v.made())
                    dve.wait_ge(rsq_v.handle, rsq_v.count)
                    V.scalar_tensor_tensor(out=y, in0=t, scalar=1.5, in1=y, op0=ALU.add, op1=ALU.mult).then_inc(rsq_v.handle, rsq_v.made())
                    dve.wait_ge(rsq_v.handle, rsq_v.count)
                    V.scalar_tensor_tensor(out=o_f[:, h, 0:n], in0=o_f[:, h, 0:n], scalar=g_sub[:, l:l + 1], in1=y, op0=ALU.mult,
                                           op1=ALU.mult).then_inc(rsq_v.handle, rsq_v.made(("o", l, h)))
                    if h:
                        lo_oa(h - 1)
                lo_oa(HEADS - 1)

                def mix(name, b):
                    t0 = TILE[name, l]

                    def lo(c):
                        dve.wait_ge(act_hi.handle, act_hi.after(("m", l, c)))
                        V.tensor_tensor(m_lo[:, c, 0:n], m_f[:, c, 0:n], m_hi[:, c, 0:n], ALU.subtract
                                        ).then_inc(act_lo.handle, act_lo.made(("m", l, c)))
                    for c in range(KC):
                        half, j = divmod(c, 4)
                        tau = t0 + 8 * half + 4 + j
                        wait_tile(dve, tau)
                        dve.wait_ge(tile_a.handle, tile_a.after(("tile", t0 + 8 * half + j)))
                        first = name == "branch0"
                        dst = m_f[:, c, 0:n] if first else gate[:, j, 0:n]
                        V.scalar_tensor_tensor(out=dst, in0=gate[:, j, 0:n], scalar=1.0, in1=tile_ps(tau, n), op0=ALU.add,
                                               op1=ALU.mult).then_inc(tile_v.handle, tile_v.made(("tile", tau)))
                        if not first:
                            dve.wait_ge(tile_v.handle, tile_v.after(("tile", tau)))
                            V.tensor_tensor(m_f[:, c, 0:n], m_f[:, c, 0:n], gate[:, j, 0:n], ALU.add
                                            ).then_inc(mixed.handle, mixed.made(("m", l, b, c)))
                        if b == 1 and c:
                            lo(c - 1)
                    if b == 1:
                        lo(KC - 1)

                mix("branch0", 0)

                t0 = TILE["in_n", l]
                dve.wait_ge(tile_v.handle, tile_v.after(("tile", TILE["branch0", l] + 15)))
                V.memset(bias_raw[:, :, :, :], 0.0).then_inc(biased.handle, biased.made(("clear", l)))
                def bias_of(c, kinds):
                    for t in kinds:
                        c0 = (8, 0, 0)[t]
                        for hh in range(2):
                            w = MASKW[t] // 8
                            o = MASKO[t]
                            V.tensor_tensor(bias[:, hh, o:o + MASKW[t]].rearrange("p (c r) -> p c r", r=8),
                                            bias_raw[:, ::-1, 2 * c + hh, c0:c0 + w].rearrange("p r c -> p c r"),
                                            mask[:, o:o + MASKW[t]].rearrange("p (c r) -> p c r", r=8), ALU.add
                                            ).then_inc(biased.handle, biased.made(("bm", l, c, t)))

                for j in range(12):
                    nt = n if j < WC else TOK
                    dst = (q, k, v_f)[j // 4]
                    if j == 10:
                        dve.wait_ge(bias_in.handle, 16 * 16 * (l + 1))
                        bias_of(0, (0, 1, 2))
                    plain(t0 + j, dst[:, j % 4, 0:nt], nt, SCALE if j < 4 else None)
                    take_ada_of("in_n", l, j)
                values_v(l, V_TILES_N, "in_n")
                if l == 0:
                    collect("in_n", 0)

                nitems = nat_items(l)
                subs = [(i, hh) for i in range(len(nitems)) for hh in range(2)]
                def max_n(s):
                    i, hh = subs[s]
                    c, q0, kind, k0, k1, tiles = nitems[i]
                    loc = k1 - k0
                    dve.wait_ge(scores_made.handle, scores_made.after(("n", l, s)))
                    if loc:
                        if hh == 0 and q0 != 2 * P:
                            dve.wait_ge(biased.handle, biased.after(("bm", l, c, kind)))
                        V.tensor_tensor(ps[:, s % 4, 0:loc], ps[:, s % 4, 0:loc], bias[:, hh, MASKO[kind]:MASKO[kind] + loc], ALU.add
                                        ).then_inc(biased.handle, biased.made(("s", l, s)))
                        dve.wait_ge(biased.handle, biased.after(("s", l, s)))
                    V.tensor_reduce(neg_max[:, s % 4:s % 4 + 1], ps[:, s % 4, 0:loc + CTX], AX_X, ALU.max, negate=True
                                    ).then_inc(max_made.handle, max_made.made(("n", l, s)))

                def divide_n(s):
                    i, hh = subs[s]
                    c, q0, kind, k0, k1, tiles = nitems[i]
                    w = k1 - k0 + CTX
                    dve.wait_ge(exp_made.handle, exp_made.after(("n", l, s)))
                    V.reciprocal(rtotal[:, s % 4:s % 4 + 1], total[:, s % 4:s % 4 + 1]).then_inc(rsum.handle, rsum.made(("n", l, s)))
                    dve.wait_ge(rsum.handle, rsum.after(("n", l, s)))
                    V.tensor_scalar(probs_n[s // 2 % 2][:, s % 2, 0:w], probs_n[s // 2 % 2][:, s % 2, 0:w], rtotal[:, s % 4:s % 4 + 1], None, ALU.mult
                                    ).then_inc(probs_made.handle, probs_made.made(("n", l, s)))

                def o_lo_n(i):
                    c, q0 = nitems[i][:2]
                    dve.wait_ge(act_hi.handle, act_hi.after(("on", l, i)))
                    V.tensor_tensor(o_lo[:, c, q0:q0 + P], ps[:, o_bank(i), 0:P], o_hi[:, c, q0:q0 + P], ALU.subtract
                                    ).then_inc(act_lo.handle, act_lo.made(("on", l, i)))

                ns = len(subs)
                for s in range(ns + 7):
                    if s < ns:
                        c, at_ = divmod(s, ns // WC)
                        if at_ in (2, 6) and c + 1 < WC:
                            bias_of(c + 1, (at_ // 4,))
                        if at_ == 0 and c:
                            bias_of(c, (2,))
                        max_n(s)
                    if 2 <= s < ns + 2:
                        divide_n(s - 2)
                    if s >= 7 and s % 2 and (s - 7) // 2 < len(nitems):
                        o_lo_n((s - 7) // 2)
                mix("branch2", 2)

                t0 = TILE["in_p", l]
                wait_tile(dve, t0 - 1)
                for g in range(WC):
                    for z0 in (0, UPAD + SEQ, UPAD + SEQ + UPAD, UW - UPAD):
                        V.memset(u_pad[:, g, z0:z0 + UPAD], 0.0).then_inc(pooled_s.handle, pooled_s.made(("zero", l)))
                offs = [(0, UPAD, SEQ), (SEQ, SEQ + 3 * UPAD, CTX)][:len(segs(n))]
                for g in range(WC):
                    tau = t0 + g
                    wait_tile(dve, tau)
                    if n > SEQ:
                        V.tensor_copy(u_pad[:, g, SEQ + 3 * UPAD:SEQ + 3 * UPAD + CTX], tile_ps(tau, TOK, SEQ)
                                      ).then_inc(pooled_s.handle, pooled_s.made())
                    V.tensor_copy(u_pad[:, g, UPAD:UPAD + SEQ].rearrange("p (r c) -> p c r", r=ROWS),
                                  tile_ps(tau, SEQ).rearrange("p (c r) -> p c r", r=ROWS)
                                  ).then_inc(tile_v.handle, tile_v.made(("tile", tau)))
                    take_ada_of("in_p", l, g)
                    dve.wait_ge(tile_v.handle, tile_v.after(("tile", tau)))
                    if g == 0:
                        dve.wait_ge(pooled_s.handle, pooled_s.after(("zero", l)))
                    w = 2 << g
                    src = u_pad[:, g, :]
                    for e in range(g + 1):
                        d_ = (1, 1, 2, 4)[e]
                        dst = win[:, e % 2, :]
                        if e:
                            dve.wait_ge(pooled_s.handle, pooled_s.after(("u", l, g, e - 1)))
                        for t_, b_, len_ in offs:
                            m_ = (7, 6, 4, 0)[e]
                            a0, a1 = b_ - m_, b_ + len_ + m_
                            if e == 0:
                                i0, i1 = src[:, a0 - 1:a1 - 1], src[:, a0:a1]
                            else:
                                i0, i1 = src[:, a0 - d_:a1 - d_], src[:, a0 + d_:a1 + d_]
                            V.tensor_tensor(dst[:, a0:a1], i0, i1, ALU.add).then_inc(pooled_s.handle, pooled_s.made(("u", l, g, e)))
                        src = dst
                    dve.wait_ge(pooled_s.handle, pooled_s.after(("u", l, g, g)))
                    for t_, b_, len_ in offs:
                        V.tensor_tensor(src[:, b_:b_ + w // 2], src[:, b_:b_ + w // 2], edge[:, g, 0, 0:w // 2], ALU.mult
                                        ).then_inc(pooled_s.handle, pooled_s.made())
                        if w > 2:
                            e0, e1 = b_ + len_ - w // 2 + 1, b_ + len_
                            V.tensor_tensor(src[:, e0:e1], src[:, e0:e1], edge[:, g, 1, 0:w // 2 - 1], ALU.mult
                                            ).then_inc(pooled_s.handle, pooled_s.made())
                    pooled_s.seen["e", l, g] = pooled_s.count
                    dve.wait_ge(pooled_s.handle, pooled_s.after(("e", l, g)))
                    if n > SEQ:
                        o = SEQ + 3 * UPAD
                        V.scalar_tensor_tensor(out=pooled[:, g, SEQ:TOK], in0=src[:, o:o + CTX], scalar=1.0 / w, in1=u_pad[:, g, o:o + CTX],
                                               op0=ALU.mult, op1=ALU.subtract).then_inc(pooled_s.handle, pooled_s.made())
                    V.scalar_tensor_tensor(out=pooled[:, g, 0:SEQ].rearrange("p (c r) -> p c r", r=ROWS),
                                           in0=src[:, UPAD:UPAD + SEQ].rearrange("p (r c) -> p c r", r=ROWS), scalar=1.0 / w,
                                           in1=u_pad[:, g, UPAD:UPAD + SEQ].rearrange("p (r c) -> p c r", r=ROWS),
                                           op0=ALU.mult, op1=ALU.subtract).then_inc(pooled_s.handle, pooled_s.made((l, g, "p")))
                    dve.wait_ge(pooled_s.handle, pooled_s.after((l, g, "p")))
                if l == 0:
                    collect("in_p", 0)
                    half_gate(0)
                    coefficients(0, 1)
                for g in range(WC):
                    b = 2048 + 1024 * (g % 2)
                    dve.wait_ge(act_hi.handle, act_hi.after(("ob", l, g)))
                    V.scalar_tensor_tensor(out=o_lo[:, g, 0:n], in0=psf[:, b:b + n], scalar=vecs[:, P_SC + WC * l + g:P_SC + WC * l + g + 1],
                                           in1=ob_hi[:, g, 0:n], op0=ALU.mult, op1=ALU.subtract
                                           ).then_inc(act_lo.handle, act_lo.made(("ob", l, g)))
                mix("branch1", 1)

                def residual(name, six, norm=None):
                    t0 = TILE[name, l]
                    for c in range(KC):
                        if norm and c:
                            square_add(*norm[:2], c - 1, norm[2])
                        wait_tile(dve, t0 + c)
                        for s, (a0, a1) in enumerate(segs(n)):
                            V.scalar_tensor_tensor(out=x[:, c, a0:a1], in0=tile_ps(t0 + c, a1, a0), scalar=mods[:, l, six, c, s:s + 1],
                                                   in1=x[:, c, a0:a1], op0=ALU.mult, op1=ALU.add
                                                   ).then_inc(tile_v.handle, tile_v.made(("tile", t0 + c)))
                        take_ada_of(name, l, c)

                residual("out", 2, (l, 1, n))
                square_add(l, 1, KC - 1, n)
                norm_v(l, 1, n)
                for g in range(4):
                    hh_, hl_, hf_ = hid[g % 2]
                    for c in range(KC):
                        dve.wait_ge(tile_a.handle, tile_a.after(("tile", TILE[f"up{g}", l] + c)))
                        V.tensor_tensor(hf_[:, c, 0:n], hf_[:, c, 0:n], hf_[:, c, 0:n], ALU.mult).then_inc(hid_s.handle, hid_s.made(("sq", l, g, c)))
                        dve.wait_ge(hid_s.handle, hid_s.after(("sq", l, g, c)))
                        V.tensor_copy(hh_[:, c, 0:n], hf_[:, c, 0:n]).then_inc(hid_s.handle, hid_s.made(("hi", l, g, c)))
                        dve.wait_ge(hid_s.handle, hid_s.after(("hi", l, g, c)))
                        V.tensor_tensor(hl_[:, c, 0:n], hf_[:, c, 0:n], hh_[:, c, 0:n], ALU.subtract
                                        ).then_inc(act_lo.handle, act_lo.made(("hid", l, g, c)))
                        take_ada_of(f"up{g}", l, c)
                    if l == 0:
                        collect(f"up{g}", 0)
                    norm = None if g < 3 else (l + 1, 0, TOK) if l + 1 < DEPTH else (DEPTH, 2, SEQ)
                    residual(f"down{g}", 5, norm)
                    if norm:
                        square_add(*norm[:2], KC - 1, norm[2])
                    dve.wait_ge(tile_v.handle, tile_v.after(("tile", TILE[f"down{g}", l] + 7)))
                    if l == 0 and g < 2:
                        collect(f"down{g}", 0)
                    if l == 0 and g == 2:
                        half_gate(1)
                        coefficients(1, 0)
                        coefficients(1, 1)
            norm_v(DEPTH, 2, SEQ)
            for i in range(4):
                dve.wait_ge(turned.handle, turned.after(("y", i, 0)))
                V.tensor_copy(x_rows[:, i, 0:512], ps[:, 4, :]).then_inc(turn_v.handle, turn_v.made(("y", i)))

        return count.counted()


_FLAT = ("b_ada", "g_mix", "g_mlp", "g_final", "pool_scale", "g_subln", "c", "c_ctx")
_INS = ("x", "c", "ctx", "c_ctx", "w_ada", "b_ada", "g_mix", "g_mlp", "w_in", "lambda_q1", "lambda_k1", "lambda_q2", "lambda_k2",
        "g_subln", "pool_w", "pool_scale", "nat_rpb", "w_branch", "w_out", "w_mlp1", "w_mlp2", "g_final")


def shape_constants():
    import numpy as np

    t = np.arange(SEQ)
    row, col = t % ROWS, t // ROWS
    nf = 16
    inv = np.float32(10000.0) ** (-np.arange(nf, dtype=np.float32) / np.float32(nf))
    p = np.arange(P)
    pos = np.where(((p // 32) % 2 == 0)[:, None], row[None, :], col[None, :]).astype(np.float32)
    ang = pos * inv[p % 16][:, None]
    sign = np.where((p % 32) < 16, -1.0, 1.0).astype(np.float32)[:, None]
    mask = np.full((P, 640), -1e30, np.float32)
    for kind, g, o, c0 in ((0, 0, MASKO[0], 0), (1, 1, MASKO[1], 8), (2, 3, MASKO[2], 40)):
        for part in range(P):
            cq = 16 * g + part // 8
            w0 = min(max(cq - 8, 0), COLS - 16)
            for j in range(MASKW[kind]):
                if w0 <= c0 + j // 8 < w0 + 16:
                    mask[part, o + j] = 0.0
    edge = np.ones((4, 2, 8), np.float32)
    for g in range(4):
        w = 2 << g
        for i in range(w // 2):
            edge[g, 0, i] = w / (i + w // 2)
            if i < w // 2 - 1:
                edge[g, 1, i] = w / (w // 2 - 1 - i + w // 2)
    return {"c_ident": np.eye(P, dtype=np.float32), "c_mask": mask, "c_cos": np.cos(ang).astype(np.float32),
            "c_sin": (np.sin(ang) * sign).astype(np.float32), "c_edge": np.ascontiguousarray(np.broadcast_to(edge, (P, 4, 2, 8)))}


def kernel(**inputs):
    import numpy as np
    import concourse.bacc as bacc
    from concourse.bass_utils import run_bass_kernel_spmd

    arrays = dict(shape_constants())
    for name in _INS:
        v = np.ascontiguousarray(inputs[name])
        if name == "nat_rpb":
            v = np.ascontiguousarray(v[:, :, ::-1].transpose(0, 2, 1, 3))
        arrays[name] = v.reshape(-1) if name in _FLAT else v.reshape(v.shape[-2:]) if name in ("x", "ctx") else v

    def build(known):
        nc = bacc.Bacc("TRN2", target_bir_lowering=False, num_devices=1, dynamic_dma_scratch_size=64)
        a = {n: nc.dram_tensor(f"in_{n}", v.shape, mybir.dt.from_np(v.dtype), kind="ExternalInput").ap() for n, v in arrays.items()}
        out = nc.dram_tensor("out_0", (SEQ, D), F32, kind="ExternalOutput").ap()
        return nc, hybrid_block(nc, a, out, known)

    _, counted = build({})
    nc, again = build(counted)
    assert again == counted
    r = run_bass_kernel_spmd(nc, [{f"in_{n}": v for n, v in arrays.items()}], core_ids=[0])
    return r.results[0]["out_0"].reshape(1, SEQ, D)
```
